# Optimizing a Trainium2 kernel written in Bass

```python
import jax, jax.numpy as jnp
from jax import lax
import numpy as np

D_MODEL = 1024
BATCH = 1
SEQ = 512
DEPTH = 1

MIX_WIDTH = D_MODEL
ATT_WIDTH = MIX_WIDTH // 2
GMLP_WIDTH = MIX_WIDTH - ATT_WIDTH
ATT_HEAD_DIM = 64
N_ATT_HEADS = ATT_WIDTH // ATT_HEAD_DIM
N_GMLP_GROUPS = 8
GMLP_GROUP_DIM = GMLP_WIDTH // N_GMLP_GROUPS
CHUNK = 128
Q_BLOCK = 128
D_FF = 2816
CONV_WIDTH = 3
EPS = 1e-6

Q_END = ATT_WIDTH
K_END = 2 * ATT_WIDTH
V_END = 3 * ATT_WIDTH
U_END = V_END + GMLP_WIDTH
G_END = U_END + GMLP_WIDTH
IN_COLS = G_END + N_ATT_HEADS


def rmsnorm(x, gain):
    xf = x.astype(jnp.float32)
    y = xf * lax.rsqrt(jnp.mean(xf * xf, axis=-1, keepdims=True) + EPS)
    return y.astype(x.dtype) * gain

def forgetting_attention(q, k, v, log_f):
    B, S, H, Dh = q.shape
    nb = S // Q_BLOCK
    c = jnp.cumsum(log_f, axis=1)
    c_k = c.transpose(0, 2, 1)[:, :, None, :]
    key_pos = jnp.arange(S)
    qb = q.reshape(B, nb, Q_BLOCK, H, Dh).transpose(1, 0, 2, 3, 4)
    cb = c.reshape(B, nb, Q_BLOCK, H).transpose(1, 0, 3, 2)
    pb = key_pos.reshape(nb, Q_BLOCK)
    scale = Dh ** -0.5

    def block(args):
        qi, ci, pi = args
        logits = jnp.einsum('bqhd,bkhd->bhqk', qi, k).astype(jnp.float32) * scale
        logits = logits + ci[..., None] - c_k
        causal = pi[:, None] >= key_pos[None, :]
        logits = jnp.where(causal, logits, -jnp.inf)
        p = jax.nn.softmax(logits, axis=-1).astype(v.dtype)
        return jnp.einsum('bhqk,bkhd->bqhd', p, v)

    out = lax.map(block, (qb, cb, pb))
    return out.transpose(1, 0, 2, 3, 4).reshape(B, S, H * Dh)

def chunked_spatial_gating(u, vg, v_gain, w_s, b_s):
    B, S, G, Dg = u.shape
    nc = S // CHUNK
    vg = rmsnorm(vg, v_gain.reshape(G, Dg))
    vc = vg.reshape(B, nc, CHUNK, G, Dg)
    w = w_s * jnp.tril(jnp.ones((CHUNK, CHUNK), dtype=w_s.dtype))
    mixed = jnp.einsum('gij,bnjgd->bnigd', w, vc) + b_s.T[None, None, :, :, None]
    return (u * mixed.reshape(B, S, G, Dg)).reshape(B, S, G * Dg)

def conv_ffn(x, w_up, conv_w, conv_b, w_down):
    h = x @ w_up
    h = lax.conv_general_dilated(
        h, conv_w[:, None, :], window_strides=(1,),
        padding=[(CONV_WIDTH - 1, 0)],
        dimension_numbers=('NWC', 'WIO', 'NWC'),
        feature_group_count=h.shape[-1]) + conv_b
    a, g = jnp.split(h, 2, axis=-1)
    return (jax.nn.silu(g) * a) @ w_down

def first_inputs(seed: int = 0) -> dict:
    key = jax.random.key(seed)
    ks = jax.random.split(key, 16)
    f32 = jnp.float32
    x = jax.random.normal(ks[0], (BATCH, SEQ, D_MODEL), f32)
    norm_mix_g = 1.0 + 0.02 * jax.random.normal(ks[1], (DEPTH, D_MODEL), f32)
    w_in = jax.random.normal(ks[2], (DEPTH, D_MODEL, IN_COLS), f32) * D_MODEL ** -0.5
    b_forget = 2.0 + 0.5 * jax.random.normal(ks[3], (DEPTH, N_ATT_HEADS), f32)
    gmlp_norm_g = 1.0 + 0.02 * jax.random.normal(ks[4], (DEPTH, GMLP_WIDTH), f32)
    w_spatial = jax.random.normal(ks[5], (DEPTH, N_GMLP_GROUPS, CHUNK, CHUNK), f32) * CHUNK ** -0.5
    b_spatial = 1.0 + 0.1 * jax.random.normal(ks[6], (DEPTH, N_GMLP_GROUPS, CHUNK), f32)
    w_out = jax.random.normal(ks[7], (DEPTH, MIX_WIDTH, D_MODEL), f32) * MIX_WIDTH ** -0.5
    norm_ffn_g = 1.0 + 0.02 * jax.random.normal(ks[8], (DEPTH, D_MODEL), f32)
    w_up = jax.random.normal(ks[9], (DEPTH, D_MODEL, 2 * D_FF), f32) * D_MODEL ** -0.5
    conv_w = jax.random.normal(ks[10], (DEPTH, CONV_WIDTH, 2 * D_FF), f32) * CONV_WIDTH ** -0.5
    conv_b = 0.01 * jax.random.normal(ks[11], (DEPTH, 2 * D_FF), f32)
    w_down = jax.random.normal(ks[12], (DEPTH, D_FF, D_MODEL), f32) * D_FF ** -0.5
    norm_final_g = 1.0 + 0.02 * jax.random.normal(ks[13], (D_MODEL,), f32)
    return {"x": x, "norm_mix_g": norm_mix_g, "w_in": w_in, "b_forget": b_forget,
            "gmlp_norm_g": gmlp_norm_g, "w_spatial": w_spatial, "b_spatial": b_spatial,
            "w_out": w_out, "norm_ffn_g": norm_ffn_g, "w_up": w_up, "conv_w": conv_w,
            "conv_b": conv_b, "w_down": w_down, "norm_final_g": norm_final_g}

def first_block(x, norm_mix_g, w_in, b_forget, gmlp_norm_g, w_spatial, b_spatial,
              w_out, norm_ffn_g, w_up, conv_w, conv_b, w_down, norm_final_g):
    B, S, _ = x.shape
    h = x
    for layer in range(DEPTH):
        xn = rmsnorm(h, norm_mix_g[layer])
        proj = xn @ w_in[layer]
        q = proj[..., :Q_END].reshape(B, S, N_ATT_HEADS, ATT_HEAD_DIM)
        k = proj[..., Q_END:K_END].reshape(B, S, N_ATT_HEADS, ATT_HEAD_DIM)
        v = proj[..., K_END:V_END].reshape(B, S, N_ATT_HEADS, ATT_HEAD_DIM)
        log_f = jax.nn.log_sigmoid(
            (proj[..., G_END:] + b_forget[layer]).astype(jnp.float32))
        att = forgetting_attention(q, k, v, log_f)
        uv = jax.nn.gelu(proj[..., V_END:G_END])
        u = uv[..., :GMLP_WIDTH].reshape(B, S, N_GMLP_GROUPS, GMLP_GROUP_DIM)
        vg = uv[..., GMLP_WIDTH:].reshape(B, S, N_GMLP_GROUPS, GMLP_GROUP_DIM)
        sg = chunked_spatial_gating(u, vg, gmlp_norm_g[layer], w_spatial[layer], b_spatial[layer])
        mix = jnp.concatenate([att, sg], axis=-1)
        h = h + mix @ w_out[layer]
        h = h + conv_ffn(rmsnorm(h, norm_ffn_g[layer]), w_up[layer], conv_w[layer],
                         conv_b[layer], w_down[layer])
    return rmsnorm(h, norm_final_g)


CHUNK_2 = 64
LEFT_CHUNKS = 8
BAND = (LEFT_CHUNKS + 1) * CHUNK_2
MLA_HEADS = 8
MLA_Q_RANK = 256
MLA_KV_RANK = 128
MLA_NOPE = 64
MLA_ROPE = 32
MLA_QK = MLA_NOPE + MLA_ROPE
MLA_V = 64
ROPE_THETA = 10000.0
CA_HEADS = 8
CA_HEAD_DIM = 64
REL_CLIP = 128
D_MIX = MLA_HEADS * MLA_V + CA_HEADS * CA_HEAD_DIM
D_IN = MLA_Q_RANK + MLA_KV_RANK + MLA_ROPE + 3 * CA_HEADS * CA_HEAD_DIM
N_MOD = 6
NEG_INF = -1e30


def rmsnorm_2(x, g):
    xf = x.astype(jnp.float32)
    y = xf * lax.rsqrt(jnp.mean(xf * xf, axis=-1, keepdims=True) + EPS)
    return (y * g.astype(jnp.float32)).astype(x.dtype)

def modulate(h, shift, scale):
    return h * (1 + scale[:, None, :]) + shift[:, None, :]

def rope(x, positions):
    half = x.shape[-1] // 2
    inv = jnp.power(ROPE_THETA, -jnp.arange(half, dtype=jnp.float32) / half)
    ang = positions.astype(jnp.float32)[..., None] * inv
    cos = jnp.cos(ang)[:, :, None, :]
    sin = jnp.sin(ang)[:, :, None, :]
    xf = x.astype(jnp.float32)
    x1, x2 = xf[..., :half], xf[..., half:]
    out = jnp.concatenate([x1 * cos - x2 * sin, x2 * cos + x1 * sin], axis=-1)
    return out.astype(x.dtype)

def mla_attention(q, k, v):
    B, S, H, Dq = q.shape
    nqb = S // Q_BLOCK
    scale = Dq ** -0.5
    key_chunk = jnp.arange(S) // CHUNK_2
    qb = q.reshape(B, nqb, Q_BLOCK, H, Dq).swapaxes(0, 1)

    def block(args):
        qi, i = args
        s = jnp.einsum('bqhd,bkhd->bhqk', qi, k,
                       preferred_element_type=jnp.float32) * scale
        q_chunk = (i * Q_BLOCK + jnp.arange(Q_BLOCK)) // CHUNK_2
        mask = key_chunk[None, :] <= q_chunk[:, None]
        s = jnp.where(mask[None, None], s, NEG_INF)
        p = jax.nn.softmax(s, axis=-1).astype(v.dtype)
        return jnp.einsum('bhqk,bkhd->bqhd', p, v)

    o = lax.map(block, (qb, jnp.arange(nqb)))
    return o.swapaxes(0, 1).reshape(B, S, H * v.shape[-1])

def chunk_attention(q, k, v, rel_bias):
    B, S, H, D = q.shape
    nc = S // CHUNK_2
    pad = LEFT_CHUNKS * CHUNK_2
    scale = D ** -0.5
    k_pad = jnp.pad(k, ((0, 0), (pad, 0), (0, 0), (0, 0)))
    v_pad = jnp.pad(v, ((0, 0), (pad, 0), (0, 0), (0, 0)))
    qi = jnp.arange(CHUNK_2)
    kj = jnp.arange(BAND)
    rel = (pad + qi[:, None]) - kj[None, :]
    bias = rel_bias[:, jnp.clip(rel, -REL_CLIP, REL_CLIP) + REL_CLIP].astype(jnp.float32)
    qc = q.reshape(B, nc, CHUNK_2, H, D).swapaxes(0, 1)

    def one_chunk(args):
        qch, ci = args
        kb = lax.dynamic_slice_in_dim(k_pad, ci * CHUNK_2, BAND, axis=1)
        vb = lax.dynamic_slice_in_dim(v_pad, ci * CHUNK_2, BAND, axis=1)
        s = jnp.einsum('bqhd,bkhd->bhqk', qch, kb,
                       preferred_element_type=jnp.float32) * scale + bias[None]
        valid = kj >= (LEFT_CHUNKS - ci) * CHUNK_2
        s = jnp.where(valid[None, None, None, :], s, NEG_INF)
        p = jax.nn.softmax(s, axis=-1).astype(vb.dtype)
        return jnp.einsum('bhqk,bkhd->bqhd', p, vb)

    o = lax.map(one_chunk, (qc, jnp.arange(nc)))
    return o.swapaxes(0, 1).reshape(B, S, H * D)

def causal_dwconv(u, w, b):
    S = u.shape[1]
    up = jnp.pad(u, ((0, 0), (CONV_WIDTH - 1, 0), (0, 0)))
    out = up[:, 0:S] * w[0]
    for j in range(1, CONV_WIDTH):
        out = out + up[:, j:j + S] * w[j]
    return out + b

def second_inputs(seed: int = 0) -> dict:
    key = jax.random.key(seed)
    ks = jax.random.split(key, 24)
    f32 = jnp.float32

    def nrm(k, shape, fan_in):
        return jax.random.normal(k, shape, f32) * (fan_in ** -0.5)

    def gain(k, shape):
        return 1.0 + 0.05 * jax.random.normal(k, shape, f32)

    L = DEPTH
    x = jax.random.normal(ks[0], (BATCH, SEQ, D_MODEL), f32)
    c = jax.random.normal(ks[1], (BATCH, D_MODEL), f32)
    offsets = jax.random.randint(ks[2], (BATCH, 1), 0, 4096, dtype=jnp.int32)
    positions = (offsets + jnp.arange(SEQ, dtype=jnp.int32)[None, :]).astype(jnp.int32)
    return {
        "x": x,
        "c": c,
        "positions": positions,
        "w_ada": nrm(ks[3], (L, D_MODEL, N_MOD * D_MODEL), D_MODEL),
        "b_ada": 0.02 * jax.random.normal(ks[4], (L, N_MOD * D_MODEL), f32),
        "g_attn_norm": gain(ks[5], (L, D_MODEL)),
        "w_in": nrm(ks[6], (L, D_MODEL, D_IN), D_MODEL),
        "g_q_latent": gain(ks[7], (L, MLA_Q_RANK)),
        "g_kv_latent": gain(ks[8], (L, MLA_KV_RANK)),
        "w_q_up": nrm(ks[9], (L, MLA_Q_RANK, MLA_HEADS * MLA_QK), MLA_Q_RANK),
        "w_kv_up": nrm(ks[10], (L, MLA_KV_RANK, MLA_HEADS * (MLA_NOPE + MLA_V)), MLA_KV_RANK),
        "g_mla_q": gain(ks[11], (L, MLA_QK)),
        "g_mla_k": gain(ks[12], (L, MLA_QK)),
        "g_ca_q": gain(ks[13], (L, CA_HEAD_DIM)),
        "g_ca_k": gain(ks[14], (L, CA_HEAD_DIM)),
        "rel_bias": 0.5 * jax.random.normal(ks[15], (L, CA_HEADS, 2 * REL_CLIP + 1), f32),
        "w_out": nrm(ks[16], (L, D_MIX, D_MODEL), D_MIX),
        "g_mlp_norm": gain(ks[17], (L, D_MODEL)),
        "w_up": nrm(ks[18], (L, D_MODEL, 2 * D_FF), D_MODEL),
        "conv_w": nrm(ks[19], (L, CONV_WIDTH, 2 * D_FF), CONV_WIDTH),
        "conv_b": 0.02 * jax.random.normal(ks[20], (L, 2 * D_FF), f32),
        "w_down": nrm(ks[21], (L, D_FF, D_MODEL), D_FF),
    }

def second_block(x, c, positions, w_ada, b_ada, g_attn_norm, w_in, g_q_latent, g_kv_latent,
              w_q_up, w_kv_up, g_mla_q, g_mla_k, g_ca_q, g_ca_k, rel_bias, w_out,
              g_mlp_norm, w_up, conv_w, conv_b, w_down):
    B, S, _ = x.shape
    split_pts = [MLA_Q_RANK, MLA_Q_RANK + MLA_KV_RANK, MLA_Q_RANK + MLA_KV_RANK + MLA_ROPE]
    for l in range(DEPTH):
        mod = jnp.dot(jax.nn.silu(c), w_ada[l]) + b_ada[l]
        sh_a, sc_a, g_a, sh_m, sc_m, g_m = jnp.split(mod, N_MOD, axis=-1)

        h = modulate(rmsnorm_2(x, g_attn_norm[l]), sh_a, sc_a)
        proj = jnp.dot(h, w_in[l])
        q_lat, kv_lat, k_rope, ca_qkv = jnp.split(proj, split_pts, axis=-1)

        q = jnp.dot(rmsnorm_2(q_lat, g_q_latent[l]), w_q_up[l]).reshape(B, S, MLA_HEADS, MLA_QK)
        kv = jnp.dot(rmsnorm_2(kv_lat, g_kv_latent[l]), w_kv_up[l]).reshape(B, S, MLA_HEADS, MLA_NOPE + MLA_V)
        k_nope, v = kv[..., :MLA_NOPE], kv[..., MLA_NOPE:]
        k = jnp.concatenate(
            [k_nope, jnp.broadcast_to(k_rope[:, :, None, :], (B, S, MLA_HEADS, MLA_ROPE))], axis=-1)
        q = rmsnorm_2(q, g_mla_q[l])
        k = rmsnorm_2(k, g_mla_k[l])
        q = jnp.concatenate([q[..., :MLA_NOPE], rope(q[..., MLA_NOPE:], positions)], axis=-1)
        k = jnp.concatenate([k[..., :MLA_NOPE], rope(k[..., MLA_NOPE:], positions)], axis=-1)
        o_mla = mla_attention(q, k, v)

        ca = ca_qkv.reshape(B, S, 3, CA_HEADS, CA_HEAD_DIM)
        cq = rmsnorm_2(ca[:, :, 0], g_ca_q[l])
        ck = rmsnorm_2(ca[:, :, 1], g_ca_k[l])
        cv = ca[:, :, 2]
        o_ca = chunk_attention(cq, ck, cv, rel_bias[l])

        mixed = jnp.dot(jnp.concatenate([o_mla, o_ca], axis=-1), w_out[l])
        x = x + g_a[:, None, :] * mixed

        h = modulate(rmsnorm_2(x, g_mlp_norm[l]), sh_m, sc_m)
        u = causal_dwconv(jnp.dot(h, w_up[l]), conv_w[l], conv_b[l])
        gate, val = jnp.split(u, 2, axis=-1)
        x = x + g_m[:, None, :] * jnp.dot(jax.nn.silu(gate) * val, w_down[l])
    return x


def setup_inputs(seed=0):
    out = dict(first_inputs(seed))
    for name, value in second_inputs(seed + 1).items():
        if name != "x":
            out[name + "_2"] = value
    return out


def reference(
    x, norm_mix_g, w_in, b_forget, gmlp_norm_g, w_spatial, b_spatial, w_out, norm_ffn_g, w_up,
    conv_w, conv_b, w_down, norm_final_g, c_2, positions_2, w_ada_2, b_ada_2, g_attn_norm_2,
    w_in_2, g_q_latent_2, g_kv_latent_2, w_q_up_2, w_kv_up_2, g_mla_q_2, g_mla_k_2, g_ca_q_2,
    g_ca_k_2, rel_bias_2, w_out_2, g_mlp_norm_2, w_up_2, conv_w_2, conv_b_2, w_down_2,
):
    x = first_block(
        x, norm_mix_g, w_in, b_forget, gmlp_norm_g, w_spatial, b_spatial, w_out, norm_ffn_g,
        w_up, conv_w, conv_b, w_down, norm_final_g,
    )
    return second_block(
        x, c_2, positions_2, w_ada_2, b_ada_2, g_attn_norm_2, w_in_2, g_q_latent_2,
        g_kv_latent_2, w_q_up_2, w_kv_up_2, g_mla_q_2, g_mla_k_2, g_ca_q_2, g_ca_k_2,
        rel_bias_2, w_out_2, g_mlp_norm_2, w_up_2, conv_w_2, conv_b_2, w_down_2,
    )


_drawn_inputs = setup_inputs


def setup_inputs(seed=0):
    import zlib

    import numpy as np

    out = dict(_drawn_inputs(seed))
    spreads = {}
    factors = {'norm_mix_g': 3.442,
     'gmlp_norm_g': 8.0,
     'norm_ffn_g': 4.451,
     'conv_b': 8.0,
     'g_attn_norm_2': 6.946,
     'g_q_latent_2': 8.0,
     'g_kv_latent_2': 5.34,
     'g_mla_q_2': 8.0,
     'g_mla_k_2': 8.0,
     'g_ca_q_2': 8.0,
     'g_ca_k_2': 8.0,
     'conv_b_2': 17.98,
     'g_mlp_norm_2': 6.337}
    for name, (base, spread) in spreads.items():
        noise = np.random.default_rng([zlib.crc32(name.encode()), seed]).standard_normal(out[name].shape)
        drawn = base * np.exp(spread * noise) if base else spread * noise
        out[name] = __import__('jax').numpy.asarray(drawn.astype(out[name].dtype))
    for name, factor in factors.items():
        out[name] = (out[name] * factor).astype(out[name].dtype)
    return out
```

```python
from contextlib import ExitStack

import numpy as np

import concourse.bass as bass
from concourse import mybir

ALU = mybir.AluOpType
ACT = mybir.ActivationFunctionType
F32 = mybir.dt.float32
F32R = mybir.dt.float32r
BF16 = mybir.dt.bfloat16
I32 = mybir.dt.int32
AX_X = mybir.AxisListType.X

P = 128
D = 1024
T = 512
KD = D // P
TB = T // P
HEADS = 8
HD = 64
PAIRS = HEADS // 2
FF = 2816
KF = FF // P
UP_TILES = 2 * KF
EPS = 1e-6
MLA_QK = 96
ROPE = 32
ROPE_THETA = 10000.0
REL_CLIP = 128
REL_LEN = T + P

CHUNK = 2048
DOWN_CHUNK = KF // 2 * P
PAIR_COLS = CHUNK // KD
ADA_COLS = 6 * D
N_ADA = ADA_COLS // PAIR_COLS
MASKED = -1e30

STREAM1 = [("f", 1), ("vg", 2), ("u", 2), ("qk", PAIRS), ("v", 2), ("out", KD // 2), ("up", KF)]
STREAM2 = [("kvr", 1), ("ql", 1), ("cv", 2), ("cqk", PAIRS), ("mq", 1), ("mkv", 1), ("out", KD // 2), ("up", KF)]
N1 = sum(n for _, n in STREAM1)
N2 = sum(n for _, n in STREAM2)
N_DOWN = 2 * KD
BASE1 = {}
BASE2 = {}
at = 0
for name, count in STREAM1:
    BASE1[name] = at
    at += count
BASE1["down"] = at
at += N_DOWN
for name, count in STREAM2:
    BASE2[name] = at
    at += count
BASE2["down"] = at
N_CHUNKS = at + N_DOWN

COLS = {}
n_cols = 0
for name, count in [
    ("mix_g", KD), ("ffn_g", KD), ("final_g", KD), ("attn2_g", KD), ("mlp2_g", KD), ("gmlp_g", 4),
    ("conv_w", 3 * UP_TILES), ("conv_b", UP_TILES), ("conv_w2", 3 * UP_TILES), ("conv_b2", UP_TILES),
    ("b_ada", N_ADA * 2), ("c", KD), ("ql_g", 2), ("kvl_g", 1), ("mq_g", 1), ("mk_g", 1), ("mkr_g", 1),
    ("cq_g", 1), ("ck_g", 1), ("b_forget", 1), ("head_row", HEADS), ("inv_freq", 1), ("q_sign", 1), ("k_sign", 1),
]:
    COLS[name] = (n_cols, count)
    n_cols += count


def build(nc, xT, cols_in, stream1, down1, stream2, down2, ada, w_spatial_T, b_spatial_rows, positions, rel_rows, outT):
    ctx = ExitStack()
    with ctx:
        def sem(name):
            return ctx.enter_context(nc.semaphore(name))

        def sb(name, shape, dt=F32, scope=ctx):
            return scope.enter_context(nc.sbuf_tensor(name, shape, dt))

        bank = [ctx.enter_context(nc.psum_tensor(f"bank{b}", [P, 512], F32)) for b in range(8)]
        SS_BANK, MOD_BANK = bank[6], bank[7]

        h = sb("h", [P, KD, T])
        xh = sb("xh", [P, KD, T], F32R)
        xl = sb("xl", [P, KD, T], F32R)
        raw = [sb(f"raw{s}", [P, CHUNK]) for s in range(2)]
        wh = [sb(f"wh{s}", [P, CHUNK], F32R) for s in range(2)]
        wl = [sb(f"wl{s}", [P, CHUNK], F32R) for s in range(2)]
        ada_raw = sb("ada_raw", [P, KD, PAIR_COLS])
        ada_acc = sb("ada_acc", [P, PAIR_COLS])
        scratch = [sb(f"scratch{s}", [P, T]) for s in range(4)]
        ss_acc = sb("ss_acc", [P, T])
        cols = sb("cols", [P, n_cols])
        csil = sb("csil", [P, KD])
        mod = sb("mod", [P, 6, KD])
        modA = sb("modA", [P, 2, KD])
        ones = sb("ones", [P, P])
        eps_c = sb("eps_c", [P, 1])
        halfpi_c = sb("halfpi_c", [P, 1])
        eps64_c = sb("eps64_c", [P, 1])

        def col(name, j=0):
            return cols[:, bass.ds(COLS[name][0] + j, 1)]

        def col_at(name, a, b):
            c = COLS[name][0]
            return cols[a:b, c:c + 1]

        with ExitStack() as s:
            acth = sb("acth", [P, KF, T], F32R, s)
            actl = sb("actl", [P, KF, T], F32R, s)

        with ExitStack() as s:
            v1 = sb("v1", [P, TB, 512], F32, s)
            vg = sb("vg", [P, TB, 512], F32, s)
            u_sb = sb("u_sb", [P, 4, T], F32, s)
            q1 = sb("q1", [P, PAIRS, T], F32, s)
            k1 = sb("k1", [P, PAIRS, T], F32, s)
            dec_q = sb("dec_q", [P, T], F32R, s)
            dec_all = sb("dec_all", [P, T], F32, s)
            dec_k = [sb(f"dec_k{b}", [P, T], F32R, s) for b in range(2)]
            lf = [sb(f"lf{b}", [P, T], F32, s) for b in range(2)]
            prob1 = [sb(f"prob1{b}", [P, T], F32, s) for b in range(3)]
            probT1 = [sb(f"probT1{b}", [P, T], F32, s) for b in range(2)]
            o1 = sb("o1", [P, TB, 512], F32, s)
            wsT = sb("wsT", [P, HEADS, P], F32, s)
            bsp = sb("bsp", [P, 4, P], F32, s)
            vsum = sb("vsum", [P, TB * HEADS], F32, s)
            vrs = sb("vrs", [P, TB * HEADS], F32, s)
            neg_max1 = sb("neg_max1", [P, 32], F32, s)
            row_sum1 = sb("row_sum1", [P, 32], F32, s)
            ident1 = sb("ident1", [P, P], F32, s)
            ident_b1 = sb("ident_b1", [P, P], BF16, s)
            causal_b = sb("causal_b", [P, P], BF16, s)

        with ExitStack() as s:
            qlh = sb("qlh", [P, 2, T], F32R, s)
            qll = sb("qll", [P, 2, T], F32R, s)
            kvh = sb("kvh", [P, T], F32R, s)
            kvl = sb("kvl", [P, T], F32R, s)
            k_rope = sb("k_rope", [P, T], F32, s)
            q_trig = sb("q_trig", [P, T], F32, s)
            v2 = sb("v2", [P, TB, 512], F32, s)
            o2 = sb("o2", [P, TB, 512], F32, s)
            prob2 = [sb(f"prob2{b}", [P, T], F32, s) for b in range(3)]
            probT2 = [sb(f"probT2{b}", [P, T], F32, s) for b in range(2)]
            neg_max2 = sb("neg_max2", [P, 64], F32, s)
            row_sum2 = sb("row_sum2", [P, 64], F32, s)
            ident2 = sb("ident2", [P, P], F32, s)
            ident_b2 = sb("ident_b2", [P, P], BF16, s)
            flip = sb("flip", [P, P], F32, s)
            ones96 = sb("ones96", [P, P], F32, s)
            ones64 = sb("ones64", [P, P], F32, s)
            chunk_b = sb("chunk_b", [P, P], BF16, s)
            sq2 = [sb(f"sq2{b}", [P, T], F32, s) for b in range(2)]
            sqk = [sb(f"sqk{b}", [P, T], F32, s) for b in range(2)]
            with ExitStack() as s2:
                cq = sb("cq", [P, PAIRS, T], F32, s2)
                ck = sb("ck", [P, PAIRS, T], F32, s2)
                rel = [sb(f"rel{b}", [P, T], F32, s2) for b in range(2)]
                pos_i = sb("pos_i", [P, T], I32, s2)
                ang = sb("ang", [P, T], F32, s2)
                turn = sb("turn", [P, T], F32, s2)
                k_trig = sb("k_trig", [P, T], F32, s2)
            with ExitStack() as s2:
                mq = sb("mq", [P, HEADS, T], F32, s2)
                mk = sb("mk", [P, HEADS, T], F32, s2)

        landed = [sem(f"landed{s}") for s in range(2)]
        hi_done = sem("hi_done")
        lo_done = sem("lo_done")
        ada_landed, ada_scaled, ada_red, ada_used = [sem(f"ada_{x}") for x in ("landed", "scaled", "red", "used")]
        x_landed, cols_landed, small_landed, pos_landed = [sem(f"{x}_landed") for x in ("x", "cols", "small", "pos")]
        rel_landed = [sem(f"rel_landed{b}") for b in range(2)]
        out_done = sem("out_done")
        setup1, setup2 = sem("setup1"), sem("setup2")
        csil_done = sem("csil_done")

        class Stage:
            pass

        def sems(stage, *names):
            return [sem(f"{stage}_{x}") for x in names]

        def norm_stage(name):
            s = Stage()
            s.sq, s.acc, s.ss, s.root, s.rstd, s.tmp, s.hi, s.lo = sems(name, "sq", "acc", "ss", "root", "rstd", "tmp", "hi", "lo")
            return s

        def residual_stage(name):
            s = Stage()
            s.mm, s.h = sems(name, "mm", "h")
            return s

        def up_stage(name, w, b):
            s = Stage()
            s.w, s.b = w, b
            s.mm, s.base, s.tap, s.conv, s.silu, s.gated, s.hi, s.lo = sems(name, "mm", "base", "tap", "conv", "silu", "gated", "hi", "lo")
            return s

        norm_mix, norm_ffn, norm_final, norm_attn2, norm_mlp2 = [norm_stage(x) for x in ("nmix", "nffn", "nfin", "natt", "nmlp")]
        pre, mod_done = sem("modulate_pre"), sem("mod_done")
        res_out1, res_down1, res_out2, res_down2 = [residual_stage(x) for x in ("ro1", "rd1", "ro2", "rd2")]
        up1, up2 = up_stage("up1", "conv_w", "conv_b"), up_stage("up2", "conv_w2", "conv_b2")
        p1 = Stage()
        p1.mm, p1.act, p1.dve = sems("p1", "mm", "act", "dve")
        p2 = Stage()
        p2.mm, p2.dve = sems("p2", "mm", "dve")
        forget = Stage()
        forget.act, forget.dve = sems("forget", "act", "dve")
        decay = Stage()
        decay.hi, decay.dve, decay.head = sems("decay", "hi", "dve", "head")
        gate = Stage()
        gate.sq, gate.sum, gate.root, gate.rstd, gate.done = sems("gate", "sq", "sum", "root", "rstd", "done")
        mixing = Stage()
        mixing.mm, mixing.bias, mixing.done = sems("mixing", "mm", "bias", "done")
        att = Stage()
        att.qk, att.max, att.exp, att.pt, att.ptc, att.pv, att.rinv, att.o = sems("att", "qk", "max", "exp", "pt", "ptc", "pv", "rinv", "o")
        mix = Stage()
        mix.mm, mix.hi, mix.lo = sems("mix", "mm", "hi", "lo")
        trig = Stage()
        trig.dve, trig.act, trig.row = sems("trig", "dve", "act", "row")
        rope = Stage()
        rope.dve, rope.sq = sems("rope", "dve", "sq")
        head = Stage()
        head.sq, head.ss, head.root, head.rstd, head.pre, head.done = sems("head", "sq", "ss", "root", "rstd", "pre", "done")
        lat = Stage()
        lat.hi, lat.lo = sems("lat", "hi", "lo")

        P1 = {"f": 1, "vg0": 2, "vg": [3, 4, 5, 6], "u": [7, 8, 9, 10], "q": [11, 13, 15, 17], "k": [12, 14, 16, 18],
              "v0": 19, "v": [20, 21, 22, 23]}
        P2 = {"kv": 1, "rope": 2, "ql": [3, 4], "v0": 5, "v": [6, 7, 8, 9], "q": [10, 12, 14, 16], "k": [11, 13, 15, 17],
              "mv": [18, 19, 20, 21], "mq": [22 + 2 * x for x in range(HEADS)], "mk": [23 + 2 * x for x in range(HEADS)]}
        CV_ORDER = [2, 3, 0, 1]

        JOB_KV, JOB_QL = 0, 1

        def job_c(p, which):
            return 2 + 2 * p + which

        def job_m(hd, which):
            return 2 + 2 * PAIRS + 2 * hd + which

        N_SQ = {}
        for x in range(2 + 2 * PAIRS + 2 * HEADS):
            N_SQ[x] = x + 1 + (x >= JOB_QL)

        UNITS = HEADS * TB

        def unit(a, u):
            return a * UNITS + u

        block = ctx.enter_context(nc.Block())

        @block.sync
        def _(sp):
            def chunk(source, j, n, slot, width, first=False):
                if not first:
                    sp.wait_ge(lo_done, n - 1)
                sp.dma_start(raw[slot][:, 0:width], source[bass.ds(j * P, P), :]).then_inc(landed[slot], 16)

            def ada_chunk(a, first=False):
                if not first:
                    sp.wait_ge(ada_red, a)
                sp.dma_start(ada_raw[:, :, :], ada[bass.ds(a * P, P), :].rearrange("p (k c) -> p k c", k=KD)).then_inc(ada_landed, 16)

            def stream(source, base, j0, count, with_ada=None):
                with sp.Fori(0, count // 2) as i:
                    for s in range(2):
                        chunk(source, i * 2 + (j0 + s), i * 2 + (base + j0 + s), (base + j0 + s) % 2, source.shape[1])
                        if with_ada:
                            with_ada(i, s)

            sp.dma_start(h[:, :, :], xT.rearrange("(k p) t -> p k t", p=P)).then_inc(x_landed, 16)
            sp.dma_start(cols[:, :], cols_in).then_inc(cols_landed, 16)
            chunk(stream1, 0, 0, 0, CHUNK, first=True)
            chunk(stream1, 1, 1, 1, CHUNK, first=True)
            sp.dma_start(wsT[:, :, :], w_spatial_T.rearrange("j (g i) -> j g i", g=HEADS)).then_inc(small_landed, 16)
            sp.dma_start(bsp[:, :, :], b_spatial_rows.rearrange("p (t i) -> p t i", t=4)).then_inc(small_landed, 16)
            ada_chunk(0, first=True)
            for n in range(2, BASE1["out"]):
                chunk(stream1, n, n, n % 2, CHUNK)

            def ada_out(i, s):
                if s:
                    ada_chunk(i + 1)

            def ada_up(i, s):
                ada_chunk(i * 2 + (3 + s))

            stream(stream1, 0, BASE1["out"], KD // 2, ada_out)
            for s in range(2):
                n = BASE1["up"] + s
                chunk(stream1, n, n, n % 2, CHUNK)
            stream(stream1, 0, BASE1["up"] + 2, KF - 2, ada_up)
            ada_chunk(N_ADA - 1)
            stream(down1, BASE1["down"], 0, N_DOWN)
            base = N1 + N_DOWN
            for j in range(BASE2["out"] - base):
                chunk(stream2, j, base + j, (base + j) % 2, CHUNK)
            stream(stream2, base, BASE2["out"] - base, KD // 2)
            stream(stream2, base, BASE2["up"] - base, KF)
            stream(down2, BASE2["down"], 0, N_DOWN)
            for m in range(KD):
                sp.wait_ge(res_down2.h, m + 1)
                sp.dma_start(outT[m * P:(m + 1) * P, :], h[:, m, :]).then_inc(out_done, 16)
            sp.wait_ge(out_done, 16 * KD)

        @block.gpsimd
        def _(pool):
            def low(n, slot):
                pool.wait_ge(hi_done, n + 1)
                pool.tensor_tensor(wl[slot][:, :], raw[slot][:, :], wh[slot][:, :].bitcast(F32), ALU.subtract).then_inc(lo_done, 1)

            def lows(a, b):
                with pool.Fori(0, (b - a) // 2) as i:
                    for s in range(2):
                        low(i * 2 + (a + s), (a + s) % 2)
                if (b - a) % 2:
                    low(b - 1, (b - 1) % 2)

            pool.memset(ones[:, :], 1.0).then_inc(setup1, 1)
            pool.memset(eps_c[:, :], EPS).then_inc(setup1, 1)
            pool.memset(halfpi_c[:, :], float(np.pi / 2)).then_inc(setup1, 1)
            pool.memset(eps64_c[:, :], HD * EPS).then_inc(setup1, 1)
            pool.memset(ident1[:, :], 0.0).then_inc(setup1, 1)
            pool.memset(ident_b1[:, :], 0.0).then_inc(setup1, 1)
            pool.memset(causal_b[:, :], 0.0).then_inc(setup1, 1)
            pool.wait_ge(setup1, 7)
            for t in (ident1, ident_b1):
                pool.affine_select(out=t[:, :], in_=t[:, :], compare_op=ALU.not_equal, fill=1.0, base=0,
                                   pattern=[[-1, P]], channel_multiplier=1).then_inc(setup1, 1)
            pool.affine_select(out=causal_b[:, :], in_=causal_b[:, :], compare_op=ALU.is_ge, fill=MASKED, base=0,
                               pattern=[[-1, P]], channel_multiplier=1).then_inc(setup1, 1)
            pool.wait_ge(small_landed, 32)
            pool.affine_select(out=wsT[:, :, :], in_=wsT[:, :, :], compare_op=ALU.is_ge, fill=0.0, base=0,
                               pattern=[[0, HEADS], [1, P]], channel_multiplier=-1).then_inc(setup1, 1)
            base = N1 + N_DOWN
            lows(0, base)
            pool.wait_ge(res_down1.h, KD)
            made = 0

            def constant(ins):
                nonlocal made
                made += 1
                ins.then_inc(setup2, 1)
                pool.wait_ge(setup2, made)

            constant(pool.memset(ident2[:, :], 0.0))
            constant(pool.memset(ident_b2[:, :], 0.0))
            constant(pool.memset(flip[:, :], 0.0))
            constant(pool.memset(ones96[0:96, :], 1.0))
            constant(pool.memset(ones96[96:P, :], 0.0))
            constant(pool.memset(ones64[:, :], 0.0))
            constant(pool.memset(chunk_b[:, :], 0.0))
            constant(pool.memset(q_trig[0:64, :], 1.0))
            for t in (ident2, ident_b2):
                constant(pool.affine_select(out=t[:, :], in_=t[:, :], compare_op=ALU.not_equal, fill=1.0, base=0,
                                   pattern=[[-1, P]], channel_multiplier=1))
            constant(pool.affine_select(out=flip[:, :], in_=flip[:, :], compare_op=ALU.not_equal, fill=1.0, base=1 - P,
                               pattern=[[1, P]], channel_multiplier=1))
            constant(pool.memset(ones64[0:64, 0:64], 1.0))
            constant(pool.memset(ones64[64:P, 64:P], 1.0))
            constant(pool.memset(chunk_b[0:64, 64:P], MASKED))
            lows(base, N_CHUNKS)

        @block.scalar
        def _(act):
            def high(n, slot, i16=None):
                if i16 is None:
                    act.wait_ge(landed[slot], 16 * (n // 2 + 1))
                    act.activation(wh[slot][:, :], raw[slot][:, :], ACT.Copy).then_inc(hi_done, 1)
                else:
                    act.wait_ge(landed[slot], i16 + 16 * (n // 2 + 1))
                    act.activation(wh[slot][:, :], raw[slot][:, :], ACT.Copy).then_inc(hi_done, 1)

            def split_next(n, used, value, i=None, per=2):
                if n + 2 >= N_CHUNKS:
                    return
                act.wait_ge(used, value)
                high(n + 2, n % 2, None if i is None else i * (16 * per // 2))

            def square(norm, m, ready, value):
                act.wait_ge(ready, value)
                act.wait_ge(norm.acc, m + 1)
                return act.activation(scratch[0][:, :], h[:, m, :], ACT.Square)

            def norm_root(norm):
                act.wait_ge(norm.ss, 1)
                act.activation(scratch[1][:, :], SS_BANK[:, :], ACT.Sqrt, bias=eps_c[:, :], scale=1.0 / D).then_inc(norm.root, 1)

            def norm_high(norm):
                for k in range(KD):
                    act.wait_ge(norm.tmp, k + 1)
                    act.activation(xh[:, k, :], scratch[(2, 3, 0)[k % 3]][:, :], ACT.Copy).then_inc(norm.hi, 1)

            def attend(a, prob, probT, neg_max, row_sum, col0, after=None):
                for step in range(UNITS + 2):
                    if step < UNITS:
                        U, w = unit(a, step), P * (step % TB + 1)
                        c = col0 + step
                        act.wait_ge(att.max, U + 1)
                        if U >= 3:
                            act.wait_ge(att.pt, U - 2)
                        act.activation(prob[U % 3][:, 0:w], bank[U % 3][:, 0:w], ACT.Exp, bias=neg_max[:, c:c + 1],
                                       scale=1.0, accum_out=row_sum[:, c:c + 1]).then_inc(att.exp, 1)
                        if after is not None and step % TB == TB - 1:
                            after(step // TB)
                    if step >= 2:
                        U, w = unit(a, step - 2), P * ((step - 2) % TB + 1)
                        act.wait_ge(att.pt, U + 1)
                        if U >= 2:
                            act.wait_ge(att.pv, U - 1)
                        act.activation(probT[U % 2][:, 0:w], bank[3 + U % 2][:, 0:w], ACT.Copy).then_inc(att.ptc, 1)

            def mix_high(e0, count, tile0):
                for e in range(count):
                    act.wait_ge(mix.mm, e0 + e + 1)
                    act.activation(xh[:, tile0 + e, :], bank[(7, 0)[e % 2]][:, :], ACT.Copy).then_inc(mix.hi, 1)

            def residual_out(res, norm, base):
                for c in range(KD // 2):
                    split_next(base + c, res.mm, 2 * c + 2)
                    for m in (2 * c, 2 * c + 1):
                        square(norm, m, res.h, m + 1).then_inc(norm.sq, 1)

            def residual_down(res, norm, base):
                def tile(i, m, base, per):
                    for e in range(2):
                        split_next(base + e, res.mm, m * 2 + (e + 1), i, per)
                    if norm is not None:
                        act.wait_ge(res.h, m + 1)
                        act.wait_ge(norm.acc, m + 1)
                        act.activation(scratch[0][:, :], h[:, m, :], ACT.Square).then_inc(norm.sq, 1)

                last = 1 if norm is None else 0
                with act.Fori(0, KD - last) as i:
                    tile(i, i, base, 2)
                for m in range(KD - last, KD):
                    tile(None, m, base + 2 * m, 2)

            def up(L, base):
                with act.Fori(0, KF // 2) as i:
                    def start(r):
                        act.wait_ge(L.mm, i * 4 + (r + 1))
                        act.activation(scratch[r][:, :], bank[r][:, :], ACT.Identity, bias=col(L.b, i * 4 + r),
                                       scale=col(L.w, i * 12 + (3 * r + 2))).then_inc(L.base, 1)

                    start(0)
                    split_next(base, L.mm, i * 4 + 2, i)
                    start(1)
                    for r in range(2):
                        act.wait_ge(L.conv, i * 4 + (r + 1))
                        act.activation(scratch[r][:, :], scratch[r][:, :], ACT.Silu).then_inc(L.silu, 1)
                    start(2)
                    split_next(base + 1, L.mm, i * 4 + 4, i)
                    start(3)
                    for r in range(2):
                        act.wait_ge(L.gated, i * 2 + (r + 1))
                        act.activation(acth[:, i * 2 + r, :], scratch[2 + r][:, :], ACT.Copy).then_inc(L.hi, 1)

            act.wait_ge(cols_landed, 16)
            act.wait_ge(setup1, 4)
            a = COLS["c"][0]
            act.activation(csil[:, :], cols[:, a:a + KD], ACT.Silu).then_inc(csil_done, 1)
            high(0, 0)
            high(1, 1)
            for k in range(KD):
                square(norm_mix, k, x_landed, 16).then_inc(norm_mix.sq, 1)
            norm_root(norm_mix)
            norm_high(norm_mix)
            split_next(0, p1.mm, P1["f"])
            act.wait_ge(forget.dve, 1)
            act.activation(lf[0][:, :], bank[4][:, :], ACT.Abs, bias=col("b_forget")).then_inc(forget.act, 1)
            act.wait_ge(forget.act, 1)
            act.activation(lf[0][:, :], lf[0][:, :], ACT.Exp, scale=-1.0).then_inc(forget.act, 1)
            act.wait_ge(forget.act, 2)
            act.activation(lf[0][:, :], lf[0][:, :], ACT.Ln, bias=ones[:, 0:1]).then_inc(forget.act, 1)
            split_next(1, p1.mm, P1["vg0"])
            split_next(2, p1.mm, P1["vg"][3])
            for t in range(TB):
                act.activation(vg[:, t, :], bank[t][:, :], ACT.Gelu_apprx_tanh).then_inc(p1.act, 1)
            for t in range(4):
                if t % 2:
                    split_next(3 + t // 2, p1.mm, P1["u"][t])
                act.wait_ge(p1.mm, P1["u"][t])
                act.activation(u_sb[:, t, :], bank[4 + t][:, :], ACT.Gelu_apprx_tanh).then_inc(p1.act, 1)
            act.wait_ge(gate.sum, TB)
            act.activation(vrs[:, :], vsum[:, :], ACT.Sqrt, bias=eps_c[:, :], scale=1.0 / HD).then_inc(gate.root, 1)
            act.wait_ge(forget.dve, 4)
            act.activation(dec_q[:, :], dec_all[:, :], ACT.Copy).then_inc(decay.hi, 1)
            for p in range(PAIRS):
                act.wait_ge(p1.mm, P1["q"][p])
                act.activation(q1[:, p, :], bank[2 * p % 4][:, :], ACT.Copy, scale=HD ** -0.5).then_inc(p1.act, 1)
                split_next(5 + p, p1.mm, P1["k"][p])
            split_next(9, p1.mm, P1["v0"])
            split_next(10, p1.mm, P1["v"][3])
            attend(0, prob1, probT1, neg_max1, row_sum1, 0)
            for t in range(4):
                act.wait_ge(mixing.done, t + 1)
                act.activation(xh[:, 4 + t, :], scratch[t][:, :], ACT.Copy).then_inc(mix.hi, 1)
            mix_high(0, 4, 0)
            residual_out(res_out1, norm_ffn, BASE1["out"])
            norm_root(norm_ffn)
            norm_high(norm_ffn)
            up(up1, BASE1["up"])
            residual_down(res_down1, norm_final, BASE1["down"])

            act.wait_ge(res_down1.h, KD)
            act.dma_start(pos_i[:, :], positions.partition_broadcast(P)).then_inc(pos_landed, 16)

            def load_rel(hd):
                src = bass.AP(rel_rows.tensor, hd * REL_LEN, [[1, P], [1, T]])
                act.dma_start(rel[hd % 2][:, :], src).then_inc(rel_landed[hd % 2], 16)

            load_rel(0)
            load_rel(1)
            norm_root(norm_final)
            for k in range(KD):
                square(norm_attn2, k, norm_final.tmp, k + 1).then_inc(norm_attn2.sq, 1)
            norm_root(norm_attn2)
            norm_high(norm_attn2)
            base = N1 + N_DOWN
            act.wait_ge(trig.dve, 8)
            act.activation(turn[:, :], ang[:, :], ACT.Abs).then_inc(trig.act, 1)
            act.wait_ge(trig.act, 1)
            act.activation(q_trig[64:96, :], turn[64:96, :], ACT.Sin, bias=halfpi_c[64:96, :], scale=-1.0).then_inc(trig.act, 1)
            act.activation(k_trig[0:64, :], turn[0:64, :], ACT.Sin, bias=halfpi_c[0:64, :], scale=-1.0).then_inc(trig.act, 1)
            act.activation(q_trig[96:P, :], ang[96:P, :], ACT.Sin).then_inc(trig.act, 1)
            act.activation(k_trig[64:P, :], ang[64:P, :], ACT.Sin).then_inc(trig.act, 1)

            def head_square(out, tile, mm):
                act.wait_ge(p2.mm, mm)
                act.activation(out, tile, ACT.Square).then_inc(head.sq, 1)

            def head_root(job, width, ss_bank, times=1):
                act.wait_ge(head.ss, job + 1)
                if job >= 4:
                    act.wait_ge(head.done, job - 3)
                act.activation(scratch[job % 4][:, :], ss_bank[:, :], ACT.Sqrt, bias=(eps_c if times == 1 else eps64_c)[:, :],
                               scale=float(times * times) / width).then_inc(head.root, 1)

            split_next(base, p2.mm, P2["rope"])
            head_square(sq2[0][:, :], bank[0][:, :], P2["kv"])
            for b in range(2):
                act.activation(sqk[b][64:P, :], bank[1][64:P, :], ACT.Square).then_inc(rope.sq, 1)
            split_next(base + 1, p2.mm, P2["ql"][1])
            head_square(sq2[1][:, :], bank[2][:, :], P2["ql"][0])
            act.wait_ge(norm_attn2.lo, KD)
            head_square(scratch[3][:, :], bank[3][:, :], P2["ql"][1])
            head_root(JOB_KV, P, bank[4])
            head_root(JOB_QL, 2 * P, bank[5])
            act.wait_ge(head.pre, 1)
            act.activation(kvh[:, :], scratch[0][:, :], ACT.Copy).then_inc(lat.hi, 1)
            for t in range(2):
                act.wait_ge(head.pre, 2 + t)
                act.activation(qlh[:, t, :], scratch[2 + t][:, :], ACT.Copy).then_inc(lat.hi, 1)
            split_next(base + 2, p2.mm, P2["v0"])
            split_next(base + 3, p2.mm, P2["v"][3])
            act.wait_ge(lat.lo, 3)
            for p in range(PAIRS + 1):
                if p < PAIRS:
                    for which in range(2):
                        x = job_c(p, which)
                        if x >= 2:
                            act.wait_ge(head.ss, x - 1)
                        head_square(sq2[which][:, :], bank[2 * (p % 2) + which][:, :], P2["qk"[which]][p])
                    split_next(base + 4 + p, p2.mm, P2["k"][p])
                if p:
                    for which in range(2):
                        x = job_c(p - 1, which)
                        head_root(x, HD, bank[6 + which], 1 if which else 8)
            attend(1, prob2, probT2, neg_max2, row_sum2, 0, lambda hd: load_rel(hd + 2) if hd + 2 < HEADS else None)
            mix_high(4, 4, 4)
            for hd in range(HEADS + 1):
                if hd < HEADS:
                    for which in range(2):
                        x = job_m(hd, which)
                        act.wait_ge(head.ss, x - (1 if which == 0 else 3) if hd else x - which)
                        if which == 0:
                            head_square(sq2[hd % 2][:, :], bank[2 * (hd % 2)][:, :], P2["mq"][hd])
                        else:
                            head_square(sqk[hd % 2][0:64, :], bank[2 * (hd % 2) + 1][0:64, :], P2["mk"][hd])
                if hd:
                    for which in range(2):
                        head_root(job_m(hd - 1, which), MLA_QK, bank[6 + which])
            split_next(base + 8, p2.mm, P2["mq"][HEADS - 1])
            split_next(base + 9, p2.mm, P2["mk"][HEADS - 1])
            attend(2, prob2, probT2, neg_max2, row_sum2, UNITS)
            mix_high(8, 4, 0)
            residual_out(res_out2, norm_mlp2, BASE2["out"])
            norm_root(norm_mlp2)
            norm_high(norm_mlp2)
            up(up2, BASE2["up"])
            residual_down(res_down2, None, BASE2["down"])

        @block.vector
        def _(dve):
            def ada_sum(a):
                dve.wait_ge(ada_landed, a * 16 + 16)
                dve.tensor_tensor(ada_raw[:, :, :], ada_raw[:, :, :],
                                  csil[:, :].rearrange("p (k c) -> p k c", c=1).broadcast_to([P, KD, PAIR_COLS]),
                                  ALU.mult).then_inc(ada_scaled, 1)
                dve.wait_ge(ada_scaled, a + 1)
                if not isinstance(a, int) or a > 0:
                    dve.wait_ge(ada_used, a)
                dve.tensor_reduce(ada_acc[:, :], ada_raw[:, :, :].rearrange("p k c -> p c k"), AX_X, ALU.add).then_inc(ada_red, 1)

            def zero(norm):
                dve.memset(ss_acc[:, :], 0.0).then_inc(norm.acc, 1)

            def add_square(norm, m):
                dve.wait_ge(norm.acc, m + 1)
                dve.wait_ge(norm.sq, m + 1)
                dve.tensor_tensor(ss_acc[:, :], ss_acc[:, :], scratch[0][:, :], ALU.add).then_inc(norm.acc, 1)

            def norm_rstd(norm):
                dve.wait_ge(norm.root, 1)
                dve.reciprocal(scratch[1][:, :], scratch[1][:, :]).then_inc(norm.rstd, 1)
                dve.wait_ge(norm.rstd, 1)

            def norm_tiles(norm, scale, shift=None, pre0=0):
                for k in range(KD + 1):
                    if k < KD:
                        tmp = scratch[(2, 3, 0)[k % 3]]
                        if k >= 3:
                            dve.wait_ge(norm.lo, k - 2)
                        if shift is None:
                            dve.scalar_tensor_tensor(tmp[:, :], h[:, k, :], scale(k), scratch[1][:, :], ALU.mult, ALU.mult).then_inc(norm.tmp, 1)
                        else:
                            dve.tensor_tensor(tmp[:, :], h[:, k, :], scratch[1][:, :], ALU.mult).then_inc(pre, 1)
                            dve.wait_ge(pre, pre0 + k + 1)
                            dve.tensor_scalar(tmp[:, :], tmp[:, :], scale(k), shift(k), ALU.mult, ALU.add).then_inc(norm.tmp, 1)
                    if k:
                        j = k - 1
                        dve.wait_ge(norm.hi, j + 1)
                        dve.tensor_tensor(xl[:, j, :], scratch[(2, 3, 0)[j % 3]][:, :], xh[:, j, :].bitcast(F32), ALU.subtract).then_inc(norm.lo, 1)

            def add_residual(res, m, b, value, gain):
                dve.wait_ge(res.mm, value)
                if gain is None:
                    dve.tensor_tensor(h[:, m, :], h[:, m, :], b[:, :], ALU.add).then_inc(res.h, 1)
                else:
                    dve.scalar_tensor_tensor(h[:, m, :], b[:, :], mod[:, gain, bass.ds(m, 1)], h[:, m, :], ALU.mult, ALU.add).then_inc(res.h, 1)

            def residual_out(res, norm, gain, ada_too):
                zero(norm)
                for m in range(KD):
                    if ada_too and m % 4 == 0:
                        ada_sum(m // 4)
                    add_residual(res, m, bank[m % 4], m + 1, gain)
                    add_square(norm, m)

            def residual_down(res, norm, gain):
                if norm is not None:
                    zero(norm)
                with dve.Fori(0, KD // 2) as i:
                    for r in range(2):
                        add_residual(res, i * 2 + r, bank[4 + r], i * 4 + (2 * r + 2), gain)
                        if norm is not None:
                            add_square(norm, i * 2 + r)

            def up(L, ada_too):
                with dve.Fori(0, KF // 2) as i:
                    def conv(r):
                        for tap in (1, 0):
                            d = 2 - tap
                            if tap == 1:
                                dve.wait_ge(L.base, i * 4 + (r + 1))
                            else:
                                dve.wait_ge(L.tap, i * 4 + (r + 1))
                            dve.scalar_tensor_tensor(scratch[r][:, d:T], bank[r][:, 0:T - d], col(L.w, i * 12 + (3 * r + tap)),
                                                     scratch[r][:, d:T], ALU.mult, ALU.add).then_inc(L.tap if tap else L.conv, 1)

                    def gated(r):
                        dve.wait_ge(L.conv, i * 4 + (r + 1))
                        dve.wait_ge(L.silu, i * 2 + (r - 1))
                        dve.tensor_tensor(scratch[r][:, :], scratch[r][:, :], scratch[r - 2][:, :], ALU.mult).then_inc(L.gated, 1)

                    def low(r):
                        dve.wait_ge(L.hi, i * 2 + (r - 1))
                        dve.tensor_tensor(actl[:, i * 2 + (r - 2), :], scratch[r][:, :], acth[:, i * 2 + (r - 2), :].bitcast(F32), ALU.subtract).then_inc(L.lo, 1)

                    if ada_too:
                        ada_sum(i * 2 + 2)
                    conv(0)
                    conv(1)
                    if ada_too:
                        ada_sum(i * 2 + 3)
                    conv(2)
                    gated(2)
                    conv(3)
                    gated(3)
                    low(2)
                    low(3)

            def attend(a, neg_max, row_sum, col0, out, after=None):
                for step in range(UNITS + 3):
                    if step < UNITS:
                        U, w, c = unit(a, step), P * (step % TB + 1), col0 + step
                        dve.wait_ge(att.qk, U + 1)
                        dve.tensor_reduce(neg_max[:, c:c + 1], bank[U % 3][:, 0:w], AX_X, ALU.max, negate=True).then_inc(att.max, 1)
                        if after is not None and step % TB == TB - 1:
                            after(step // TB)
                    if step >= 3:
                        u = step - 3
                        U, c = unit(a, u), col0 + u
                        hd, i = u // TB, u % TB
                        dve.wait_ge(att.exp, U + 1)
                        dve.reciprocal(row_sum[:, c:c + 1], row_sum[:, c:c + 1]).then_inc(att.rinv, 1)
                        dve.wait_ge(att.pv, U + 1)
                        dve.wait_ge(att.rinv, U + 1)
                        dve.tensor_scalar(out[:, i, HD * hd:HD * hd + HD], bank[5 + U % 2][:, 0:HD], row_sum[:, c:c + 1], None, ALU.mult).then_inc(att.o, 1)

            def mix_low(e0, count, tile0, source):
                for e in range(count):
                    dve.wait_ge(mix.hi, e0 + e + 1)
                    dve.tensor_tensor(xl[:, tile0 + e, :], source(e)[:, :], xh[:, tile0 + e, :].bitcast(F32), ALU.subtract).then_inc(mix.lo, 1)

            zero(norm_mix)
            for k in range(KD):
                add_square(norm_mix, k)
            norm_rstd(norm_mix)
            dve.wait_ge(cols_landed, 16)
            norm_tiles(norm_mix, lambda k: col("mix_g", k))
            dve.wait_ge(p1.mm, P1["f"])
            dve.tensor_scalar(lf[1][:, :], bank[4][:, :], col("b_forget"), 0.0, ALU.add, ALU.min).then_inc(forget.dve, 1)
            dve.memset(scratch[0][:, :], 1.0).then_inc(forget.dve, 1)
            dve.wait_ge(forget.act, 3)
            dve.wait_ge(forget.dve, 2)
            dve.tensor_tensor(lf[1][:, :], lf[1][:, :], lf[0][:, :], ALU.subtract).then_inc(forget.dve, 1)
            dve.wait_ge(forget.dve, 3)
            dve.tensor_tensor_scan(dec_all[:, :], scratch[0][:, :], lf[1][:, :], 0.0, ALU.mult, ALU.add).then_inc(forget.dve, 1)
            for t in range(TB):
                dve.wait_ge(p1.act, t + 1)
                dve.tensor_tensor(scratch[2 + t % 2][:, :], vg[:, t, :], vg[:, t, :], ALU.mult).then_inc(gate.sq, 1)
                dve.wait_ge(gate.sq, t + 1)
                dve.tensor_reduce(vsum[:, HEADS * t:HEADS * t + HEADS], scratch[2 + t % 2][:, :].rearrange("p (g d) -> p g d", g=HEADS),
                                  AX_X, ALU.add).then_inc(gate.sum, 1)
            dve.wait_ge(decay.hi, 1)
            dve.tensor_tensor(lf[0][:, :], dec_all[:, :], dec_q[:, :].bitcast(F32), ALU.subtract).then_inc(decay.dve, 1)
            dve.wait_ge(decay.dve, 1)
            dve.tensor_scalar(dec_all[0:32, :], dec_q[0:32, :].bitcast(F32), -1.0, None, ALU.mult).then_inc(decay.dve, 1)
            dve.tensor_scalar(dec_all[32:64, :], lf[0][32:64, :], -1.0, None, ALU.mult).then_inc(decay.dve, 1)
            dve.memset(dec_all[64:P, :], 1.0).then_inc(decay.dve, 1)
            dve.tensor_copy(dec_q[96:P, :], lf[0][96:P, :]).then_inc(decay.dve, 1)
            dve.wait_ge(decay.dve, 5)
            dve.tensor_scalar(dec_q[0:64, :], dec_all[0:64, :], 0.0, 1.0, ALU.mult, ALU.add).then_inc(decay.dve, 1)
            dve.wait_ge(decay.dve, 6)
            dve.wait_ge(gate.root, 1)
            dve.reciprocal(vrs[:, :], vrs[:, :]).then_inc(gate.rstd, 1)
            dve.wait_ge(gate.rstd, 1)
            for t in range(TB):
                groups = vg[:, t, :].rearrange("p (g d) -> p g d", g=HEADS)
                dve.tensor_tensor(groups, groups,
                                  vrs[:, HEADS * t:HEADS * t + HEADS].rearrange("p (g c) -> p g c", c=1).broadcast_to([P, HEADS, HD]),
                                  ALU.mult).then_inc(gate.done, 1)
            for p in range(PAIRS):
                dve.wait_ge(p1.mm, P1["k"][p])
                dve.tensor_copy(k1[:, p, :], bank[(2 * p + 1) % 4][:, :]).then_inc(p1.dve, 1)
            for t in range(TB):
                dve.wait_ge(p1.mm, P1["v"][t])
                dve.tensor_copy(v1[:, t, :], bank[4 + t][:, :]).then_inc(p1.dve, 1)

            def decay_head(hd):
                if hd < HEADS:
                    dve.tensor_scalar(dec_k[hd % 2][:, :], dec_all[:, :], col("head_row", hd), None, ALU.mult).then_inc(decay.head, 1)

            decay_head(0)
            decay_head(1)
            attend(0, neg_max1, row_sum1, 0, o1, lambda hd: decay_head(hd + 2))
            dve.wait_ge(small_landed, 32)
            for t in range(4):
                dve.wait_ge(mixing.mm, t + 1)
                dve.scalar_tensor_tensor(scratch[t][:, :].rearrange("p (n i) -> p n i", n=TB), bank[1 + t][:, :].rearrange("p (n i) -> p n i", n=TB),
                                         col("gmlp_g", t), bsp[:, t:t + 1, :].broadcast_to([P, TB, P]), ALU.mult, ALU.add).then_inc(mixing.bias, 1)
                dve.wait_ge(mixing.bias, t + 1)
                dve.tensor_tensor(scratch[t][:, :], scratch[t][:, :], u_sb[:, t, :], ALU.mult).then_inc(mixing.done, 1)
            mix_low(0, 4, 4, lambda e: scratch[e])
            mix_low(4, 4, 0, lambda e: bank[(7, 0)[e % 2]])
            dve.wait_ge(csil_done, 1)
            residual_out(res_out1, norm_ffn, None, True)
            norm_rstd(norm_ffn)
            norm_tiles(norm_ffn, lambda k: col("ffn_g", k))
            up(up1, True)
            dve.wait_ge(ada_used, N_ADA)
            a = COLS["b_ada"][0]
            dve.tensor_tensor(mod[:, :, :], MOD_BANK[:, 0:6 * KD].rearrange("p (j k) -> p j k", j=6),
                              cols[:, a:a + 6 * KD].rearrange("p (j k) -> p j k", j=6), ALU.add).then_inc(mod_done, 1)
            dve.wait_ge(mod_done, 1)
            for j, g in enumerate(("attn2_g", "mlp2_g")):
                a = COLS[g][0]
                dve.scalar_tensor_tensor(modA[:, j, :], mod[:, 3 * j + 1, :], 1.0, cols[:, a:a + KD], ALU.add, ALU.mult).then_inc(mod_done, 1)
            residual_down(res_down1, norm_final, None)

            norm_rstd(norm_final)
            zero(norm_attn2)
            for k in range(KD):
                dve.scalar_tensor_tensor(h[:, k, :], h[:, k, :], col("final_g", k), scratch[1][:, :], ALU.mult, ALU.mult).then_inc(norm_final.tmp, 1)
            for k in range(KD):
                add_square(norm_attn2, k)
            norm_rstd(norm_attn2)
            dve.wait_ge(mod_done, 3)
            norm_tiles(norm_attn2, lambda k: modA[:, 0, k:k + 1], lambda k: mod[:, 0, k:k + 1], 0)
            TURNS = 1.5 * 2.0 ** 23
            C1, C2 = 6.28125, 507.0 / 2 ** 18
            C3 = float(2 * np.pi - C1 - C2)
            dve.wait_ge(pos_landed, 16)
            steps = [
                lambda: dve.tensor_copy(ang[:, :], pos_i[:, :]),
                lambda: dve.tensor_scalar(ang[:, :], ang[:, :], col("inv_freq"), None, ALU.mult),
                lambda: dve.tensor_scalar(turn[:, :], ang[:, :], float(0.5 / np.pi), TURNS, ALU.mult, ALU.add),
                lambda: dve.tensor_scalar(turn[:, :], turn[:, :], -TURNS, None, ALU.add),
                lambda: dve.scalar_tensor_tensor(ang[:, :], turn[:, :], -C1, ang[:, :], ALU.mult, ALU.add),
                lambda: dve.scalar_tensor_tensor(ang[:, :], turn[:, :], -C2, ang[:, :], ALU.mult, ALU.add),
                lambda: dve.scalar_tensor_tensor(ang[:, :], turn[:, :], -C3, ang[:, :], ALU.mult, ALU.add),
                lambda: dve.tensor_scalar(ang[:, :], ang[:, :], 3.1415925, -3.1415925, ALU.min, ALU.max),
            ]
            for n, step in enumerate(steps):
                step().then_inc(trig.dve, 1)
                dve.wait_ge(trig.dve, n + 1)
            dve.wait_ge(trig.act, 5)
            dve.wait_ge(setup2, 14)
            dve.tensor_scalar(q_trig[:, :], q_trig[:, :], col("mq_g"), col("q_sign"), ALU.mult, ALU.mult).then_inc(trig.row, 1)
            dve.tensor_scalar(k_trig[:, :], k_trig[:, :], col("mkr_g"), col("k_sign"), ALU.mult, ALU.mult).then_inc(trig.row, 1)
            dve.wait_ge(trig.row, 2)
            dve.wait_ge(rope.sq, 2)
            dve.tensor_tensor(k_rope[64:P, :], bank[1][64:P, :], k_trig[64:P, :], ALU.mult).then_inc(rope.dve, 1)
            dve.tensor_tensor(turn[64:P, :], bank[1][0:64, :], k_trig[0:64, :], ALU.mult).then_inc(rope.dve, 1)
            dve.wait_ge(rope.dve, 2)
            dve.tensor_tensor(k_rope[64:P, :], k_rope[64:P, :], turn[64:P, :], ALU.add).then_inc(rope.dve, 1)

            def head_rstd(job):
                dve.wait_ge(head.root, job + 1)
                dve.reciprocal(scratch[job % 4][:, :], scratch[job % 4][:, :]).then_inc(head.rstd, 1)
                dve.wait_ge(head.rstd, job + 1)
                return scratch[job % 4]

            r = head_rstd(JOB_KV)
            dve.scalar_tensor_tensor(r[:, :], bank[0][:, :], col("kvl_g"), r[:, :], ALU.mult, ALU.mult).then_inc(head.pre, 1)
            r = head_rstd(JOB_QL)
            for t in range(2):
                dve.scalar_tensor_tensor(scratch[2 + t][:, :], bank[2 + t][:, :], col("ql_g", t), r[:, :], ALU.mult, ALU.mult).then_inc(head.pre, 1)
            dve.wait_ge(lat.hi, 1)
            dve.tensor_tensor(kvl[:, :], scratch[0][:, :], kvh[:, :].bitcast(F32), ALU.subtract).then_inc(lat.lo, 1)
            for t in range(2):
                dve.wait_ge(lat.hi, 2 + t)
                dve.tensor_tensor(qll[:, t, :], scratch[2 + t][:, :], qlh[:, t, :].bitcast(F32), ALU.subtract).then_inc(lat.lo, 1)
            for n, t in enumerate(CV_ORDER):
                dve.wait_ge(p2.mm, P2["v"][n])
                dve.tensor_copy(v2[:, t, :], bank[4 + t][:, :]).then_inc(p2.dve, 1)
            for p in range(PAIRS):
                for which, (out, g) in enumerate(((cq, "cq_g"), (ck, "ck_g"))):
                    r = head_rstd(job_c(p, which))
                    dve.scalar_tensor_tensor(out[:, p, :], bank[2 * (p % 2) + which][:, :], col(g), r[:, :], ALU.mult, ALU.mult).then_inc(head.done, 1)
            attend(1, neg_max2, row_sum2, 0, o2)
            mix_low(8, 4, 4, lambda e: bank[(7, 0)[e % 2]])
            for t in range(TB):
                dve.wait_ge(p2.mm, P2["mv"][t])
                dve.tensor_copy(v2[:, t, :], bank[4 + t % 2][:, :]).then_inc(p2.dve, 1)
            for hd in range(HEADS):
                tile = bank[2 * (hd % 2)]
                r = head_rstd(job_m(hd, 0))
                dve.tensor_tensor(mq[:, hd, :], tile[:, :], q_trig[:, :], ALU.mult).then_inc(head.pre, 1)
                dve.wait_ge(head.pre, 4 + 2 * hd)
                dve.tensor_tensor(mq[:, hd, :], mq[:, hd, :], r[:, :], ALU.mult).then_inc(head.done, 1)
                tile = bank[2 * (hd % 2) + 1]
                r = head_rstd(job_m(hd, 1))
                dve.scalar_tensor_tensor(mk[0:64, hd, :], tile[0:64, :], col_at("mk_g", 0, 64), r[0:64, :], ALU.mult, ALU.mult).then_inc(head.pre, 1)
                dve.tensor_tensor(mk[64:P, hd, :], k_rope[64:P, :], r[64:P, :], ALU.mult).then_inc(head.done, 1)
            attend(2, neg_max2, row_sum2, UNITS, o2)
            mix_low(12, 4, 0, lambda e: bank[(7, 0)[e % 2]])
            residual_out(res_out2, norm_mlp2, 2, False)
            norm_rstd(norm_mlp2)
            norm_tiles(norm_mlp2, lambda k: modA[:, 1, k:k + 1], lambda k: mod[:, 3, k:k + 1], KD)
            up(up2, False)
            residual_down(res_down2, None, 5)

        @block.tensor
        def _(pe):
            def split_product(out, lhs, rhs, first, last):
                for n, (a, b) in enumerate(((0, 0), (0, 1), (1, 0))):
                    ins = pe.matmul(out, lhs[a], rhs[b], start=first and n == 0, stop=last and n == 2)
                return ins

            def weights(slot, a, b):
                return wh[slot][:, a:b], wl[slot][:, a:b]

            def inputs(k, a=0, b=T):
                return xh[:, k, a:b], xl[:, k, a:b]

            def features_tile(out, slot, half, ready=None):
                for k in range(KD):
                    if ready is not None:
                        pe.wait_ge(ready, k + 1)
                    a = PAIR_COLS * k + P * half
                    ins = split_product(out[:, :], weights(slot, a, a + P), inputs(k), k == 0, k == KD - 1)
                return ins

            def tokens_tiles(banks, order, slots, n0, mm, ready=None):
                for c in range(2):
                    pe.wait_ge(lo_done, n0 + c + 1)
                    for t in order:
                        if c == 0 and ready is not None:
                            ready(t)
                        for kk in range(4):
                            k = 4 * c + kk
                            ins = split_product(banks[t][:, :], inputs(k, P * t, P * t + P), weights(slots[c], 512 * kk, 512 * kk + 512),
                                                k == 0, k == KD - 1)
                        if c == 1 or t == order[-1]:
                            ins.then_inc(mm, 1)

            def norm_sum(norm):
                pe.wait_ge(norm.acc, KD + 1)
                pe.matmul(SS_BANK[:, :], ones[:, :], ss_acc[:, :], start=True, stop=True).then_inc(norm.ss, 1)

            def attend(a, scores, v, prob, probT, ident):
                for step in range(UNITS + 3):
                    if step < UNITS:
                        U, hd, i = unit(a, step), step // TB, step % TB
                        if U >= 3:
                            pe.wait_ge(att.exp, U - 2)
                        scores(hd, i, bank[U % 3], P * (i + 1)).then_inc(att.qk, 1)
                    if 2 <= step < UNITS + 2:
                        U, i = unit(a, step - 2), (step - 2) % TB
                        pe.wait_ge(att.exp, U + 1)
                        if U >= 2:
                            pe.wait_ge(att.ptc, U - 1)
                        for j in range(i + 1):
                            ins = pe.transpose(bank[3 + U % 2][:, P * j:P * j + P], prob[U % 3][:, P * j:P * j + P], ident[:, :])
                        ins.then_inc(att.pt, 1)
                    if step >= 3:
                        u = step - 3
                        U, hd, i = unit(a, u), u // TB, u % TB
                        pe.wait_ge(att.ptc, U + 1)
                        if U >= 2:
                            pe.wait_ge(att.o, U - 1)
                        for j in range(i + 1):
                            ins = pe.matmul(bank[5 + U % 2][:, 0:HD], probT[U % 2][:, P * j:P * j + P], v[:, j, HD * hd:HD * hd + HD],
                                            start=j == 0, stop=j == i)
                        ins.then_inc(att.pv, 1)

            def transpose_heads(a, out, ident, lo0):
                pe.wait_ge(att.o, unit(a, UNITS))
                for e in range(4):
                    if e >= 2:
                        pe.wait_ge(mix.lo, lo0 + e - 1)
                    for t in range(TB):
                        ins = pe.transpose(bank[(7, 0)[e % 2]][:, P * t:P * t + P], out[:, t, P * e:P * e + P], ident[:, :])
                    ins.then_inc(mix.mm, 1)

            def ada_columns(a):
                pe.wait_ge(ada_red, a + 1)
                for j in range(2):
                    ins = pe.matmul(MOD_BANK[:, bass.ds(a * 2 + j, 1)], ada_acc[:, P * j:P * j + P], ones[:, 0:1], start=True, stop=True)
                ins.then_inc(ada_used, 1)

            def residual_out(res, base, ada_too):
                for m in range(KD):
                    n = base + m // 2
                    if m % 2 == 0:
                        pe.wait_ge(lo_done, n + 1)
                    if m >= 4:
                        pe.wait_ge(res.h, m - 3)
                    features_tile(bank[m % 4], n % 2, m % 2).then_inc(res.mm, 1)
                    if ada_too and m % 4 == 1:
                        ada_columns(m // 4)

            def residual_down(res, base):
                def two_tiles(i, first=False):
                    m0, c0 = (0, base) if first else (2, base + 4)
                    for r in range(2):
                        for e in range(2):
                            slot = (base + e) % 2
                            pe.wait_ge(lo_done, i * 4 + (c0 + 2 * r + e + 1))
                            if e == 0 and not first:
                                pe.wait_ge(res.h, i * 2 + (m0 + r - 1))
                            for kk in range(KF // 2):
                                k = KF // 2 * e + kk
                                ins = split_product(bank[4 + r][:, :], weights(slot, P * kk, P * kk + P), (acth[:, k, :], actl[:, k, :]),
                                                    k == 0, k == KF - 1)
                            ins.then_inc(res.mm, 1)

                two_tiles(0, True)
                with pe.Fori(0, KD // 2 - 1) as i:
                    two_tiles(i)

            def up(L, norm, base, ada_too):
                def two_chunks(i, first=False):
                    c0 = 0 if first else 2
                    for c in range(2):
                        pe.wait_ge(lo_done, i * 2 + (base + c0 + c + 1))
                        for half in range(2):
                            r = 2 * c + half
                            if not first:
                                if r < 2:
                                    pe.wait_ge(L.gated, i * 2 + (r + 1))
                                else:
                                    pe.wait_ge(L.lo, i * 2 + (r - 1))
                            features_tile(bank[r], (base + c) % 2, half, norm.lo if first and r == 0 else None).then_inc(L.mm, 1)
                        if ada_too:
                            ada_columns(i * 2 + (2 + c0 + c))

                two_chunks(0, True)
                with pe.Fori(0, KF // 2 - 1) as i:
                    two_chunks(i)

            pe.wait_ge(setup1, 11)
            norm_sum(norm_mix)
            pe.wait_ge(lo_done, 1)
            features_tile(bank[4], 0, 0, norm_mix.lo).then_inc(p1.mm, 1)
            tokens_tiles(bank[0:4], range(TB), (1, 0), BASE1["vg"], p1.mm)
            for t in range(4):
                n = BASE1["u"] + t // 2
                pe.wait_ge(lo_done, n + 1)
                if t == 0:
                    pe.wait_ge(forget.act, 1)
                    pe.wait_ge(forget.dve, 1)
                features_tile(bank[4 + t], n % 2, t % 2).then_inc(p1.mm, 1)
            for p in range(PAIRS):
                n = BASE1["qk"] + p
                pe.wait_ge(lo_done, n + 1)
                for half in range(2):
                    t = 2 * p + half
                    if t < 4:
                        pe.wait_ge(p1.act, t + 1)
                    elif half == 0:
                        pe.wait_ge(p1.act, 9 + p - 2)
                    else:
                        pe.wait_ge(p1.dve, p - 1)
                    features_tile(bank[t % 4], n % 2, half).then_inc(p1.mm, 1)
            n = BASE1["v"]
            tokens_tiles(bank[4:8], range(TB), (n % 2, (n + 1) % 2), n, p1.mm,
                         lambda t: pe.wait_ge(p1.act, 5 + t))

            def rows(hd):
                return slice(HD * (hd % 2), HD * (hd % 2) + HD)

            def forgetting(hd, i, out, w):
                r = rows(hd)
                pe.matmul(out[:, 0:w], q1[r, hd // 2, P * i:P * i + P], k1[r, hd // 2, 0:w], start=True, stop=False)
                pe.wait_ge(decay.head, hd + 1)
                pe.matmul(out[:, 0:w], dec_q[:, P * i:P * i + P], dec_k[hd % 2][:, 0:w], start=False, stop=False)
                return pe.matmul(out[:, w - P:w], ident_b1[:, :], causal_b[:, :], start=False, stop=True)

            pe.wait_ge(p1.act, 12)
            pe.wait_ge(p1.dve, 8)
            attend(0, forgetting, v1, prob1, probT1, ident1)
            pe.wait_ge(gate.done, TB)
            for t in range(4):
                for n in range(TB):
                    for g in (2 * t, 2 * t + 1):
                        a = HD * (g % 2)
                        ins = pe.matmul(bank[1 + t][a:a + HD, P * n:P * n + P], vg[:, n, HD * g:HD * g + HD], wsT[:, g, :], start=True, stop=True)
                ins.then_inc(mixing.mm, 1)
            transpose_heads(0, o1, ident1, 4)
            pe.wait_ge(mix.lo, 8)
            residual_out(res_out1, BASE1["out"], True)
            norm_sum(norm_ffn)
            up(up1, norm_ffn, BASE1["up"], True)
            pe.wait_ge(up1.lo, KF)
            residual_down(res_down1, BASE1["down"])
            norm_sum(norm_final)

            norm_sum(norm_attn2)
            base = N1 + N_DOWN
            pe.wait_ge(setup2, 14)

            def head_sum(job, out, ones_of, squares):
                pe.wait_ge(head.sq, N_SQ[job])
                for n, sq in enumerate(squares):
                    ins = pe.matmul(out[:, :], ones_of[:, :], sq[:, :], start=n == 0, stop=n == len(squares) - 1)
                ins.then_inc(head.ss, 1)

            pe.wait_ge(lo_done, base + 1)
            features_tile(bank[0], base % 2, 0, norm_attn2.lo).then_inc(p2.mm, 1)
            features_tile(bank[1], base % 2, 1).then_inc(p2.mm, 1)
            pe.wait_ge(lo_done, base + 2)
            for half in range(2):
                features_tile(bank[2 + half], (base + 1) % 2, half).then_inc(p2.mm, 1)
            head_sum(JOB_KV, bank[4], ones, [sq2[0]])
            head_sum(JOB_QL, bank[5], ones, [sq2[1], scratch[3]])

            def sums_taken(t):
                if t < 2:
                    pe.wait_ge(head.root, t + 1)

            n = BASE2["cv"]
            tokens_tiles(bank[4:8], CV_ORDER, (n % 2, (n + 1) % 2), n, p2.mm, sums_taken)
            for p in range(PAIRS + 1):
                if p < PAIRS:
                    n = BASE2["cqk"] + p
                    pe.wait_ge(lo_done, n + 1)
                    for which in range(2):
                        if p < 2:
                            pe.wait_ge(lat.lo, 3)
                            pe.wait_ge(rope.dve, 2)
                        else:
                            pe.wait_ge(head.done, 2 * (p - 2) + which + 1)
                        features_tile(bank[2 * (p % 2) + which], n % 2, which).then_inc(p2.mm, 1)
                if p:
                    for which in range(2):
                        if p == 1:
                            pe.wait_ge(p2.dve, TB)
                        else:
                            pe.wait_ge(head.root, job_c(p - 2, which) + 1)
                        head_sum(job_c(p - 1, which), bank[6 + which], ones64, [sq2[which]])

            def chunked(hd, i, out, w):
                r = rows(hd)
                pe.matmul(out[:, 0:w], cq[r, hd // 2, P * i:P * i + P], ck[r, hd // 2, 0:w], start=True, stop=False)
                if i == 0:
                    pe.wait_ge(rel_landed[hd % 2], 16 * (hd // 2 + 1))
                pe.matmul(out[:, 0:w], flip[:, :], rel[hd % 2][:, T - w:T], start=False, stop=False)
                return pe.matmul(out[:, w - P:w], ident_b2[:, :], chunk_b[:, :], start=False, stop=True)

            pe.wait_ge(head.done, 2 * PAIRS)
            attend(1, chunked, v2, prob2, probT2, ident2)
            transpose_heads(1, o2, ident2, 8)
            n = BASE2["mkv"]
            pe.wait_ge(lo_done, n + 1)
            for t in range(TB):
                if t < 2:
                    pe.wait_ge(att.o, unit(2, 0))
                else:
                    pe.wait_ge(p2.dve, TB + t - 1)
                split_product(bank[4 + t % 2][:, :], (kvh[:, P * t:P * t + P], kvl[:, P * t:P * t + P]), weights(n % 2, 1024, 1536),
                              True, True).then_inc(p2.mm, 1)
            nq = BASE2["mq"]
            for hd in range(HEADS + 1):
                if hd < HEADS:
                    if hd == 0:
                        pe.wait_ge(mix.lo, 12)
                    if hd >= 2:
                        pe.wait_ge(head.done, 2 * PAIRS + 2 * (hd - 1))
                    for k in range(2):
                        a = 1024 * k + P * hd
                        ins = split_product(bank[2 * (hd % 2)][:, :], weights(nq % 2, a, a + P), (qlh[:, k, :], qll[:, k, :]), k == 0, k == 1)
                    ins.then_inc(p2.mm, 1)
                    split_product(bank[2 * (hd % 2) + 1][:, :], weights(n % 2, P * hd, P * hd + P), (kvh[:, :], kvl[:, :]), True, True).then_inc(p2.mm, 1)
                if hd:
                    for which in range(2):
                        x = job_m(hd - 1, which)
                        if hd >= 2:
                            pe.wait_ge(head.root, x - 1)
                        head_sum(x, bank[6 + which], ones96, [(sq2, sqk)[which][(hd - 1) % 2]])

            def latent(hd, i, out, w):
                pe.matmul(out[:, 0:w], mq[:, hd, P * i:P * i + P], mk[:, hd, 0:w], start=True, stop=False)
                return pe.matmul(out[:, w - P:w], ident_b2[:, :], chunk_b[:, :], start=False, stop=True)

            pe.wait_ge(head.done, 2 * PAIRS + 2 * HEADS)
            attend(2, latent, v2, prob2, probT2, ident2)
            transpose_heads(2, o2, ident2, 12)
            pe.wait_ge(mix.lo, 16)
            residual_out(res_out2, BASE2["out"], False)
            norm_sum(norm_mlp2)
            up(up2, norm_mlp2, BASE2["up"], False)
            pe.wait_ge(up2.lo, KF)
            residual_down(res_down2, BASE2["down"])


def pair_chunks(w):
    n = w.shape[1] // PAIR_COLS
    return w.reshape(KD, P, n, PAIR_COLS).transpose(2, 1, 0, 3).reshape(n * P, CHUNK)


def wide_chunks(w):
    return w.reshape(2, 4, P, 512).transpose(0, 2, 1, 3).reshape(2 * P, CHUNK)


def down_chunks(w):
    return w.reshape(2, KF // 2, P, KD, P).transpose(3, 0, 2, 1, 4).reshape(N_DOWN * P, DOWN_CHUNK)


def up_chunks(w, gate, value):
    g, v = pair_chunks(w[:, gate * FF:(gate + 1) * FF]), pair_chunks(w[:, value * FF:(value + 1) * FF])
    return np.stack([g.reshape(-1, P, CHUNK), v.reshape(-1, P, CHUNK)], 1).reshape(-1, CHUNK)


def pad_columns(w, n):
    return np.concatenate([w, np.zeros((w.shape[0], n - w.shape[1]), w.dtype)], 1)


def up_columns(a, gate, value):
    t = a.reshape(a.shape[0], 2, KF // 2, 2, P)
    return np.stack([t[:, gate], t[:, value]], 2).reshape(a.shape[0], UP_TILES, P)


def kernel(**inputs):
    import concourse.bacc as bacc
    from concourse.bass_utils import run_bass_kernel_spmd

    f = {k: np.asarray(v) for k, v in inputs.items()}
    f32 = np.float32

    w = f["w_in"][0]
    wf = np.zeros((D, 2 * P), f32)
    for quadrant in range(4):
        wf[:, 32 * quadrant:32 * quadrant + HEADS] = w[:, 2560:2568]
    qk = np.concatenate([np.concatenate([w[:, P * p:P * p + P], w[:, 512 + P * p:512 + P * p + P]], 1) for p in range(PAIRS)], 1)
    stream1 = np.concatenate([
        pair_chunks(wf), wide_chunks(w[:, 2048:2560]), pair_chunks(w[:, 1536:2048]), pair_chunks(qk), wide_chunks(w[:, 1024:1536]),
        pair_chunks(f["w_out"][0]), up_chunks(f["w_up"][0], 1, 0)])
    w = f["w_in_2"][0]
    x, xs = w[:, 384:416], np.concatenate([w[:, 400:416], w[:, 384:400]], 1)
    kvr = np.concatenate([w[:, 256:384], x, x, xs, xs], 1)
    ca = w[:, 416:]
    cqk = np.concatenate([np.concatenate([ca[:, P * p:P * p + P], ca[:, 512 + P * p:512 + P * p + P]], 1) for p in range(PAIRS)], 1)
    wq = f["w_q_up_2"][0].reshape(2 * P, HEADS, MLA_QK)
    wq = np.concatenate([wq, wq[:, :, 80:96], wq[:, :, 64:80]], 2).reshape(2, P, HEADS * P)
    wkv = f["w_kv_up_2"][0].reshape(P, HEADS, P)
    wk = np.concatenate([wkv[:, :, :HD], np.zeros((P, HEADS, HD), f32)], 2).reshape(P, HEADS * P)
    mkv = pad_columns(np.concatenate([wk, wkv[:, :, HD:].reshape(P, 512)], 1), CHUNK)
    stream2 = np.concatenate([
        pair_chunks(kvr), pair_chunks(w[:, :256]), wide_chunks(ca[:, 1024:]), pair_chunks(cqk),
        wq.transpose(1, 0, 2).reshape(P, CHUNK), mkv, pair_chunks(f["w_out_2"][0]), up_chunks(f["w_up_2"][0], 0, 1)])

    parts = {}

    def features(name, a):
        parts[name] = a.reshape(-1, P).T

    features("mix_g", f["norm_mix_g"][0])
    features("ffn_g", f["norm_ffn_g"][0])
    features("final_g", f["norm_final_g"])
    features("attn2_g", f["g_attn_norm_2"][0])
    features("mlp2_g", f["g_mlp_norm_2"][0])
    features("gmlp_g", f["gmlp_norm_g"][0])
    parts["conv_w"] = up_columns(f["conv_w"][0], 1, 0).transpose(2, 1, 0).reshape(P, -1)
    parts["conv_b"] = up_columns(f["conv_b"], 1, 0)[0].T
    parts["conv_w2"] = up_columns(f["conv_w_2"][0], 0, 1).transpose(2, 1, 0).reshape(P, -1)
    parts["conv_b2"] = up_columns(f["conv_b_2"], 0, 1)[0].T
    features("b_ada", f["b_ada_2"][0])
    features("c", f["c_2"][0])
    features("ql_g", f["g_q_latent_2"][0])
    features("kvl_g", f["g_kv_latent_2"][0])
    g = f["g_mla_q_2"][0]
    features("mq_g", np.concatenate([g, g[80:96], g[64:80]]))
    g = f["g_mla_k_2"][0]
    features("mk_g", np.concatenate([g[:64], g[:64]]))
    swapped = np.concatenate([g[80:96], g[64:80]])
    features("mkr_g", np.concatenate([g[64:96], g[64:96], swapped, swapped]))
    features("cq_g", np.tile(f["g_ca_q_2"][0], 2))
    features("ck_g", np.tile(f["g_ca_k_2"][0], 2))
    b_forget = np.zeros(P, f32)
    for quadrant in range(4):
        b_forget[32 * quadrant:32 * quadrant + HEADS] = f["b_forget"][0]
    features("b_forget", b_forget)
    parts["head_row"] = (np.arange(P)[:, None] % 32 == np.arange(HEADS)[None, :]).astype(f32)
    half = ROPE // 2
    inv = np.power(f32(ROPE_THETA), -np.arange(half, dtype=f32) / f32(half)).astype(f32)
    features("inv_freq", np.tile(inv, P // half))
    sign = np.concatenate([-np.ones(half, f32), np.ones(half, f32)])
    scale = f32(MLA_QK ** -0.5)
    features("q_sign", np.concatenate([np.ones(96, f32), sign]) * scale)
    features("k_sign", np.concatenate([np.ones(64, f32), sign, sign]))
    packed = np.concatenate([parts[name].astype(f32) for name in COLS], 1)

    distance = np.clip(T - 1 - np.arange(REL_LEN), -REL_CLIP, REL_CLIP)
    arrays = {
        "xT": f["x"][0].T,
        "cols_in": packed,
        "stream1": stream1,
        "down1": down_chunks(f["w_down"][0]),
        "stream2": stream2,
        "down2": down_chunks(f["w_down_2"][0]),
        "ada": pair_chunks(f["w_ada_2"][0]),
        "w_spatial_T": f["w_spatial"][0].transpose(2, 0, 1).reshape(P, HEADS * P),
        "b_spatial_rows": np.repeat(f["b_spatial"][0].reshape(4, 2, 1, P), HD, axis=2).transpose(1, 2, 0, 3).reshape(P, 4 * P),
        "positions": f["positions_2"].reshape(1, T).astype(np.int32),
        "rel_rows": f["rel_bias_2"][0][:, distance + REL_CLIP],
    }
    nc = bacc.Bacc("TRN2", target_bir_lowering=False, num_devices=1)
    args = {}
    for name, a in arrays.items():
        a = arrays[name] = np.ascontiguousarray(a)
        args[name] = nc.dram_tensor(name, a.shape, mybir.dt.from_np(a.dtype), kind="ExternalInput").ap()
    outT = nc.dram_tensor("outT", (D, T), F32, kind="ExternalOutput").ap()
    build(nc, **args, outT=outT)
    r = run_bass_kernel_spmd(nc, [arrays], core_ids=[0])
    return np.ascontiguousarray(r.results[0]["outT"].T).reshape(1, T, D)
```

```python
from contextlib import ExitStack

import numpy as np

import concourse.bass as bass
from concourse import mybir

ALU = mybir.AluOpType
ACT = mybir.ActivationFunctionType
F32 = mybir.dt.float32
F32R = mybir.dt.float32r
BF16 = mybir.dt.bfloat16
I32 = mybir.dt.int32
AX_X = mybir.AxisListType.X

P = 128
D = 1024
T = 512
KD = D // P
TB = T // P
HEADS = 8
HD = 64
PAIRS = HEADS // 2
FF = 2816
KF = FF // P
UP_TILES = 2 * KF
EPS = 1e-6
MLA_QK = 96
ROPE = 32
ROPE_THETA = 10000.0
REL_CLIP = 128
REL_LEN = T + P

CHUNK = 2048
DOWN_CHUNK = KF // 2 * P
PAIR_COLS = CHUNK // KD
ADA_COLS = 6 * D
N_ADA = ADA_COLS // PAIR_COLS
MASKED = -1e30
X_PARTS = 4

STREAM1 = [("ua", 1), ("vg", 2), ("ub", 1), ("f", 1), ("v", 2), ("qk", PAIRS), ("out", KD // 2), ("up", KF)]
STREAM2 = [("kvr", 1), ("ql", 1), ("cv", 2), ("cqk", PAIRS), ("mq", 1), ("mkv", 1), ("out", KD // 2), ("up", KF)]
N1 = sum(n for _, n in STREAM1)
N2 = sum(n for _, n in STREAM2)
N_DOWN = 2 * KD
BASE1 = {}
BASE2 = {}
at = 0
for name, count in STREAM1:
    BASE1[name] = at
    at += count
BASE1["down"] = at
at += N_DOWN
for name, count in STREAM2:
    BASE2[name] = at
    at += count
BASE2["down"] = at
N_CHUNKS = at + N_DOWN

COLS = {}
n_cols = 0
for name, count in [
    ("mix_g", KD), ("ffn_g", KD), ("final_g", KD), ("attn2_g", KD), ("mlp2_g", KD), ("gmlp_g", 4),
    ("conv_w", 3 * UP_TILES), ("conv_b", UP_TILES), ("conv_w2", 3 * UP_TILES), ("conv_b2", UP_TILES),
    ("b_ada", N_ADA * 2), ("c", KD), ("ql_g", 2), ("kvl_g", 1), ("mq_g", 1), ("mk_g", 1), ("mkr_g", 1),
    ("cq_g", 1), ("ck_g", 1), ("b_forget", 1), ("head_row", HEADS), ("inv_freq", 1), ("q_sign", 1), ("k_sign", 1),
]:
    COLS[name] = (n_cols, count)
    n_cols += count


def build(nc, xT, cols_in, stream1, down1, stream2, down2, ada, w_spatial_T, b_spatial_rows, positions, rel_rows, outT):
    ctx = ExitStack()
    with ctx:
        def sem(name):
            return ctx.enter_context(nc.semaphore(name))

        def sb(name, shape, dt=F32, scope=ctx):
            return scope.enter_context(nc.sbuf_tensor(name, shape, dt))

        bank = [ctx.enter_context(nc.psum_tensor(f"bank{b}", [P, 512], F32)) for b in range(8)]
        SS_BANK, MOD_BANK = bank[6], bank[7]

        h = sb("h", [P, KD, T])
        xh = sb("xh", [P, KD, T], F32R)
        xl = sb("xl", [P, KD, T], F32R)
        raw = [sb(f"raw{s}", [P, CHUNK]) for s in range(2)]
        wh = [sb(f"wh{s}", [P, CHUNK], F32R) for s in range(2)]
        wl = [sb(f"wl{s}", [P, CHUNK], F32R) for s in range(2)]
        ada_raw = sb("ada_raw", [P, KD, PAIR_COLS])
        ada_acc = sb("ada_acc", [P, PAIR_COLS])
        scratch = [sb(f"scratch{s}", [P, T]) for s in range(4)]
        ss_acc = sb("ss_acc", [P, T])
        trig_room = ada_raw[:, :, :].rearrange("p k c -> p (k c)")
        q_trig, k_trig, ang, turn = [trig_room[:, T * b:T * b + T] for b in range(4)]
        pos_i = turn.bitcast(I32)
        cols = sb("cols", [P, n_cols])
        csil = sb("csil", [P, KD])
        mod = sb("mod", [P, 6, KD])
        modA = sb("modA", [P, 2, KD])
        ones = sb("ones", [P, P])
        eps_c = sb("eps_c", [P, 1])
        halfpi_c = sb("halfpi_c", [P, 1])
        eps64_c = sb("eps64_c", [P, 1])
        eps2_c = sb("eps2_c", [P, 1])
        final_w = sb("final_w", [P, KD])

        def col(name, j=0):
            return cols[:, bass.ds(COLS[name][0] + j, 1)]

        def col_at(name, a, b):
            c = COLS[name][0]
            return cols[a:b, c:c + 1]

        with ExitStack() as s:
            acth = sb("acth", [P, KF, T], F32R, s)
            actl = sb("actl", [P, KF, T], F32R, s)

        with ExitStack() as s:
            v1 = sb("v1", [P, TB, 512], F32, s)
            vg = sb("vg", [P, TB, 512], F32, s)
            u_sb = sb("u_sb", [P, 4, T], F32, s)
            q1 = sb("q1", [P, PAIRS, T], F32, s)
            k1 = sb("k1", [P, PAIRS, T], F32, s)
            dec_q = sb("dec_q", [P, T], F32R, s)
            dec_all = sb("dec_all", [P, T], F32, s)
            dec_k = [sb(f"dec_k{b}", [P, T], F32R, s) for b in range(2)]
            lf = [sb(f"lf{b}", [P, T], F32, s) for b in range(2)]
            prob1 = [sb(f"prob1{b}", [P, T], F32, s) for b in range(4)]
            probT1 = [sb(f"probT1{b}", [P, T], F32, s) for b in range(2)]
            o1 = sb("o1", [P, TB, 512], F32, s)
            wsT = sb("wsT", [P, HEADS, P], F32, s)
            bsp = sb("bsp", [P, 4, P], F32, s)
            vsum = sb("vsum", [P, TB * HEADS], F32, s)
            vrs = sb("vrs", [P, TB * HEADS], F32, s)
            neg_max1 = sb("neg_max1", [P, 32], F32, s)
            row_sum1 = sb("row_sum1", [P, 32], F32, s)
            ident1 = sb("ident1", [P, P], F32, s)
            ident_b1 = sb("ident_b1", [P, P], BF16, s)
            causal_b = sb("causal_b", [P, P], BF16, s)

        with ExitStack() as s:
            qlh = sb("qlh", [P, 2, T], F32R, s)
            qll = sb("qll", [P, 2, T], F32R, s)
            kvh = sb("kvh", [P, T], F32R, s)
            kvl = sb("kvl", [P, T], F32R, s)
            k_rope = sb("k_rope", [P, T], F32, s)
            v2 = sb("v2", [P, TB, 512], F32, s)
            o2 = sb("o2", [P, TB, 512], F32, s)
            prob2 = [sb(f"prob2{b}", [P, T], F32, s) for b in range(4)]
            probT2 = [sb(f"probT2{b}", [P, T], F32, s) for b in range(2)]
            neg_max2 = sb("neg_max2", [P, 64], F32, s)
            row_sum2 = sb("row_sum2", [P, 64], F32, s)
            ident2 = sb("ident2", [P, P], F32, s)
            ident_b2 = sb("ident_b2", [P, P], BF16, s)
            flip = sb("flip", [P, P], F32, s)
            flip_r = sb("flip_r", [P, P], F32R, s)
            ones96 = sb("ones96", [P, P], F32, s)
            ones64 = sb("ones64", [P, P], F32, s)
            chunk_b = sb("chunk_b", [P, P], BF16, s)
            sq2 = [sb(f"sq2{b}", [P, T], F32, s) for b in range(2)]
            sqk = [sb(f"sqk{b}", [P, T], F32, s) for b in range(2)]
            with ExitStack() as s2:
                cq = sb("cq", [P, PAIRS, T], F32, s2)
                ck = sb("ck", [P, PAIRS, T], F32, s2)
                rel = [sb(f"rel{b}", [P, T], F32, s2) for b in range(2)]
                rel_h = [sb(f"rel_h{b}", [P, T], F32R, s2) for b in range(2)]
                rel_l = [sb(f"rel_l{b}", [P, T], F32R, s2) for b in range(2)]
            with ExitStack() as s2:
                mq = sb("mq", [P, HEADS, T], F32, s2)
                mk = sb("mk", [P, HEADS, T], F32, s2)

        landed = [sem(f"landed{s}") for s in range(2)]
        hi_done = sem("hi_done")
        lo_done = sem("lo_done")
        ada_landed, ada_scaled, ada_red, ada_used = [sem(f"ada_{x}") for x in ("landed", "scaled", "red", "used")]
        x_landed = [sem(f"x_landed{b}") for b in range(X_PARTS)]
        cols_landed, small_landed, pos_landed = [sem(f"{x}_landed") for x in ("cols", "small", "pos")]
        rel_landed = [sem(f"rel_landed{b}") for b in range(2)]
        rel_high, rel_low = sem("rel_high"), sem("rel_low")
        out_done = sem("out_done")
        setup1, setup2 = sem("setup1"), sem("setup2")
        csil_done = sem("csil_done")

        class Stage:
            pass

        def sems(stage, *names):
            return [sem(f"{stage}_{x}") for x in names]

        def norm_stage(name):
            s = Stage()
            s.sq, s.acc, s.ss, s.rstd, s.tmp, s.hi, s.lo = sems(name, "sq", "acc", "ss", "rstd", "tmp", "hi", "lo")
            return s

        def residual_stage(name):
            s = Stage()
            s.mm, s.h = sems(name, "mm", "h")
            return s

        def up_stage(name, w, b):
            s = Stage()
            s.w, s.b = w, b
            s.mm, s.base, s.tap, s.conv, s.silu, s.gated, s.hi, s.lo = sems(name, "mm", "base", "tap", "conv", "silu", "gated", "hi", "lo")
            return s

        norm_mix, norm_ffn, norm_final, norm_attn2, norm_mlp2 = [norm_stage(x) for x in ("nmix", "nffn", "nfin", "natt", "nmlp")]
        mod_done = sem("mod_done")
        res_out1, res_down1, res_out2, res_down2 = [residual_stage(x) for x in ("ro1", "rd1", "ro2", "rd2")]
        up1, up2 = up_stage("up1", "conv_w", "conv_b"), up_stage("up2", "conv_w2", "conv_b2")
        p1 = Stage()
        p1.mm, p1.act, p1.dve = sems("p1", "mm", "act", "dve")
        p2 = Stage()
        p2.mm, p2.dve = sems("p2", "mm", "dve")
        forget = Stage()
        forget.act, forget.dve = sems("forget", "act", "dve")
        decay = Stage()
        decay.hi, decay.dve, decay.head = sems("decay", "hi", "dve", "head")
        gate = Stage()
        gate.sq, gate.sum, gate.rstd, gate.done = sems("gate", "sq", "sum", "rstd", "done")
        mixing = Stage()
        mixing.mm, mixing.bias, mixing.done = sems("mixing", "mm", "bias", "done")
        att = Stage()
        att.qk, att.max, att.exp, att.pt, att.ptc, att.pv, att.rinv, att.o = sems("att", "qk", "max", "exp", "pt", "ptc", "pv", "rinv", "o")
        mix = Stage()
        mix.mm, mix.hi, mix.lo = sems("mix", "mm", "hi", "lo")
        trig = Stage()
        trig.dve, trig.act, trig.row = sems("trig", "dve", "act", "row")
        weighted_acc = sem("weighted_acc")
        rope = Stage()
        rope.dve, rope.sq = sems("rope", "dve", "sq")
        head = Stage()
        head.sq, head.ss, head.root, head.rstd, head.pre, head.done = sems("head", "sq", "ss", "root", "rstd", "pre", "done")
        lat = Stage()
        lat.hi, lat.lo = sems("lat", "hi", "lo")

        P1 = {"u": [1, 2, 8, 9], "vg0": 3, "vg": [4, 5, 6, 7], "f": 10, "v0": 11, "v": [12, 13, 14, 15],
              "q": [16, 18, 20, 22], "k": [17, 19, 21, 23]}
        P2 = {"kv": 1, "rope": 2, "ql": [3, 4], "v0": 5, "v": [6, 7, 8, 9], "q": [10, 12, 14, 16], "k": [11, 13, 15, 17],
              "mv": [18, 19, 20, 21], "mq": [22 + 2 * x for x in range(HEADS)], "mk": [23 + 2 * x for x in range(HEADS)]}
        CV_ORDER = [2, 3, 0, 1]

        JOB_KV, JOB_QL = 0, 1

        def job_c(p, which):
            return 2 + 2 * p + which

        def job_m(hd, which):
            return 2 + 2 * PAIRS + 2 * hd + which

        N_SQ = {}
        for x in range(2 + 2 * PAIRS + 2 * HEADS):
            N_SQ[x] = x + 1 + (x >= JOB_QL)

        def c_bank(p):
            return (0, 2, 4, 2)[p]

        def m_bank(hd):
            return 2 * (hd % 3)

        UNITS = HEADS * TB
        PAIR_UNITS = 2 * TB
        Q_STEPS = TB
        LAG = 3
        S_BANKS = [bank[0:3], bank[0:3] + bank[7:8], bank[0:3] + bank[7:8]]
        NEXT_BANK = bank[7]
        HT_BANKS = [bank[7], bank[0], bank[1], bank[2]]
        MIX_BANKS = [bank[4], bank[7], bank[5], bank[6]]
        OUT_BANKS = bank[3:7]

        def unit(a, u):
            return a * UNITS + u

        def scores_bank(a, U):
            return S_BANKS[a][U % len(S_BANKS[a])]

        block = ctx.enter_context(nc.Block())

        @block.sync
        def _(sp):
            def chunk(source, j, n, slot, width, first=False):
                if not first:
                    sp.wait_ge(lo_done, n - 1)
                sp.dma_start(raw[slot][:, 0:width], source[bass.ds(j * P, P), :]).then_inc(landed[slot], 16)

            def ada_chunk(a, first=False):
                if not first:
                    sp.wait_ge(ada_red, a)
                sp.dma_start(ada_raw[:, :, :], ada[bass.ds(a * P, P), :].rearrange("p (k c) -> p k c", k=KD)).then_inc(ada_landed, 16)

            def stream(source, base, j0, count, with_ada=None):
                with sp.Fori(0, count // 2) as i:
                    for s in range(2):
                        chunk(source, i * 2 + (j0 + s), i * 2 + (base + j0 + s), (base + j0 + s) % 2, source.shape[1])
                        if with_ada:
                            with_ada(i, s)

            for b in range(X_PARTS):
                n = KD // X_PARTS
                sp.dma_start(h[:, n * b:n * b + n, :], xT[n * P * b:n * P * (b + 1), :].rearrange("(k p) t -> p k t", p=P)).then_inc(x_landed[b], 16)
            chunk(stream1, 0, 0, 0, CHUNK, first=True)
            chunk(stream1, 1, 1, 1, CHUNK, first=True)
            sp.dma_start(wsT[:, :, :], w_spatial_T.rearrange("j (g i) -> j g i", g=HEADS)).then_inc(small_landed, 16)
            sp.dma_start(bsp[:, :, :], b_spatial_rows.rearrange("p (t i) -> p t i", t=4)).then_inc(small_landed, 16)
            ada_chunk(0, first=True)
            for n in range(2, BASE1["out"]):
                chunk(stream1, n, n, n % 2, CHUNK)

            def ada_out(i, s):
                if s:
                    ada_chunk(i + 1)

            def ada_up(i, s):
                ada_chunk(i * 2 + (3 + s))

            stream(stream1, 0, BASE1["out"], KD // 2, ada_out)
            for s in range(2):
                n = BASE1["up"] + s
                chunk(stream1, n, n, n % 2, CHUNK)
            stream(stream1, 0, BASE1["up"] + 2, KF - 2, ada_up)
            ada_chunk(N_ADA - 1)
            stream(down1, BASE1["down"], 0, N_DOWN)
            base = N1 + N_DOWN
            for j in range(BASE2["out"] - base):
                chunk(stream2, j, base + j, (base + j) % 2, CHUNK)
            stream(stream2, base, BASE2["out"] - base, KD // 2)
            stream(stream2, base, BASE2["up"] - base, KF)
            stream(down2, BASE2["down"], 0, N_DOWN)
            for m in range(KD):
                sp.wait_ge(res_down2.h, m + 1)
                sp.dma_start(outT[m * P:(m + 1) * P, :], h[:, m, :]).then_inc(out_done, 16)
            sp.wait_ge(out_done, 16 * KD)

        @block.gpsimd
        def _(pool):
            def low(n, slot):
                pool.wait_ge(hi_done, n + 1)
                pool.tensor_tensor(wl[slot][:, :], raw[slot][:, :], wh[slot][:, :].bitcast(F32), ALU.subtract).then_inc(lo_done, 1)

            def lows(a, b):
                with pool.Fori(0, (b - a) // 2) as i:
                    for s in range(2):
                        low(i * 2 + (a + s), (a + s) % 2)
                if (b - a) % 2:
                    low(b - 1, (b - 1) % 2)

            pool.memset(ones[:, :], 1.0).then_inc(setup1, 1)
            pool.memset(eps_c[:, :], EPS).then_inc(setup1, 1)
            pool.memset(halfpi_c[:, :], float(np.pi / 2)).then_inc(setup1, 1)
            pool.memset(eps64_c[:, :], HD * EPS).then_inc(setup1, 1)
            pool.memset(eps2_c[:, :], EPS * EPS).then_inc(setup1, 1)
            pool.memset(ident1[:, :], 0.0).then_inc(setup1, 1)
            pool.memset(ident_b1[:, :], 0.0).then_inc(setup1, 1)
            pool.memset(causal_b[:, :], 0.0).then_inc(setup1, 1)
            pool.wait_ge(setup1, 8)
            for t in (ident1, ident_b1):
                pool.affine_select(out=t[:, :], in_=t[:, :], compare_op=ALU.not_equal, fill=1.0, base=0,
                                   pattern=[[-1, P]], channel_multiplier=1).then_inc(setup1, 1)
            pool.affine_select(out=causal_b[:, :], in_=causal_b[:, :], compare_op=ALU.is_ge, fill=MASKED, base=0,
                               pattern=[[-1, P]], channel_multiplier=1).then_inc(setup1, 1)
            low(0, 0)
            low(1, 1)
            pool.wait_ge(small_landed, 32)
            pool.affine_select(out=wsT[:, :, :], in_=wsT[:, :, :], compare_op=ALU.is_ge, fill=0.0, base=0,
                               pattern=[[0, HEADS], [1, P]], channel_multiplier=-1).then_inc(setup1, 1)
            base = N1 + N_DOWN
            lows(2, base + 2)
            pool.wait_ge(res_down1.h, KD)
            made = 0

            def constant(ins):
                nonlocal made
                made += 1
                ins.then_inc(setup2, 1)
                pool.wait_ge(setup2, made)

            constant(pool.memset(ident2[:, :], 0.0))
            constant(pool.memset(ident_b2[:, :], 0.0))
            constant(pool.memset(flip[:, :], 0.0))
            constant(pool.memset(ones96[0:96, :], 1.0))
            constant(pool.memset(ones96[96:P, :], 0.0))
            constant(pool.memset(ones64[:, :], 0.0))
            constant(pool.memset(chunk_b[:, :], 0.0))
            for t in (ident2, ident_b2):
                constant(pool.affine_select(out=t[:, :], in_=t[:, :], compare_op=ALU.not_equal, fill=1.0, base=0,
                                   pattern=[[-1, P]], channel_multiplier=1))
            constant(pool.affine_select(out=flip[:, :], in_=flip[:, :], compare_op=ALU.not_equal, fill=1.0, base=1 - P,
                               pattern=[[1, P]], channel_multiplier=1))
            constant(pool.tensor_copy(flip_r[:, :], flip[:, :]))
            constant(pool.memset(ones64[0:64, 0:64], 1.0))
            constant(pool.memset(ones64[64:P, 64:P], 1.0))
            constant(pool.memset(chunk_b[0:64, 64:P], MASKED))
            lows(base + 2, BASE2["out"])
            for hd in range(HEADS):
                b = hd % 2
                pool.wait_ge(rel_landed[b], 16 * (hd // 2 + 1))
                if hd >= 2:
                    pool.wait_ge(att.qk, unit(1, TB * (hd - 1)))
                pool.tensor_copy(rel_h[b][:, :], rel[b][:, :]).then_inc(rel_high, 1)
                pool.wait_ge(rel_high, hd + 1)
                pool.tensor_tensor(rel_l[b][:, :], rel[b][:, :], rel_h[b][:, :].bitcast(F32), ALU.subtract).then_inc(rel_low, 1)
            lows(BASE2["out"], N_CHUNKS)

        LN_EXP = "natural_log_exp_and_others"

        @block.scalar
        def _(act):
            def high(n, slot, i16=None):
                if i16 is None:
                    act.wait_ge(landed[slot], 16 * (n // 2 + 1))
                    act.activation(wh[slot][:, :], raw[slot][:, :], ACT.Copy).then_inc(hi_done, 1)
                else:
                    act.wait_ge(landed[slot], i16 + 16 * (n // 2 + 1))
                    act.activation(wh[slot][:, :], raw[slot][:, :], ACT.Copy).then_inc(hi_done, 1)

            def split_next(n, used, value, i=None, per=2):
                if n + 2 >= N_CHUNKS:
                    return
                act.wait_ge(used, value)
                high(n + 2, n % 2, None if i is None else i * (16 * per // 2))

            def square(norm, m, ready, value):
                act.wait_ge(ready, value)
                act.wait_ge(norm.acc, m + 1)
                return act.activation(scratch[0][:, :], h[:, m, :], ACT.Square)

            def rsqrt(out, mean_of, width, eps, done, count, times=1):
                act.activation(out, mean_of, ACT.Ln, bias=eps[:, :], scale=float(times * times) / width).then_inc(done, 1)
                act.wait_ge(done, count + 1)
                act.activation(out, out, ACT.Exp, scale=-0.5).then_inc(done, 1)

            def norm_rsqrt(norm):
                act.wait_ge(norm.ss, 1)
                rsqrt(scratch[1][:, :], SS_BANK[:, :], D, eps_c, norm.rstd, 0)

            def norm_high(norm, shift=None, aside=None):
                for k in range(KD):
                    if k == KD // 2 and aside is not None:
                        aside()
                    act.wait_ge(norm.tmp, k + 1)
                    tile = scratch[(2, 3, 0)[k % 3]][:, :]
                    if shift is None:
                        act.activation(xh[:, k, :], tile, ACT.Copy).then_inc(norm.hi, 1)
                    else:
                        act.activation(xh[:, k, :], tile, ACT.Identity, bias=mod[:, shift, k:k + 1]).then_inc(norm.hi, 1)

            def attend(a, prob, probT, neg_max, row_sum, col0, after=None, beside=None):
                for step in range(UNITS + LAG):
                    if beside is not None:
                        beside(step)
                    if step < UNITS:
                        U, w = unit(a, step), P * (step % TB + 1)
                        c = col0 + step
                        act.wait_ge(att.max, U + 1)
                        if U >= 4:
                            act.wait_ge(att.pt, U - 3)
                        act.activation(prob[U % 4][:, 0:w], scores_bank(a, U)[:, 0:w], ACT.Exp, bias=neg_max[:, c:c + 1],
                                       scale=1.0, accum_out=row_sum[:, c:c + 1]).then_inc(att.exp, 1)
                        if after is not None and step % TB == TB - 1:
                            after(step // TB)
                    if step >= LAG:
                        U, w = unit(a, step - LAG), P * ((step - LAG) % TB + 1)
                        act.wait_ge(att.pt, U + 1)
                        if U >= 2:
                            act.wait_ge(att.pv, U - 1)
                        act.activation(probT[U % 2][:, 0:w], bank[3 + U % 2][:, 0:w], ACT.Copy).then_inc(att.ptc, 1)

            def mix_high(e0, count, tile0):
                for e in range(count):
                    act.wait_ge(mix.mm, e0 + e + 1)
                    act.activation(xh[:, tile0 + e, :], HT_BANKS[e][:, :], ACT.Copy).then_inc(mix.hi, 1)

            def residual_out(res, norm, base):
                for c in range(KD // 2):
                    split_next(base + c, res.mm, 2 * c + 2)
                    for m in (2 * c, 2 * c + 1):
                        square(norm, m, res.h, m + 1).then_inc(norm.sq, 1)

            def residual_down(res, norm, base, aside=None):
                def tile(m, base, i=None):
                    for e in range(2):
                        split_next(base + e, res.mm, m * 2 + (e + 1), i)
                    if norm is not None:
                        act.wait_ge(res.h, m + 1)
                        act.wait_ge(norm.acc, m + 1)
                        act.activation(scratch[0][:, :], h[:, m, :], ACT.Square).then_inc(norm.sq, 1)

                tile(0, base)
                if aside is not None:
                    aside()
                last = 1 if norm is None else 0
                with act.Fori(0, KD - 1 - last) as i:
                    tile(i + 1, base + 2, i)
                if last:
                    tile(KD - 1, base + 2 * (KD - 1))

            def up(L, base):
                act.preload_act_table(ACT.Silu)
                with act.Fori(0, KF // 2) as i:
                    def start(r):
                        act.wait_ge(L.mm, i * 4 + (r + 1))
                        act.activation(scratch[r][:, :], bank[r][:, :], ACT.Identity, bias=col(L.b, i * 4 + r),
                                       scale=col(L.w, i * 12 + (3 * r + 2))).then_inc(L.base, 1)

                    start(0)
                    split_next(base, L.mm, i * 4 + 2, i)
                    start(1)
                    for r in range(2):
                        act.wait_ge(L.conv, i * 4 + (r + 1))
                        act.activation(scratch[r][:, :], scratch[r][:, :], ACT.Silu).then_inc(L.silu, 1)
                    start(2)
                    split_next(base + 1, L.mm, i * 4 + 4, i)
                    start(3)
                    for r in range(2):
                        act.wait_ge(L.gated, i * 2 + (r + 1))
                        act.activation(acth[:, i * 2 + r, :], scratch[2 + r][:, :], ACT.Copy).then_inc(L.hi, 1)

            act.dma_start(cols[:, :], cols_in).then_inc(cols_landed, 16)
            act.preload_act_table(ACT.Silu)
            act.wait_ge(cols_landed, 16)
            a = COLS["c"][0]
            act.activation(csil[:, :], cols[:, a:a + KD], ACT.Silu).then_inc(csil_done, 1)
            act.preload_act_table_set(LN_EXP)
            act.wait_ge(setup1, 5)
            for k in range(KD):
                act.wait_ge(x_landed[k * X_PARTS // KD], 16)
                if k >= 4:
                    act.wait_ge(norm_mix.acc, k - 2)
                act.activation(scratch[k % 4][:, :], h[:, k, :], ACT.Square).then_inc(norm_mix.sq, 1)
            high(0, 0)
            norm_rsqrt(norm_mix)
            norm_high(norm_mix, None, lambda: high(1, 1))
            def gelu_u(t):
                act.wait_ge(p1.mm, P1["u"][t])
                act.activation(u_sb[:, t, :], bank[4 + t][:, :], ACT.Gelu_apprx_tanh).then_inc(p1.act, 1)

            split_next(0, p1.mm, P1["u"][1])
            gelu_u(0)
            gelu_u(1)
            split_next(1, p1.mm, P1["vg0"])
            split_next(2, p1.mm, P1["vg"][3])
            for t in range(TB):
                act.activation(vg[:, t, :], bank[t][:, :], ACT.Gelu_apprx_tanh).then_inc(p1.act, 1)
            split_next(3, p1.mm, P1["u"][3])
            gelu_u(2)
            gelu_u(3)
            split_next(4, p1.mm, P1["f"])
            act.preload_act_table_set(LN_EXP)
            act.wait_ge(gate.sum, TB)
            rsqrt(vrs[:, :], vsum[:, :], HD, eps_c, gate.rstd, 0)
            act.wait_ge(forget.dve, 1)
            act.activation(lf[0][:, :], bank[4][:, :], ACT.Abs, bias=col("b_forget")).then_inc(forget.act, 1)
            act.wait_ge(forget.act, 1)
            act.activation(lf[0][:, :], lf[0][:, :], ACT.Exp, scale=-1.0).then_inc(forget.act, 1)
            act.wait_ge(forget.act, 2)
            act.activation(lf[0][:, :], lf[0][:, :], ACT.Ln, bias=ones[:, 0:1]).then_inc(forget.act, 1)
            act.wait_ge(forget.dve, 4)
            act.activation(dec_q[:, :], dec_all[:, :], ACT.Copy).then_inc(decay.hi, 1)
            split_next(5, p1.mm, P1["v0"])
            split_next(6, p1.mm, P1["v"][3])

            def queries(p):
                act.wait_ge(p1.mm, P1["q"][p])
                act.activation(q1[:, p, :], (bank[0] if p == 0 else NEXT_BANK)[:, :], ACT.Copy, scale=HD ** -0.5).then_inc(p1.act, 1)

            queries(0)
            split_next(7, p1.mm, P1["k"][0])

            def beside(step):
                p = step // PAIR_UNITS + 1
                if p < PAIRS and step % PAIR_UNITS == Q_STEPS:
                    queries(p)
                if p < PAIRS and step % PAIR_UNITS == PAIR_UNITS - 1:
                    split_next(7 + p, p1.mm, P1["k"][p])
                if step >= UNITS - 4 and step < UNITS:
                    t = step - (UNITS - 4)
                    act.wait_ge(p1.mm, P1["k"][PAIRS - 1])
                    act.wait_ge(mixing.done, t + 1)
                    act.activation(xh[:, 4 + t, :], scratch[t][:, :], ACT.Copy).then_inc(mix.hi, 1)

            attend(0, prob1, probT1, neg_max1, row_sum1, 0, None, beside)
            mix_high(0, 4, 0)
            residual_out(res_out1, norm_ffn, BASE1["out"])
            norm_rsqrt(norm_ffn)
            norm_high(norm_ffn)
            up(up1, BASE1["up"])

            def sines():
                act.wait_ge(trig.dve, 8)
                act.activation(turn, ang, ACT.Abs).then_inc(trig.act, 1)
                act.wait_ge(trig.act, 1)
                act.activation(q_trig[64:96, :], turn[64:96, :], ACT.Sin, bias=halfpi_c[64:96, :], scale=-1.0).then_inc(trig.act, 1)
                act.activation(k_trig[0:64, :], turn[0:64, :], ACT.Sin, bias=halfpi_c[0:64, :], scale=-1.0).then_inc(trig.act, 1)
                act.activation(q_trig[96:P, :], ang[96:P, :], ACT.Sin).then_inc(trig.act, 1)
                act.activation(k_trig[64:P, :], ang[64:P, :], ACT.Sin).then_inc(trig.act, 1)
                act.preload_act_table_set(LN_EXP)

            act.wait_ge(ada_red, N_ADA)
            act.dma_start(pos_i, positions.partition_broadcast(P)).then_inc(pos_landed, 16)
            residual_down(res_down1, norm_final, BASE1["down"], sines)

            act.wait_ge(res_down1.h, KD)
            def load_rel(hd):
                if hd >= 2:
                    act.wait_ge(rel_low, hd - 1)
                src = bass.AP(rel_rows.tensor, hd * REL_LEN, [[1, P], [1, T]])
                act.dma_start(rel[hd % 2][:, :], src).then_inc(rel_landed[hd % 2], 16)

            load_rel(0)
            load_rel(1)
            act.wait_ge(norm_final.ss, 1)
            rsqrt(scratch[1][:, :], bank[0][:, :], D, eps2_c, norm_attn2.rstd, 0)
            norm_high(norm_attn2, 0)
            rsqrt(ss_acc[:, :], SS_BANK[:, :], D, eps_c, norm_final.rstd, 0)
            base = N1 + N_DOWN

            def head_square(out, tile, mm):
                act.wait_ge(p2.mm, mm)
                act.activation(out, tile, ACT.Square).then_inc(head.sq, 1)

            def head_root(job, width, ss_bank, times=1):
                act.wait_ge(head.ss, job + 1)
                if job >= 4:
                    act.wait_ge(head.done, job - 3)
                r = scratch[job % 4]
                act.activation(r[:, :], ss_bank[:, :], ACT.Ln, bias=(eps_c if times == 1 else eps64_c)[:, :],
                               scale=float(times * times) / width).then_inc(head.root, 1)
                act.wait_ge(head.root, job + 1)
                act.activation(r[:, :], r[:, :], ACT.Exp, scale=-0.5).then_inc(head.rstd, 1)

            split_next(base, p2.mm, P2["rope"])
            head_square(sq2[0][:, :], bank[0][:, :], P2["kv"])
            for b in range(2):
                act.activation(sqk[b][64:P, :], bank[1][64:P, :], ACT.Square).then_inc(rope.sq, 1)
            split_next(base + 1, p2.mm, P2["ql"][1])
            head_square(sq2[1][:, :], bank[2][:, :], P2["ql"][0])
            act.wait_ge(norm_attn2.lo, KD)
            head_square(scratch[3][:, :], bank[3][:, :], P2["ql"][1])
            head_root(JOB_KV, P, bank[4])
            head_root(JOB_QL, 2 * P, bank[5])
            act.wait_ge(head.pre, 1)
            act.activation(kvh[:, :], scratch[0][:, :], ACT.Copy).then_inc(lat.hi, 1)
            for t in range(2):
                act.wait_ge(head.pre, 2 + t)
                act.activation(qlh[:, t, :], scratch[2 + t][:, :], ACT.Copy).then_inc(lat.hi, 1)
            split_next(base + 2, p2.mm, P2["v0"])
            split_next(base + 3, p2.mm, P2["v"][3])
            act.wait_ge(lat.lo, 3)
            for p in range(PAIRS + 1):
                if p < PAIRS:
                    for which in range(2):
                        x = job_c(p, which)
                        if x >= 2:
                            act.wait_ge(head.ss, x - 1)
                        head_square(sq2[which][:, :], bank[c_bank(p) + which][:, :], P2["qk"[which]][p])
                    split_next(base + 4 + p, p2.mm, P2["k"][p])
                if p:
                    for which in range(2):
                        x = job_c(p - 1, which)
                        head_root(x, HD, bank[6 + which], 1 if which else 8)
            attend(1, prob2, probT2, neg_max2, row_sum2, 0, lambda hd: load_rel(hd + 2) if hd + 2 < HEADS else None)
            mix_high(4, 4, 4)
            for hd in range(HEADS + 1):
                if hd < HEADS:
                    for which in range(2):
                        x = job_m(hd, which)
                        act.wait_ge(head.ss, x - 3 if hd else x - which)
                        if which == 0:
                            head_square(sq2[hd % 2][:, :], bank[m_bank(hd)][:, :], P2["mq"][hd])
                        else:
                            head_square(sqk[hd % 2][0:64, :], bank[m_bank(hd) + 1][0:64, :], P2["mk"][hd])
                if hd:
                    for which in range(2):
                        head_root(job_m(hd - 1, which), MLA_QK, bank[6 + which])
            split_next(base + 8, p2.mm, P2["mq"][HEADS - 1])
            split_next(base + 9, p2.mm, P2["mk"][HEADS - 1])
            attend(2, prob2, probT2, neg_max2, row_sum2, UNITS)
            mix_high(8, 4, 0)
            residual_out(res_out2, norm_mlp2, BASE2["out"])
            norm_rsqrt(norm_mlp2)
            norm_high(norm_mlp2, 3)
            up(up2, BASE2["up"])
            residual_down(res_down2, None, BASE2["down"])

        @block.vector
        def _(dve):
            def ada_sum(a):
                dve.wait_ge(ada_landed, a * 16 + 16)
                dve.tensor_tensor(ada_raw[:, :, :], ada_raw[:, :, :],
                                  csil[:, :].rearrange("p (k c) -> p k c", c=1).broadcast_to([P, KD, PAIR_COLS]),
                                  ALU.mult).then_inc(ada_scaled, 1)
                dve.wait_ge(ada_scaled, a + 1)
                if not isinstance(a, int) or a > 0:
                    dve.wait_ge(ada_used, a)
                dve.tensor_reduce(ada_acc[:, :], ada_raw[:, :, :].rearrange("p k c -> p c k"), AX_X, ALU.add).then_inc(ada_red, 1)

            def zero(norm):
                dve.memset(ss_acc[:, :], 0.0).then_inc(norm.acc, 1)

            def add_square(norm, m):
                dve.wait_ge(norm.acc, m + 1)
                dve.wait_ge(norm.sq, m + 1)
                dve.tensor_tensor(ss_acc[:, :], ss_acc[:, :], scratch[0][:, :], ALU.add).then_inc(norm.acc, 1)

            def norm_tiles(norm, scale, shift=None):
                dve.wait_ge(norm.rstd, 2)
                for k in range(KD + 1):
                    if k < KD:
                        if k >= 3:
                            dve.wait_ge(norm.lo, k - 2)
                        dve.scalar_tensor_tensor(scratch[(2, 3, 0)[k % 3]][:, :], h[:, k, :], scale(k), scratch[1][:, :], ALU.mult, ALU.mult).then_inc(norm.tmp, 1)
                    if k:
                        j = k - 1
                        tile, hi = scratch[(2, 3, 0)[j % 3]][:, :], xh[:, j, :].bitcast(F32)
                        dve.wait_ge(norm.hi, j + 1)
                        if shift is None:
                            dve.tensor_tensor(xl[:, j, :], tile, hi, ALU.subtract).then_inc(norm.lo, 1)
                        else:
                            dve.scalar_tensor_tensor(xl[:, j, :], tile, shift(j), hi, ALU.add, ALU.subtract).then_inc(norm.lo, 1)

            def add_residual(res, m, b, value, gain):
                dve.wait_ge(res.mm, value)
                if gain is None:
                    dve.tensor_tensor(h[:, m, :], h[:, m, :], b[:, :], ALU.add).then_inc(res.h, 1)
                else:
                    dve.scalar_tensor_tensor(h[:, m, :], b[:, :], mod[:, gain, bass.ds(m, 1)], h[:, m, :], ALU.mult, ALU.add).then_inc(res.h, 1)

            def residual_out(res, norm, gain, ada_too):
                zero(norm)
                for m in range(KD):
                    if ada_too and m % 4 == 0:
                        ada_sum(m // 4)
                    add_residual(res, m, OUT_BANKS[m % 4], m + 1, gain)
                    add_square(norm, m)

            def residual_down(res, gain):
                with dve.Fori(0, KD // 2) as i:
                    for r in range(2):
                        add_residual(res, i * 2 + r, bank[4 + r], i * 4 + (2 * r + 2), gain)

            def residual_down_final(res, norm, weighted, aside):
                zero(norm)
                dve.memset(weighted[:, :], 0.0).then_inc(weighted_acc, 1)

                def tiles(m0, i):
                    for r in range(2):
                        m = i * 2 + (m0 + r)
                        add_residual(res, m, bank[4 + r], i * 4 + (2 * m0 + 2 * r + 2), None)
                        dve.wait_ge(weighted_acc, m + 1)
                        dve.wait_ge(norm.sq, m + 1)
                        dve.scalar_tensor_tensor(weighted[:, :], scratch[0][:, :], final_w[:, bass.ds(m, 1)], weighted[:, :],
                                                 ALU.mult, ALU.add).then_inc(weighted_acc, 1)
                        add_square(norm, m)

                tiles(0, 0)
                aside()
                with dve.Fori(0, KD // 2 - 1) as i:
                    tiles(2, i)

            def up(L, ada_too):
                with dve.Fori(0, KF // 2) as i:
                    def conv(r):
                        for tap in (1, 0):
                            d = 2 - tap
                            if tap == 1:
                                dve.wait_ge(L.base, i * 4 + (r + 1))
                            else:
                                dve.wait_ge(L.tap, i * 4 + (r + 1))
                            dve.scalar_tensor_tensor(scratch[r][:, d:T], bank[r][:, 0:T - d], col(L.w, i * 12 + (3 * r + tap)),
                                                     scratch[r][:, d:T], ALU.mult, ALU.add).then_inc(L.tap if tap else L.conv, 1)

                    def gated(r):
                        dve.wait_ge(L.conv, i * 4 + (r + 1))
                        dve.wait_ge(L.silu, i * 2 + (r - 1))
                        dve.tensor_tensor(scratch[r][:, :], scratch[r][:, :], scratch[r - 2][:, :], ALU.mult).then_inc(L.gated, 1)

                    def low(r):
                        dve.wait_ge(L.hi, i * 2 + (r - 1))
                        dve.tensor_tensor(actl[:, i * 2 + (r - 2), :], scratch[r][:, :], acth[:, i * 2 + (r - 2), :].bitcast(F32), ALU.subtract).then_inc(L.lo, 1)

                    if ada_too:
                        ada_sum(i * 2 + 2)
                    conv(0)
                    conv(1)
                    if ada_too:
                        ada_sum(i * 2 + 3)
                    conv(2)
                    gated(2)
                    conv(3)
                    gated(3)
                    low(2)
                    low(3)

            def attend(a, neg_max, row_sum, col0, out, beside=None):
                for step in range(UNITS + LAG + 1):
                    if step < UNITS:
                        U, w, c = unit(a, step), P * (step % TB + 1), col0 + step
                        dve.wait_ge(att.qk, U + 1)
                        dve.tensor_reduce(neg_max[:, c:c + 1], scores_bank(a, U)[:, 0:w], AX_X, ALU.max, negate=True).then_inc(att.max, 1)
                        if beside is not None:
                            beside(step)
                    if step > LAG:
                        u = step - LAG - 1
                        U, c = unit(a, u), col0 + u
                        hd, i = u // TB, u % TB
                        dve.wait_ge(att.exp, U + 1)
                        dve.reciprocal(row_sum[:, c:c + 1], row_sum[:, c:c + 1]).then_inc(att.rinv, 1)
                        dve.wait_ge(att.pv, U + 1)
                        dve.wait_ge(att.rinv, U + 1)
                        dve.tensor_scalar(out[:, i, HD * hd:HD * hd + HD], bank[5 + U % 2][:, 0:HD], row_sum[:, c:c + 1], None, ALU.mult).then_inc(att.o, 1)

            def mix_low(e0, count, tile0, source):
                for e in range(count):
                    dve.wait_ge(mix.hi, e0 + e + 1)
                    dve.tensor_tensor(xl[:, tile0 + e, :], source(e)[:, :], xh[:, tile0 + e, :].bitcast(F32), ALU.subtract).then_inc(mix.lo, 1)

            zero(norm_mix)
            for k in range(KD):
                dve.wait_ge(norm_mix.acc, k + 1)
                dve.wait_ge(norm_mix.sq, k + 1)
                dve.tensor_tensor(ss_acc[:, :], ss_acc[:, :], scratch[k % 4][:, :], ALU.add).then_inc(norm_mix.acc, 1)
            dve.wait_ge(cols_landed, 16)
            norm_tiles(norm_mix, lambda k: col("mix_g", k))
            for t in range(TB):
                dve.wait_ge(p1.act, 3 + t)
                dve.tensor_tensor(scratch[2 + t % 2][:, :], vg[:, t, :], vg[:, t, :], ALU.mult).then_inc(gate.sq, 1)
                dve.wait_ge(gate.sq, t + 1)
                dve.tensor_reduce(vsum[:, HEADS * t:HEADS * t + HEADS], scratch[2 + t % 2][:, :].rearrange("p (g d) -> p g d", g=HEADS),
                                  AX_X, ALU.add).then_inc(gate.sum, 1)
            dve.wait_ge(p1.mm, P1["f"])
            dve.tensor_scalar(lf[1][:, :], bank[4][:, :], col("b_forget"), 0.0, ALU.add, ALU.min).then_inc(forget.dve, 1)
            dve.memset(scratch[0][:, :], 1.0).then_inc(forget.dve, 1)
            dve.wait_ge(forget.act, 3)
            dve.wait_ge(forget.dve, 2)
            dve.tensor_tensor(lf[1][:, :], lf[1][:, :], lf[0][:, :], ALU.subtract).then_inc(forget.dve, 1)
            dve.wait_ge(forget.dve, 3)
            dve.tensor_tensor_scan(dec_all[:, :], scratch[0][:, :], lf[1][:, :], 0.0, ALU.mult, ALU.add).then_inc(forget.dve, 1)
            dve.wait_ge(decay.hi, 1)
            dve.tensor_tensor(lf[0][:, :], dec_all[:, :], dec_q[:, :].bitcast(F32), ALU.subtract).then_inc(decay.dve, 1)
            dve.wait_ge(decay.dve, 1)
            dve.tensor_scalar(dec_all[0:32, :], dec_q[0:32, :].bitcast(F32), -1.0, None, ALU.mult).then_inc(decay.dve, 1)
            dve.tensor_scalar(dec_all[32:64, :], lf[0][32:64, :], -1.0, None, ALU.mult).then_inc(decay.dve, 1)
            dve.memset(dec_all[64:P, :], 1.0).then_inc(decay.dve, 1)
            dve.tensor_copy(dec_q[96:P, :], lf[0][96:P, :]).then_inc(decay.dve, 1)
            dve.wait_ge(decay.dve, 5)
            dve.tensor_scalar(dec_q[0:64, :], dec_all[0:64, :], 0.0, 1.0, ALU.mult, ALU.add).then_inc(decay.dve, 1)
            dve.wait_ge(decay.dve, 6)
            dve.wait_ge(gate.rstd, 2)
            for t in range(TB):
                groups = vg[:, t, :].rearrange("p (g d) -> p g d", g=HEADS)
                dve.tensor_tensor(groups, groups,
                                  vrs[:, HEADS * t:HEADS * t + HEADS].rearrange("p (g c) -> p g c", c=1).broadcast_to([P, HEADS, HD]),
                                  ALU.mult).then_inc(gate.done, 1)
            for t in range(TB):
                dve.wait_ge(p1.mm, P1["v"][t])
                dve.tensor_copy(v1[:, t, :], bank[t][:, :]).then_inc(p1.dve, 1)
            dve.wait_ge(small_landed, 32)
            for t in range(4):
                dve.wait_ge(mixing.mm, t + 1)
                dve.scalar_tensor_tensor(scratch[t][:, :].rearrange("p (n i) -> p n i", n=TB), MIX_BANKS[t][:, :].rearrange("p (n i) -> p n i", n=TB),
                                         col("gmlp_g", t), bsp[:, t:t + 1, :].broadcast_to([P, TB, P]), ALU.mult, ALU.add).then_inc(mixing.bias, 1)
                dve.wait_ge(mixing.bias, t + 1)
                dve.tensor_tensor(scratch[t][:, :], scratch[t][:, :], u_sb[:, t, :], ALU.mult).then_inc(mixing.done, 1)

            def keys(p):
                dve.wait_ge(p1.mm, P1["k"][p])
                dve.tensor_copy(k1[:, p, :], (bank[1] if p == 0 else NEXT_BANK)[:, :]).then_inc(p1.dve, 1)

            keys(0)

            def decay_head(hd):
                if hd < HEADS:
                    dve.tensor_scalar(dec_k[hd % 2][:, :], dec_all[:, :], col("head_row", hd), None, ALU.mult).then_inc(decay.head, 1)

            decay_head(0)
            decay_head(1)

            def beside(step):
                if step % TB == TB - 1:
                    decay_head(step // TB + 2)
                p = step // PAIR_UNITS + 1
                if p < PAIRS and step % PAIR_UNITS == PAIR_UNITS - 1:
                    keys(p)

            attend(0, neg_max1, row_sum1, 0, o1, beside)
            mix_low(0, 4, 4, lambda e: scratch[e])
            mix_low(4, 4, 0, lambda e: HT_BANKS[e])
            dve.wait_ge(csil_done, 1)
            residual_out(res_out1, norm_ffn, None, True)
            norm_tiles(norm_ffn, lambda k: col("ffn_g", k))
            up(up1, True)
            dve.wait_ge(ada_used, N_ADA)
            a = COLS["b_ada"][0]
            dve.tensor_tensor(mod[:, :, :], MOD_BANK[:, 0:6 * KD].rearrange("p (j k) -> p j k", j=6),
                              cols[:, a:a + 6 * KD].rearrange("p (j k) -> p j k", j=6), ALU.add).then_inc(mod_done, 1)
            dve.wait_ge(mod_done, 1)
            for j, g in enumerate(("attn2_g", "mlp2_g")):
                a = COLS[g][0]
                dve.scalar_tensor_tensor(modA[:, j, :], mod[:, 3 * j + 1, :], 1.0, cols[:, a:a + KD], ALU.add, ALU.mult).then_inc(mod_done, 1)
            a = COLS["final_g"][0]
            gains = cols[:, a:a + KD]
            dve.tensor_tensor(final_w[:, :], gains, gains, ALU.mult).then_inc(mod_done, 1)
            dve.wait_ge(mod_done, 4)
            dve.tensor_scalar(final_w[:, :], final_w[:, :], EPS, None, ALU.add).then_inc(mod_done, 1)
            dve.tensor_tensor(modA[:, 0, :], modA[:, 0, :], gains, ALU.mult).then_inc(mod_done, 1)
            dve.wait_ge(mod_done, 6)
            TURNS = 1.5 * 2.0 ** 23
            C1, C2 = 6.28125, 507.0 / 2 ** 18
            C3 = float(2 * np.pi - C1 - C2)
            dve.wait_ge(pos_landed, 16)
            steps = [
                lambda: dve.tensor_copy(ang, pos_i),
                lambda: dve.tensor_scalar(ang, ang, col("inv_freq"), None, ALU.mult),
                lambda: dve.tensor_scalar(turn, ang, float(0.5 / np.pi), TURNS, ALU.mult, ALU.add),
                lambda: dve.tensor_scalar(turn, turn, -TURNS, None, ALU.add),
                lambda: dve.scalar_tensor_tensor(ang, turn, -C1, ang, ALU.mult, ALU.add),
                lambda: dve.scalar_tensor_tensor(ang, turn, -C2, ang, ALU.mult, ALU.add),
                lambda: dve.scalar_tensor_tensor(ang, turn, -C3, ang, ALU.mult, ALU.add),
                lambda: dve.tensor_scalar(ang, ang, 3.1415925, -3.1415925, ALU.min, ALU.max),
            ]
            for n, step in enumerate(steps):
                step().then_inc(trig.dve, 1)
                dve.wait_ge(trig.dve, n + 1)
            dve.memset(q_trig[0:64, :], 1.0).then_inc(trig.dve, 1)

            def trig_rows():
                dve.wait_ge(trig.act, 5)
                dve.wait_ge(trig.dve, 9)
                dve.tensor_scalar(q_trig, q_trig, col("mq_g"), col("q_sign"), ALU.mult, ALU.mult).then_inc(trig.row, 1)
                dve.tensor_scalar(k_trig, k_trig, col("mkr_g"), col("k_sign"), ALU.mult, ALU.mult).then_inc(trig.row, 1)

            residual_down_final(res_down1, norm_final, scratch[3], trig_rows)

            norm_tiles(norm_attn2, lambda k: modA[:, 0, k:k + 1], lambda k: mod[:, 0, k:k + 1])
            dve.wait_ge(trig.row, 2)
            dve.wait_ge(rope.sq, 2)
            dve.tensor_tensor(k_rope[64:P, :], bank[1][64:P, :], k_trig[64:P, :], ALU.mult).then_inc(rope.dve, 1)
            dve.tensor_tensor(turn[64:P, :], bank[1][0:64, :], k_trig[0:64, :], ALU.mult).then_inc(rope.dve, 1)
            dve.wait_ge(rope.dve, 2)
            dve.tensor_tensor(k_rope[64:P, :], k_rope[64:P, :], turn[64:P, :], ALU.add).then_inc(rope.dve, 1)

            def head_rstd(job):
                dve.wait_ge(head.rstd, job + 1)
                return scratch[job % 4]

            r = head_rstd(JOB_KV)
            dve.scalar_tensor_tensor(r[:, :], bank[0][:, :], col("kvl_g"), r[:, :], ALU.mult, ALU.mult).then_inc(head.pre, 1)
            r = head_rstd(JOB_QL)
            for t in range(2):
                dve.scalar_tensor_tensor(scratch[2 + t][:, :], bank[2 + t][:, :], col("ql_g", t), r[:, :], ALU.mult, ALU.mult).then_inc(head.pre, 1)
            dve.wait_ge(lat.hi, 1)
            dve.tensor_tensor(kvl[:, :], scratch[0][:, :], kvh[:, :].bitcast(F32), ALU.subtract).then_inc(lat.lo, 1)
            for t in range(2):
                dve.wait_ge(lat.hi, 2 + t)
                dve.tensor_tensor(qll[:, t, :], scratch[2 + t][:, :], qlh[:, t, :].bitcast(F32), ALU.subtract).then_inc(lat.lo, 1)
            dve.wait_ge(norm_final.rstd, 2)
            for k in range(KD):
                dve.scalar_tensor_tensor(h[:, k, :], h[:, k, :], col("final_g", k), ss_acc[:, :], ALU.mult, ALU.mult).then_inc(norm_final.tmp, 1)
            for n, t in enumerate(CV_ORDER):
                dve.wait_ge(p2.mm, P2["v"][n])
                dve.tensor_copy(v2[:, t, :], bank[4 + t][:, :]).then_inc(p2.dve, 1)
            for p in range(PAIRS):
                for which, (out, g) in enumerate(((cq, "cq_g"), (ck, "ck_g"))):
                    r = head_rstd(job_c(p, which))
                    dve.scalar_tensor_tensor(out[:, p, :], bank[c_bank(p) + which][:, :], col(g), r[:, :], ALU.mult, ALU.mult).then_inc(head.done, 1)
            attend(1, neg_max2, row_sum2, 0, o2)
            mix_low(8, 4, 4, lambda e: HT_BANKS[e])
            for t in range(TB):
                dve.wait_ge(p2.mm, P2["mv"][t])
                dve.tensor_copy(v2[:, t, :], bank[4 + t % 2][:, :]).then_inc(p2.dve, 1)
            for hd in range(HEADS):
                tile = bank[m_bank(hd)]
                r = head_rstd(job_m(hd, 0))
                dve.tensor_tensor(mq[:, hd, :], tile[:, :], q_trig, ALU.mult).then_inc(head.pre, 1)
                dve.wait_ge(head.pre, 4 + 2 * hd)
                dve.tensor_tensor(mq[:, hd, :], mq[:, hd, :], r[:, :], ALU.mult).then_inc(head.done, 1)
                tile = bank[m_bank(hd) + 1]
                r = head_rstd(job_m(hd, 1))
                dve.scalar_tensor_tensor(mk[0:64, hd, :], tile[0:64, :], col_at("mk_g", 0, 64), r[0:64, :], ALU.mult, ALU.mult).then_inc(head.pre, 1)
                dve.tensor_tensor(mk[64:P, hd, :], k_rope[64:P, :], r[64:P, :], ALU.mult).then_inc(head.done, 1)
            attend(2, neg_max2, row_sum2, UNITS, o2)
            dve.wait_ge(norm_final.tmp, KD)
            mix_low(12, 4, 0, lambda e: HT_BANKS[e])
            residual_out(res_out2, norm_mlp2, 2, False)
            norm_tiles(norm_mlp2, lambda k: modA[:, 1, k:k + 1], lambda k: mod[:, 3, k:k + 1])
            up(up2, False)
            residual_down(res_down2, 5)

        @block.tensor
        def _(pe):
            def split_product(out, lhs, rhs, first, last):
                for n, (a, b) in enumerate(((0, 0), (0, 1), (1, 0))):
                    ins = pe.matmul(out, lhs[a], rhs[b], start=first and n == 0, stop=last and n == 2)
                return ins

            def weights(slot, a, b):
                return wh[slot][:, a:b], wl[slot][:, a:b]

            def inputs(k, a=0, b=T):
                return xh[:, k, a:b], xl[:, k, a:b]

            def features_tile(out, slot, half):
                for k in range(KD):
                    a = PAIR_COLS * k + P * half
                    ins = split_product(out[:, :], weights(slot, a, a + P), inputs(k), k == 0, k == KD - 1)
                return ins

            def features_pair(banks, slot, mm, order, ready):
                for n, k in enumerate(order):
                    ready(k)
                    for half in range(2):
                        a = PAIR_COLS * k + P * half
                        ins = split_product(banks[half][:, :], weights(slot, a, a + P), inputs(k), n == 0, n == KD - 1)
                        if n == KD - 1:
                            ins.then_inc(mm, 1)

            def tokens_tiles(banks, order, slots, n0, mm, ready=None):
                for c in range(2):
                    pe.wait_ge(lo_done, n0 + c + 1)
                    for t in order:
                        if c == 0 and ready is not None:
                            ready(t)
                        for kk in range(4):
                            k = 4 * c + kk
                            ins = split_product(banks[t][:, :], inputs(k, P * t, P * t + P), weights(slots[c], 512 * kk, 512 * kk + 512),
                                                k == 0, k == KD - 1)
                        if c == 1 or t == order[-1]:
                            ins.then_inc(mm, 1)

            def norm_sum(norm):
                pe.wait_ge(norm.acc, KD + 1)
                pe.matmul(SS_BANK[:, :], ones[:, :], ss_acc[:, :], start=True, stop=True).then_inc(norm.ss, 1)

            def attend(a, scores, v, prob, probT, ident, beside=None):
                for step in range(UNITS + LAG + 1):
                    if step < UNITS:
                        U, hd, i = unit(a, step), step // TB, step % TB
                        n = len(S_BANKS[a])
                        if U >= n:
                            pe.wait_ge(att.exp, U - n + 1)
                        scores(hd, i, scores_bank(a, U), P * (i + 1)).then_inc(att.qk, 1)
                    if LAG <= step < UNITS + LAG:
                        U, i = unit(a, step - LAG), (step - LAG) % TB
                        pe.wait_ge(att.exp, U + 1)
                        if U >= 2:
                            pe.wait_ge(att.ptc, U - 1)
                        for j in range(i + 1):
                            ins = pe.transpose(bank[3 + U % 2][:, P * j:P * j + P], prob[U % 4][:, P * j:P * j + P], ident[:, :])
                        ins.then_inc(att.pt, 1)
                    if step > LAG:
                        u = step - LAG - 1
                        U, hd, i = unit(a, u), u // TB, u % TB
                        pe.wait_ge(att.ptc, U + 1)
                        if U >= 2:
                            pe.wait_ge(att.o, U - 1)
                        for j in range(i + 1):
                            ins = pe.matmul(bank[5 + U % 2][:, 0:HD], probT[U % 2][:, P * j:P * j + P], v[:, j, HD * hd:HD * hd + HD],
                                            start=j == 0, stop=j == i)
                        ins.then_inc(att.pv, 1)
                    if beside is not None:
                        beside(step)

            def transpose_heads(a, out, ident):
                pe.wait_ge(att.o, unit(a, UNITS))
                for e in range(4):
                    for t in range(TB):
                        ins = pe.transpose(HT_BANKS[e][:, P * t:P * t + P], out[:, t, P * e:P * e + P], ident[:, :])
                    ins.then_inc(mix.mm, 1)

            def ada_columns(a):
                pe.wait_ge(ada_red, a + 1)
                for j in range(2):
                    ins = pe.matmul(MOD_BANK[:, bass.ds(a * 2 + j, 1)], ada_acc[:, P * j:P * j + P], ones[:, 0:1], start=True, stop=True)
                ins.then_inc(ada_used, 1)

            def residual_out(res, base, parts, ada_too):
                order = [4, 5, 6, 7, 0, 1, 2, 3]

                def ready(k):
                    pe.wait_ge(mix.lo, parts if k >= 4 else parts + k + 1)

                for m in range(KD):
                    n = base + m // 2
                    if m % 2 == 0:
                        pe.wait_ge(lo_done, n + 1)
                    if m >= 4:
                        pe.wait_ge(res.h, m - 3)
                    if m == 0:
                        features_pair(OUT_BANKS[0:2], n % 2, res.mm, order, ready)
                    elif m >= 2:
                        features_tile(OUT_BANKS[m % 4], n % 2, m % 2).then_inc(res.mm, 1)
                    if ada_too and m % 4 == 1:
                        ada_columns(m // 4)

            def residual_down(L, res, base, ada_too):
                def two_tiles(i, first=False):
                    m0, c0 = (0, base) if first else (2, base + 4)
                    for r in range(2):
                        for e in range(2):
                            slot = (base + e) % 2
                            pe.wait_ge(lo_done, i * 4 + (c0 + 2 * r + e + 1))
                            if e == 0 and not first:
                                pe.wait_ge(res.h, i * 2 + (m0 + r - 1))
                            for kk in range(KF // 2):
                                k = KF // 2 * e + kk
                                if first and r == 0:
                                    pe.wait_ge(L.lo, k + 1)
                                ins = split_product(bank[4 + r][:, :], weights(slot, P * kk, P * kk + P), (acth[:, k, :], actl[:, k, :]),
                                                    k == 0, k == KF - 1)
                            ins.then_inc(res.mm, 1)
                            if ada_too and first and r == 0 and e == 0:
                                ada_columns(N_ADA - 1)

                two_tiles(0, True)
                with pe.Fori(0, KD // 2 - 1) as i:
                    two_tiles(i)

            def up(L, norm, base, ada_too):
                def chunks(count, i, first=False):
                    c0 = 0 if first else 2
                    for c in range(count):
                        pe.wait_ge(lo_done, i * count + (base + c0 + c + 1))
                        for half in range(2):
                            r = 2 * (c % 2) + half
                            m = c0 // 2 + c // 2
                            if not first:
                                pe.wait_ge(L.conv, i * (2 * count) + (4 * m + r - 3))
                            if first and c == 0:
                                if half == 0:
                                    features_pair(bank[0:2], base % 2, L.mm, range(KD), lambda k: pe.wait_ge(norm.lo, k + 1))
                            else:
                                features_tile(bank[r], (base + c) % 2, half).then_inc(L.mm, 1)
                            if ada_too and half == 0 and not (first and c == 0):
                                ada_columns(i * count + (1 + c0 + c))

                chunks(2, 0, True)
                with pe.Fori(0, (KF - 2) // 4) as i:
                    chunks(4, i)

            pe.wait_ge(setup1, 1)
            norm_sum(norm_mix)
            pe.wait_ge(lo_done, BASE1["ua"] + 1)
            features_pair(bank[4:6], BASE1["ua"] % 2, p1.mm, range(KD), lambda k: pe.wait_ge(norm_mix.lo, k + 1))
            n = BASE1["vg"]
            tokens_tiles(bank[0:4], range(TB), (n % 2, (n + 1) % 2), n, p1.mm)
            n = BASE1["ub"]
            pe.wait_ge(lo_done, n + 1)
            for half in range(2):
                features_tile(bank[6 + half], n % 2, half).then_inc(p1.mm, 1)
            n = BASE1["f"]
            pe.wait_ge(lo_done, n + 1)
            pe.wait_ge(p1.act, 1)
            features_tile(bank[4], n % 2, 0).then_inc(p1.mm, 1)
            n = BASE1["v"]
            tokens_tiles(bank[0:4], range(TB), (n % 2, (n + 1) % 2), n, p1.mm,
                         lambda t: pe.wait_ge(p1.act, 3 + t))
            pe.wait_ge(setup1, 12)
            pe.wait_ge(gate.done, TB)
            pe.wait_ge(forget.act, 1)
            pe.wait_ge(forget.dve, 1)
            pe.wait_ge(p1.act, 8)
            for t in range(4):
                for c in range(TB):
                    for g in (2 * t, 2 * t + 1):
                        a = HD * (g % 2)
                        ins = pe.matmul(MIX_BANKS[t][a:a + HD, P * c:P * c + P], vg[:, c, HD * g:HD * g + HD], wsT[:, g, :], start=True, stop=True)
                ins.then_inc(mixing.mm, 1)
            n = BASE1["qk"]
            pe.wait_ge(lo_done, n + 1)
            for half in range(2):
                pe.wait_ge(p1.dve, half + 1)
                features_tile(bank[half], n % 2, half).then_inc(p1.mm, 1)

            def next_pair(step):
                p, x = step // PAIR_UNITS + 1, step % PAIR_UNITS
                half = 0 if x < Q_STEPS else 1
                share = (2, 3)[half]
                first = (x - half * Q_STEPS) * share
                if p >= PAIRS or first >= KD:
                    return
                n = BASE1["qk"] + p
                if x == 0:
                    pe.wait_ge(lo_done, n + 1)
                    if p == 1:
                        pe.wait_ge(mixing.done, 2)
                    else:
                        pe.wait_ge(p1.dve, TB + p)
                elif x == Q_STEPS:
                    pe.wait_ge(p1.act, 9 + p)
                for k in range(first, min(first + share, KD)):
                    a = PAIR_COLS * k + P * half
                    ins = split_product(NEXT_BANK[:, :], weights(n % 2, a, a + P), inputs(k), k == 0, k == KD - 1)
                    if k == KD - 1:
                        ins.then_inc(p1.mm, 1)

            def rows(hd):
                return slice(HD * (hd % 2), HD * (hd % 2) + HD)

            def forgetting(hd, i, out, w):
                r = rows(hd)
                if hd % 2 == 0 and i == 0:
                    pe.wait_ge(p1.act, 9 + hd // 2)
                    pe.wait_ge(p1.dve, TB + 1 + hd // 2)
                pe.matmul(out[:, 0:w], q1[r, hd // 2, P * i:P * i + P], k1[r, hd // 2, 0:w], start=True, stop=False)
                pe.wait_ge(decay.head, hd + 1)
                pe.matmul(out[:, 0:w], dec_q[:, P * i:P * i + P], dec_k[hd % 2][:, 0:w], start=False, stop=False)
                return pe.matmul(out[:, w - P:w], ident_b1[:, :], causal_b[:, :], start=False, stop=True)

            pe.wait_ge(mixing.done, 4)
            attend(0, forgetting, v1, prob1, probT1, ident1, next_pair)
            transpose_heads(0, o1, ident1)
            residual_out(res_out1, BASE1["out"], 4, True)
            norm_sum(norm_ffn)
            up(up1, norm_ffn, BASE1["up"], True)
            residual_down(up1, res_down1, BASE1["down"], True)
            pe.wait_ge(weighted_acc, KD + 1)
            pe.matmul(bank[0][:, :], ones[:, :], scratch[3][:, :], start=True, stop=True)
            norm_sum(norm_final)

            base = N1 + N_DOWN
            pe.wait_ge(setup2, 14)

            def head_sum(job, out, ones_of, squares):
                pe.wait_ge(head.sq, N_SQ[job])
                for n, sq in enumerate(squares):
                    ins = pe.matmul(out[:, :], ones_of[:, :], sq[:, :], start=n == 0, stop=n == len(squares) - 1)
                ins.then_inc(head.ss, 1)

            pe.wait_ge(lo_done, base + 1)
            features_pair(bank[0:2], base % 2, p2.mm, range(KD), lambda k: pe.wait_ge(norm_attn2.lo, k + 1))
            pe.wait_ge(lo_done, base + 2)
            for half in range(2):
                features_tile(bank[2 + half], (base + 1) % 2, half).then_inc(p2.mm, 1)
            head_sum(JOB_KV, bank[4], ones, [sq2[0]])
            head_sum(JOB_QL, bank[5], ones, [sq2[1], scratch[3]])

            def sums_taken(t):
                if t < 2:
                    pe.wait_ge(head.root, t + 1)
                elif t == 2:
                    pe.wait_ge(norm_final.rstd, 1)

            n = BASE2["cv"]
            tokens_tiles(bank[4:8], CV_ORDER, (n % 2, (n + 1) % 2), n, p2.mm, sums_taken)
            for p in range(PAIRS + 1):
                if p < PAIRS:
                    n = BASE2["cqk"] + p
                    pe.wait_ge(lo_done, n + 1)
                    for which in range(2):
                        if p < 2:
                            pe.wait_ge(lat.lo, 3)
                            pe.wait_ge(rope.dve, 2)
                        elif p == 3:
                            pe.wait_ge(head.done, 2 + which + 1)
                        features_tile(bank[c_bank(p) + which], n % 2, which).then_inc(p2.mm, 1)
                if p:
                    for which in range(2):
                        if p == 1:
                            pe.wait_ge(p2.dve, TB)
                        else:
                            pe.wait_ge(head.root, job_c(p - 2, which) + 1)
                        head_sum(job_c(p - 1, which), bank[6 + which], ones64, [sq2[which]])

            def chunked(hd, i, out, w):
                r = rows(hd)
                if hd == 0 and i == 0:
                    pe.wait_ge(head.done, 2)
                if hd == 0 and i == 2:
                    pe.wait_ge(head.done, 2 * PAIRS)
                pe.matmul(out[:, 0:w], cq[r, hd // 2, P * i:P * i + P], ck[r, hd // 2, 0:w], start=True, stop=False)
                if i == 0:
                    pe.wait_ge(rel_low, hd + 1)
                for part in (rel_h, rel_l):
                    pe.matmul(out[:, 0:w], flip_r[:, :], part[hd % 2][:, T - w:T], start=False, stop=False)
                return pe.matmul(out[:, w - P:w], ident_b2[:, :], chunk_b[:, :], start=False, stop=True)

            attend(1, chunked, v2, prob2, probT2, ident2)
            transpose_heads(1, o2, ident2)
            n = BASE2["mkv"]
            pe.wait_ge(lo_done, n + 1)
            for t in range(TB):
                if t < 2:
                    pe.wait_ge(att.o, unit(2, 0))
                else:
                    pe.wait_ge(p2.dve, TB + t - 1)
                split_product(bank[4 + t % 2][:, :], (kvh[:, P * t:P * t + P], kvl[:, P * t:P * t + P]), weights(n % 2, 1024, 1536),
                              True, True).then_inc(p2.mm, 1)
            nq = BASE2["mq"]
            for hd in range(HEADS + 1):
                if hd < HEADS:
                    if hd < 2:
                        pe.wait_ge(mix.lo, 11 + hd)
                    if hd == 2:
                        pe.wait_ge(p2.dve, 2 * TB)
                    if hd >= 3:
                        pe.wait_ge(head.done, 2 * PAIRS + 2 * (hd - 2))
                    for k in range(2):
                        a = 1024 * k + P * hd
                        ins = split_product(bank[m_bank(hd)][:, :], weights(nq % 2, a, a + P), (qlh[:, k, :], qll[:, k, :]), k == 0, k == 1)
                    ins.then_inc(p2.mm, 1)
                    split_product(bank[m_bank(hd) + 1][:, :], weights(n % 2, P * hd, P * hd + P), (kvh[:, :], kvl[:, :]), True, True).then_inc(p2.mm, 1)
                if hd:
                    for which in range(2):
                        x = job_m(hd - 1, which)
                        if hd >= 2:
                            pe.wait_ge(head.root, x - 1)
                        head_sum(x, bank[6 + which], ones96, [(sq2, sqk)[which][(hd - 1) % 2]])

            def latent(hd, i, out, w):
                pe.matmul(out[:, 0:w], mq[:, hd, P * i:P * i + P], mk[:, hd, 0:w], start=True, stop=False)
                return pe.matmul(out[:, w - P:w], ident_b2[:, :], chunk_b[:, :], start=False, stop=True)

            pe.wait_ge(head.done, 2 * PAIRS + 2 * HEADS)
            attend(2, latent, v2, prob2, probT2, ident2)
            transpose_heads(2, o2, ident2)
            residual_out(res_out2, BASE2["out"], 12, False)
            norm_sum(norm_mlp2)
            up(up2, norm_mlp2, BASE2["up"], False)
            residual_down(up2, res_down2, BASE2["down"], False)


def pair_chunks(w):
    n = w.shape[1] // PAIR_COLS
    return w.reshape(KD, P, n, PAIR_COLS).transpose(2, 1, 0, 3).reshape(n * P, CHUNK)


def wide_chunks(w):
    return w.reshape(2, 4, P, 512).transpose(0, 2, 1, 3).reshape(2 * P, CHUNK)


def down_chunks(w):
    return w.reshape(2, KF // 2, P, KD, P).transpose(3, 0, 2, 1, 4).reshape(N_DOWN * P, DOWN_CHUNK)


def up_chunks(w, gate, value):
    g, v = pair_chunks(w[:, gate * FF:(gate + 1) * FF]), pair_chunks(w[:, value * FF:(value + 1) * FF])
    return np.stack([g.reshape(-1, P, CHUNK), v.reshape(-1, P, CHUNK)], 1).reshape(-1, CHUNK)


def pad_columns(w, n):
    return np.concatenate([w, np.zeros((w.shape[0], n - w.shape[1]), w.dtype)], 1)


def up_columns(a, gate, value):
    t = a.reshape(a.shape[0], 2, KF // 2, 2, P)
    return np.stack([t[:, gate], t[:, value]], 2).reshape(a.shape[0], UP_TILES, P)


def kernel(**inputs):
    import concourse.bacc as bacc
    from concourse.bass_utils import run_bass_kernel_spmd

    f = {k: np.asarray(v) for k, v in inputs.items()}
    f32 = np.float32

    w = f["w_in"][0]
    wf = np.zeros((D, 2 * P), f32)
    for quadrant in range(4):
        wf[:, 32 * quadrant:32 * quadrant + HEADS] = w[:, 2560:2568]
    qk = np.concatenate([np.concatenate([w[:, P * p:P * p + P], w[:, 512 + P * p:512 + P * p + P]], 1) for p in range(PAIRS)], 1)
    stream1 = np.concatenate([
        pair_chunks(w[:, 1536:1792]), wide_chunks(w[:, 2048:2560]), pair_chunks(w[:, 1792:2048]), pair_chunks(wf), wide_chunks(w[:, 1024:1536]), pair_chunks(qk),
        pair_chunks(f["w_out"][0]), up_chunks(f["w_up"][0], 1, 0)])
    w = f["w_in_2"][0]
    x, xs = w[:, 384:416], np.concatenate([w[:, 400:416], w[:, 384:400]], 1)
    kvr = np.concatenate([w[:, 256:384], x, x, xs, xs], 1)
    ca = w[:, 416:]
    cqk = np.concatenate([np.concatenate([ca[:, P * p:P * p + P], ca[:, 512 + P * p:512 + P * p + P]], 1) for p in range(PAIRS)], 1)
    wq = f["w_q_up_2"][0].reshape(2 * P, HEADS, MLA_QK)
    wq = np.concatenate([wq, wq[:, :, 80:96], wq[:, :, 64:80]], 2).reshape(2, P, HEADS * P)
    wkv = f["w_kv_up_2"][0].reshape(P, HEADS, P)
    wk = np.concatenate([wkv[:, :, :HD], np.zeros((P, HEADS, HD), f32)], 2).reshape(P, HEADS * P)
    mkv = pad_columns(np.concatenate([wk, wkv[:, :, HD:].reshape(P, 512)], 1), CHUNK)
    stream2 = np.concatenate([
        pair_chunks(kvr), pair_chunks(w[:, :256]), wide_chunks(ca[:, 1024:]), pair_chunks(cqk),
        wq.transpose(1, 0, 2).reshape(P, CHUNK), mkv, pair_chunks(f["w_out_2"][0]), up_chunks(f["w_up_2"][0], 0, 1)])

    parts = {}

    def features(name, a):
        parts[name] = a.reshape(-1, P).T

    features("mix_g", f["norm_mix_g"][0])
    features("ffn_g", f["norm_ffn_g"][0])
    features("final_g", f["norm_final_g"])
    features("attn2_g", f["g_attn_norm_2"][0])
    features("mlp2_g", f["g_mlp_norm_2"][0])
    features("gmlp_g", f["gmlp_norm_g"][0])
    parts["conv_w"] = up_columns(f["conv_w"][0], 1, 0).transpose(2, 1, 0).reshape(P, -1)
    parts["conv_b"] = up_columns(f["conv_b"], 1, 0)[0].T
    parts["conv_w2"] = up_columns(f["conv_w_2"][0], 0, 1).transpose(2, 1, 0).reshape(P, -1)
    parts["conv_b2"] = up_columns(f["conv_b_2"], 0, 1)[0].T
    features("b_ada", f["b_ada_2"][0])
    features("c", f["c_2"][0])
    features("ql_g", f["g_q_latent_2"][0])
    features("kvl_g", f["g_kv_latent_2"][0])
    g = f["g_mla_q_2"][0]
    features("mq_g", np.concatenate([g, g[80:96], g[64:80]]))
    g = f["g_mla_k_2"][0]
    features("mk_g", np.concatenate([g[:64], g[:64]]))
    swapped = np.concatenate([g[80:96], g[64:80]])
    features("mkr_g", np.concatenate([g[64:96], g[64:96], swapped, swapped]))
    features("cq_g", np.tile(f["g_ca_q_2"][0], 2))
    features("ck_g", np.tile(f["g_ca_k_2"][0], 2))
    b_forget = np.zeros(P, f32)
    for quadrant in range(4):
        b_forget[32 * quadrant:32 * quadrant + HEADS] = f["b_forget"][0]
    features("b_forget", b_forget)
    parts["head_row"] = (np.arange(P)[:, None] % 32 == np.arange(HEADS)[None, :]).astype(f32)
    half = ROPE // 2
    inv = np.power(f32(ROPE_THETA), -np.arange(half, dtype=f32) / f32(half)).astype(f32)
    features("inv_freq", np.tile(inv, P // half))
    sign = np.concatenate([-np.ones(half, f32), np.ones(half, f32)])
    scale = f32(MLA_QK ** -0.5)
    features("q_sign", np.concatenate([np.ones(96, f32), sign]) * scale)
    features("k_sign", np.concatenate([np.ones(64, f32), sign, sign]))
    packed = np.concatenate([parts[name].astype(f32) for name in COLS], 1)

    distance = np.clip(T - 1 - np.arange(REL_LEN), -REL_CLIP, REL_CLIP)
    arrays = {
        "xT": f["x"][0].T,
        "cols_in": packed,
        "stream1": stream1,
        "down1": down_chunks(f["w_down"][0]),
        "stream2": stream2,
        "down2": down_chunks(f["w_down_2"][0]),
        "ada": pair_chunks(f["w_ada_2"][0]),
        "w_spatial_T": f["w_spatial"][0].transpose(2, 0, 1).reshape(P, HEADS * P),
        "b_spatial_rows": np.repeat(f["b_spatial"][0].reshape(4, 2, 1, P), HD, axis=2).transpose(1, 2, 0, 3).reshape(P, 4 * P),
        "positions": f["positions_2"].reshape(1, T).astype(np.int32),
        "rel_rows": f["rel_bias_2"][0][:, distance + REL_CLIP],
    }
    nc = bacc.Bacc("TRN2", target_bir_lowering=False, num_devices=1)
    args = {}
    for name, a in arrays.items():
        a = arrays[name] = np.ascontiguousarray(a)
        args[name] = nc.dram_tensor(name, a.shape, mybir.dt.from_np(a.dtype), kind="ExternalInput").ap()
    outT = nc.dram_tensor("outT", (D, T), F32, kind="ExternalOutput").ap()
    build(nc, **args, outT=outT)
    r = run_bass_kernel_spmd(nc, [arrays], core_ids=[0])
    return np.ascontiguousarray(r.results[0]["outT"].T).reshape(1, T, D)
```

```python
from contextlib import ExitStack

import numpy as np

import concourse.bass as bass
from concourse import mybir

ALU = mybir.AluOpType
ACT = mybir.ActivationFunctionType
F32 = mybir.dt.float32
F32R = mybir.dt.float32r
BF16 = mybir.dt.bfloat16
I32 = mybir.dt.int32
AX_X = mybir.AxisListType.X

P = 128
D = 1024
T = 512
KD = D // P
TB = T // P
HEADS = 8
HD = 64
PAIRS = HEADS // 2
FF = 2816
KF = FF // P
UP_TILES = 2 * KF
EPS = 1e-6
MLA_QK = 96
ROPE = 32
ROPE_THETA = 10000.0
REL_CLIP = 128
REL_LEN = T + P

CHUNK = 2048
DOWN_CHUNK = KF // 2 * P
PAIR_COLS = CHUNK // KD
ADA_COLS = 6 * D
ADA_TILES = 2
N_ADA = ADA_COLS // (ADA_TILES * P)
ADA_EARLY = 3
MASKED = -1e30
H = T // 2

STREAM1 = [("ua", 1), ("vg", 2), ("ub", 1), ("f", 1), ("v", 2), ("qk", PAIRS), ("out", KD // 2), ("up", KF)]
STREAM2 = [("kvr", 1), ("ql", 1), ("cqk", PAIRS), ("cv", 2), ("mq", 1), ("mkv", 1), ("out", KD // 2), ("up", KF)]
N1 = sum(n for _, n in STREAM1)
N2 = sum(n for _, n in STREAM2)
N_DOWN = 2 * KD
BASE1 = {}
BASE2 = {}
at = 0
for name, count in STREAM1:
    BASE1[name] = at
    at += count
BASE1["down"] = at
at += N_DOWN
for name, count in STREAM2:
    BASE2[name] = at
    at += count
BASE2["down"] = at
N_CHUNKS = at + N_DOWN

COLS = {}
n_cols = 0
for name, count in [
    ("mix_g", KD), ("ffn_g", KD), ("final_g", KD), ("attn2_g", KD), ("mlp2_g", KD), ("gmlp_g", 4),
    ("conv_w", 3 * UP_TILES), ("conv_b", UP_TILES), ("conv_w2", 3 * UP_TILES), ("conv_b2", UP_TILES),
    ("b_ada", N_ADA * ADA_TILES), ("ql_g", 2), ("kvl_g", 1), ("mq_g", 1), ("mk_g", 1), ("mkr_g", 1),
    ("cq_g", 1), ("ck_g", 1), ("b_forget", 1), ("head_row", HEADS), ("inv_freq", 1), ("q_sign", 1), ("k_sign", 1),
]:
    COLS[name] = (n_cols, count)
    n_cols += count


def build(nc, xT, cols_in, stream1, down1, stream2, down2, ada, c_row, w_spatial_T, b_spatial_rows, positions, rel_rows, outT):
    ctx = ExitStack()
    with ctx:
        def sem(name):
            return ctx.enter_context(nc.semaphore(name))

        def sb(name, shape, dt=F32, scope=ctx):
            return scope.enter_context(nc.sbuf_tensor(name, shape, dt))

        bank = [ctx.enter_context(nc.psum_tensor(f"bank{b}", [P, 512], F32)) for b in range(8)]
        SS_BANKS = bank[2:4]
        SS_FINAL = bank[6]

        def half(j):
            return slice(H * j, H * j + H)

        h = sb("h", [P, KD, T])
        xh = sb("xh", [P, KD, T], F32R)
        xl = sb("xl", [P, KD, T], F32R)
        raw = [sb(f"raw{s}", [P, CHUNK]) for s in range(2)]
        wh = [sb(f"wh{s}", [P, CHUNK], F32R) for s in range(2)]
        wl = [sb(f"wl{s}", [P, CHUNK], F32R) for s in range(2)]
        ada_raw = sb("ada_raw", [P, ADA_TILES, D])
        scratch = [sb(f"scratch{s}", [P, T]) for s in range(4)]
        ss_acc = sb("ss_acc", [P, T])
        ss_final = sb("ss_final", [P, T])
        trig_room = ada_raw[:, :, :].rearrange("p k c -> p (k c)")
        q_trig, k_trig, ang, turn = [trig_room[:, T * b:T * b + T] for b in range(4)]
        pos_i = turn.bitcast(I32)
        cols = sb("cols", [P, n_cols])
        mod_sum = sb("mod_sum", [P, N_ADA * ADA_TILES])
        mod = sb("mod", [P, 6, KD])
        modA = sb("modA", [P, 2, KD])
        ones = sb("ones", [P, P])
        eps_c = sb("eps_c", [P, 1])
        halfpi_c = sb("halfpi_c", [P, 1])
        eps64_c = sb("eps64_c", [P, 1])
        eps2_c = sb("eps2_c", [P, 1])
        final_w = sb("final_w", [P, KD])

        def col(name, j=0):
            return cols[:, bass.ds(COLS[name][0] + j, 1)]

        def col_at(name, a, b):
            c = COLS[name][0]
            return cols[a:b, c:c + 1]

        with ExitStack() as s:
            acth = sb("acth", [P, KF, T], F32R, s)
            actl = sb("actl", [P, KF, T], F32R, s)

        with ExitStack() as s:
            v1 = sb("v1", [P, TB, 512], F32, s)
            u_sb = sb("u_sb", [P, 4, T], F32, s)
            q1 = sb("q1", [P, PAIRS, T], F32, s)
            k1 = sb("k1", [P, PAIRS, T], F32, s)
            dec_q = sb("dec_q", [P, T], F32R, s)
            dec_all = sb("dec_all", [P, T], F32, s)
            dec_k = [sb(f"dec_k{b}", [P, T], F32R, s) for b in range(2)]
            lf = [sb(f"lf{b}", [P, T], F32, s) for b in range(2)]
            prob1 = [sb(f"prob1{b}", [P, T], F32, s) for b in range(4)]
            probT1 = [sb(f"probT1{b}", [P, T], F32, s) for b in range(2)]
            oh = sb("oh", [P, PAIRS, T], F32R, s)
            csil = sb("csil", [P, D], F32, s)
            wsT = sb("wsT", [P, HEADS, P], F32, s)
            bsp = sb("bsp", [P, 4, P], F32, s)
            vsum = sb("vsum", [P, TB * HEADS], F32, s)
            vrs = sb("vrs", [P, TB * HEADS], F32, s)
            neg_max1 = sb("neg_max1", [P, 32], F32, s)
            row_sum1 = sb("row_sum1", [P, 32], F32, s)
            ident1 = sb("ident1", [P, P], F32, s)
            ident_b1 = sb("ident_b1", [P, P], BF16, s)
            causal_b = sb("causal_b", [P, P], BF16, s)
            with ExitStack() as s2:
                vg = sb("vg", [P, TB, 512], F32, s2)
            with ExitStack() as s2:
                ol = sb("ol", [P, PAIRS, T], F32R, s2)

        with ExitStack() as s:
            qlh = sb("qlh", [P, 2, T], F32R, s)
            qll = sb("qll", [P, 2, T], F32R, s)
            kvh = sb("kvh", [P, T], F32R, s)
            kvl = sb("kvl", [P, T], F32R, s)
            k_rope = sb("k_rope", [P, T], F32, s)
            v2 = sb("v2", [P, TB, 512], F32, s)
            prob2 = [sb(f"prob2{b}", [P, T], F32, s) for b in range(4)]
            probT2 = [sb(f"probT2{b}", [P, T], F32, s) for b in range(2)]
            neg_max2 = sb("neg_max2", [P, 64], F32, s)
            row_sum2 = sb("row_sum2", [P, 64], F32, s)
            ident2 = sb("ident2", [P, P], F32, s)
            ident_b2 = sb("ident_b2", [P, P], BF16, s)
            flip = sb("flip", [P, P], F32, s)
            flip_r = sb("flip_r", [P, P], F32R, s)
            ones96 = sb("ones96", [P, P], F32, s)
            ones64 = sb("ones64", [P, P], F32, s)
            chunk_b = sb("chunk_b", [P, P], BF16, s)
            sq2 = [sb(f"sq2{b}", [P, T], F32, s) for b in range(2)]
            sqk = [sb(f"sqk{b}", [P, T], F32, s) for b in range(2)]
            with ExitStack() as s2:
                cq = sb("cq", [P, PAIRS, T], F32, s2)
                ck = sb("ck", [P, PAIRS, T], F32, s2)
                rel = [sb(f"rel{b}", [P, T], F32, s2) for b in range(2)]
                rel_h = [sb(f"rel_h{b}", [P, T], F32R, s2) for b in range(2)]
                rel_l = [sb(f"rel_l{b}", [P, T], F32R, s2) for b in range(2)]
            with ExitStack() as s2:
                mq = sb("mq", [P, HEADS, T], F32, s2)
                mk = sb("mk", [P, HEADS, T], F32, s2)

        landed = [sem(f"landed{s}") for s in range(2)]
        hi_done = sem("hi_done")
        hi_first, lo_first = sem("hi_first"), sem("lo_first")
        lo_done = sem("lo_done")
        ada_landed, ada_scaled, ada_red = [sem(f"ada_{x}") for x in ("landed", "scaled", "red")]
        x_landed = [sem(f"x_landed{j}") for j in range(2)]
        cols_landed, small_landed, pos_landed = [sem(f"{x}_landed") for x in ("cols", "small", "pos")]
        rel_landed = [sem(f"rel_landed{b}") for b in range(2)]
        rel_high, rel_low = sem("rel_high"), sem("rel_low")
        out_done = sem("out_done")
        setup1, setup2 = sem("setup1"), sem("setup2")
        c_landed, csil_done, csil_moved = sem("c_landed"), sem("csil_done"), sem("csil_moved")

        class Stage:
            pass

        def sems(stage, *names):
            return [sem(f"{stage}_{x}") for x in names]

        def norm_stage(name):
            s = Stage()
            s.sq, s.acc, s.ss, s.rstd, s.tmp, s.hi, s.lo = sems(name, "sq", "acc", "ss", "rstd", "tmp", "hi", "lo")
            return s

        def residual_stage(name):
            s = Stage()
            s.mm, s.h = sems(name, "mm", "h")
            return s

        def up_stage(name, w, b):
            s = Stage()
            s.w, s.b = w, b
            s.mm, s.base, s.tap, s.conv, s.silu, s.gated, s.hi, s.lo = sems(name, "mm", "base", "tap", "conv", "silu", "gated", "hi", "lo")
            return s

        norm_mix, norm_ffn, norm_final, norm_attn2, norm_mlp2 = [norm_stage(x) for x in ("nmix", "nffn", "nfin", "natt", "nmlp")]
        mod_done = sem("mod_done")
        res_out1, res_down1, res_out2, res_down2 = [residual_stage(x) for x in ("ro1", "rd1", "ro2", "rd2")]
        up1, up2 = up_stage("up1", "conv_w", "conv_b"), up_stage("up2", "conv_w2", "conv_b2")
        p1 = Stage()
        p1.mm, p1.act, p1.dve = sems("p1", "mm", "act", "dve")
        p2 = Stage()
        p2.mm, p2.dve = sems("p2", "mm", "dve")
        forget = Stage()
        forget.act, forget.dve = sems("forget", "act", "dve")
        decay = Stage()
        decay.hi, decay.dve, decay.head = sems("decay", "hi", "dve", "head")
        gate = Stage()
        gate.sq, gate.sum, gate.rstd, gate.done = sems("gate", "sq", "sum", "rstd", "done")
        mixing = Stage()
        mixing.mm, mixing.bias, mixing.done = sems("mixing", "mm", "bias", "done")
        att = Stage()
        att.qk, att.max, att.exp, att.rinv, att.norm, att.pt, att.ptc, att.pv = sems("att", "qk", "max", "exp", "rinv", "norm", "pt", "ptc", "pv")
        heads = Stage()
        heads.hi, heads.lo = sems("heads", "hi", "lo")
        mix = Stage()
        mix.hi, mix.lo = sems("mix", "hi", "lo")
        trig = Stage()
        trig.dve, trig.act, trig.row = sems("trig", "dve", "act", "row")
        weighted_acc = sem("weighted_acc")
        rope = Stage()
        rope.dve, rope.sq = sems("rope", "dve", "sq")
        head = Stage()
        head.sq, head.ss, head.root, head.rstd, head.pre, head.done = sems("head", "sq", "ss", "root", "rstd", "pre", "done")
        lat = Stage()
        lat.hi, lat.lo = sems("lat", "hi", "lo")

        P1 = {"u": [1, 2, 8, 9], "vg0": 3, "vg": [4, 5, 6, 7], "f": 10, "v0": 11, "v": [12, 13, 14, 15],
              "q": [16, 18, 20, 22], "k": [17, 19, 21, 23]}
        P2 = {"kv": 1, "rope": 2, "ql": [3, 4], "q": [5, 7, 9, 11], "k": [6, 8, 10, 12], "v0": 13, "v": [14, 15, 16, 17],
              "mq": [18 + 2 * x for x in range(HEADS)], "mk": [19 + 2 * x for x in range(HEADS)], "mv": [34, 35, 36, 37]}
        V2_BANKS = bank[4:6] + bank[0:2]

        JOB_KV, JOB_QL = 0, 1

        def job_c(p, which):
            return 2 + 2 * p + which

        def job_m(hd, which):
            return 2 + 2 * PAIRS + 2 * hd + which

        N_SQ = {}
        for x in range(2 + 2 * PAIRS + 2 * HEADS):
            N_SQ[x] = x + 1 + (x >= JOB_QL)

        def c_bank(p):
            return (6, 4, 0)[p % 3]

        def m_bank(hd):
            return 2 * (hd % 3)

        UNITS = HEADS * TB
        PAIR_UNITS = 2 * TB
        Q_STEPS = TB
        NORM_LAG = 2
        LAG = 3
        S_BANKS = [[bank[0], bank[2], bank[1]], [bank[2], bank[7], bank[0], bank[1]], [bank[0], bank[1], bank[7], bank[2]]]
        NEXT_BANK = bank[7]
        HEADS_BANKS = bank[5:7]
        MIX_BANKS = [bank[4], bank[7], bank[5], bank[6]]
        FIRST_OUT = bank[0:2]
        OUT_BANKS = bank[3:7]
        PIECES = [(KD - 2, 0, OUT_BANKS[2]), (KD - 1, 0, OUT_BANKS[3]), (KD - 2, 1, OUT_BANKS[0]), (KD - 1, 1, OUT_BANKS[1])]
        WHOLE = KD - 2
        DOWN_PIECES = [bank[5], bank[7]]

        def unit(a, u):
            return a * UNITS + u

        def head_tiles(a, p):
            if a == 0:
                return oh[:, p, :], ol[:, p, :]
            k = (None, 4, 0)[a] + p
            return xh[:, k, :], xl[:, k, :]

        CSIL_HALVES = [ss_final, bank[7]]
        c_raw = k1[:, 0:D // T, :].rearrange("p k t -> p (k t)")
        q1_room = [q1[:, b, 0:H] for b in range(4)]

        def norm_tile(x):
            return scratch[2 + x % 2][:, half(x // 2 % 2)]

        def sq_room(n):
            return scratch[n // 2 % 2][:, half(n % 2)] if n < KD else q1_room[n % 4]

        def scores_bank(a, U):
            return S_BANKS[a][U % len(S_BANKS[a])]

        block = ctx.enter_context(nc.Block())

        @block.sync
        def _(sp):
            def chunk(source, j, n, slot, width, first=False):
                if not first:
                    sp.wait_ge(lo_done, n - 1)
                sp.dma_start(raw[slot][:, 0:width], source[bass.ds(j * P, P), :]).then_inc(landed[slot], 16)

            def ada_chunk(a, first=False):
                if not first:
                    sp.wait_ge(ada_red, a)
                sp.dma_start(ada_raw[:, :, :], ada[bass.ds(a * P, P), :].rearrange("p (e k) -> p e k", e=ADA_TILES)).then_inc(ada_landed, 16)

            def stream(source, base, j0, count, with_ada=None):
                with sp.Fori(0, count // 2) as i:
                    for s in range(2):
                        chunk(source, i * 2 + (j0 + s), i * 2 + (base + j0 + s), (base + j0 + s) % 2, source.shape[1])
                        if with_ada:
                            with_ada(i, s)

            for j in range(2):
                sp.dma_start(h[:, :, half(j)], xT[:, half(j)].rearrange("(k p) t -> p k t", p=P)).then_inc(x_landed[j], 16)
                chunk(stream1, j, j, j, CHUNK, first=True)
            sp.dma_start(wsT[:, :, :], w_spatial_T.rearrange("j (g i) -> j g i", g=HEADS)).then_inc(small_landed, 16)
            sp.dma_start(bsp[:, :, :], b_spatial_rows.rearrange("p (t i) -> p t i", t=4)).then_inc(small_landed, 16)
            sp.dma_start(c_raw, c_row.partition_broadcast(P)).then_inc(c_landed, 16)
            ada_chunk(0, first=True)
            for n in range(2, BASE1["out"]):
                chunk(stream1, n, n, n % 2, CHUNK)

            def ada_out(i, s):
                if s:
                    ada_chunk(i + 1)

            def ada_up(i, s):
                ada_chunk(i * 2 + (4 + s))

            stream(stream1, 0, BASE1["out"], KD // 2, ada_out)
            ada_chunk(3)
            for s in range(2):
                n = BASE1["up"] + s
                chunk(stream1, n, n, n % 2, CHUNK)
            stream(stream1, 0, BASE1["up"] + 2, KF - 2, ada_up)
            stream(down1, BASE1["down"], 0, N_DOWN)
            base = N1 + N_DOWN
            for j in range(BASE2["out"] - base):
                chunk(stream2, j, base + j, (base + j) % 2, CHUNK)
            stream(stream2, base, BASE2["out"] - base, KD // 2)
            stream(stream2, base, BASE2["up"] - base, KF)
            stream(down2, BASE2["down"], 0, N_DOWN)
            for m in range(KD):
                sp.wait_ge(res_down2.h, m + 1)
                sp.dma_start(outT[m * P:(m + 1) * P, :], h[:, m, :]).then_inc(out_done, 16)
            sp.wait_ge(out_done, 16 * KD)

        @block.gpsimd
        def _(pool):
            def low(n, slot):
                pool.wait_ge(hi_done, n + 1)
                pool.tensor_tensor(wl[slot][:, :], raw[slot][:, :], wh[slot][:, :].bitcast(F32), ALU.subtract).then_inc(lo_done, 1)

            def lows(a, b):
                with pool.Fori(0, (b - a) // 2) as i:
                    for s in range(2):
                        low(i * 2 + (a + s), (a + s) % 2)
                if (b - a) % 2:
                    low(b - 1, (b - 1) % 2)

            pool.memset(ones[:, :], 1.0).then_inc(setup1, 1)
            pool.memset(eps_c[:, :], EPS).then_inc(setup1, 1)
            pool.memset(halfpi_c[:, :], float(np.pi / 2)).then_inc(setup1, 1)
            pool.memset(eps64_c[:, :], HD * EPS).then_inc(setup1, 1)
            pool.memset(eps2_c[:, :], EPS * EPS).then_inc(setup1, 1)
            pool.memset(ident1[:, :], 0.0).then_inc(setup1, 1)
            pool.memset(ident_b1[:, :], 0.0).then_inc(setup1, 1)
            pool.memset(causal_b[:, :], 0.0).then_inc(setup1, 1)
            pool.wait_ge(setup1, 8)
            for t in (ident1, ident_b1):
                pool.affine_select(out=t[:, :], in_=t[:, :], compare_op=ALU.not_equal, fill=1.0, base=0,
                                   pattern=[[-1, P]], channel_multiplier=1).then_inc(setup1, 1)
            pool.affine_select(out=causal_b[:, :], in_=causal_b[:, :], compare_op=ALU.is_ge, fill=MASKED, base=0,
                               pattern=[[-1, P]], channel_multiplier=1).then_inc(setup1, 1)
            w = CHUNK // 2
            pool.wait_ge(hi_first, 1)
            pool.tensor_tensor(wl[0][:, 0:w], raw[0][:, 0:w], wh[0][:, 0:w].bitcast(F32), ALU.subtract).then_inc(lo_first, 1)
            pool.wait_ge(hi_done, 1)
            pool.tensor_tensor(wl[0][:, w:], raw[0][:, w:], wh[0][:, w:].bitcast(F32), ALU.subtract).then_inc(lo_done, 1)
            low(1, 1)
            pool.wait_ge(small_landed, 32)
            pool.affine_select(out=wsT[:, :, :], in_=wsT[:, :, :], compare_op=ALU.is_ge, fill=0.0, base=0,
                               pattern=[[0, HEADS], [1, P]], channel_multiplier=-1).then_inc(setup1, 1)
            base = N1 + N_DOWN
            lows(2, base + 2)
            pool.wait_ge(res_down1.h, KD + 1)
            made = 0

            def constant(ins):
                nonlocal made
                made += 1
                ins.then_inc(setup2, 1)
                pool.wait_ge(setup2, made)

            constant(pool.memset(ident2[:, :], 0.0))
            constant(pool.memset(ident_b2[:, :], 0.0))
            constant(pool.memset(flip[:, :], 0.0))
            constant(pool.memset(ones96[0:96, :], 1.0))
            constant(pool.memset(ones96[96:P, :], 0.0))
            constant(pool.memset(ones64[:, :], 0.0))
            constant(pool.memset(chunk_b[:, :], 0.0))
            for t in (ident2, ident_b2):
                constant(pool.affine_select(out=t[:, :], in_=t[:, :], compare_op=ALU.not_equal, fill=1.0, base=0,
                                   pattern=[[-1, P]], channel_multiplier=1))
            constant(pool.affine_select(out=flip[:, :], in_=flip[:, :], compare_op=ALU.not_equal, fill=1.0, base=1 - P,
                               pattern=[[1, P]], channel_multiplier=1))
            constant(pool.tensor_copy(flip_r[:, :], flip[:, :]))
            constant(pool.memset(ones64[0:64, 0:64], 1.0))
            constant(pool.memset(ones64[64:P, 64:P], 1.0))
            constant(pool.memset(chunk_b[0:64, 64:P], MASKED))
            for t in rel:
                constant(pool.memset(t[64:P, T - 64:T], MASKED))

            def rel_parts(hd):
                b = hd % 2
                pool.wait_ge(rel_landed[b], 32 * (hd // 2 + 1))
                if hd >= 2:
                    pool.wait_ge(att.qk, unit(1, TB * (hd - 1)))
                pool.tensor_copy(rel_h[b][:, :], rel[b][:, :]).then_inc(rel_high, 1)
                pool.wait_ge(rel_high, hd + 1)
                pool.tensor_tensor(rel_l[b][:, :], rel[b][:, :], rel_h[b][:, :].bitcast(F32), ALU.subtract).then_inc(rel_low, 1)

            lows(base + 2, base + 4)
            rel_parts(0)
            rel_parts(1)
            lows(base + 4, BASE2["mkv"])
            for hd in range(2, HEADS):
                rel_parts(hd)
            lows(BASE2["mkv"], N_CHUNKS)

        LN_EXP = "natural_log_exp_and_others"

        @block.scalar
        def _(act):
            def high(n, slot, i16=None):
                if i16 is None:
                    act.wait_ge(landed[slot], 16 * (n // 2 + 1))
                    act.activation(wh[slot][:, :], raw[slot][:, :], ACT.Copy).then_inc(hi_done, 1)
                else:
                    act.wait_ge(landed[slot], i16 + 16 * (n // 2 + 1))
                    act.activation(wh[slot][:, :], raw[slot][:, :], ACT.Copy).then_inc(hi_done, 1)

            def split_next(n, used, value, i=None, per=2):
                if n + 2 >= N_CHUNKS:
                    return
                act.wait_ge(used, value)
                high(n + 2, n % 2, None if i is None else i * (16 * per // 2))

            def split_quarter(n, x, used, value):
                m, w = n + 2, CHUNK // 4
                if x == 0:
                    act.wait_ge(used, value)
                    act.wait_ge(landed[m % 2], 16 * (m // 2 + 1))
                ins = act.activation(wh[m % 2][:, w * x:w * x + w], raw[m % 2][:, w * x:w * x + w], ACT.Copy)
                if x == 3:
                    ins.then_inc(hi_done, 1)

            def quarters(n, used, value):
                return {KD + x: lambda x=x: split_quarter(n, x, used, value) for x in range(4)}

            def square(norm, m, ready, value, added, tokens=slice(0, T)):
                act.wait_ge(ready, value)
                act.wait_ge(norm.acc, added)
                act.activation(scratch[0][:, tokens], h[:, m, tokens], ACT.Square).then_inc(norm.sq, 1)

            def rsqrt(out, mean_of, width, eps, done, count, times=1):
                act.activation(out, mean_of, ACT.Ln, bias=eps[:, :], scale=float(times * times) / width).then_inc(done, 1)
                act.wait_ge(done, count + 1)
                act.activation(out, out, ACT.Exp, scale=-0.5).then_inc(done, 1)

            def norm_rsqrt(norm, j, eps):
                act.wait_ge(norm.ss, j + 1)
                rsqrt(scratch[1][:, half(j)], SS_BANKS[j][:, half(j)], D, eps, norm.rstd, 2 * j)

            def norm_high(norm, eps, shift=None, aside=()):
                for x in range(2 * KD):
                    j, k = x // KD, x % KD
                    if x in aside:
                        aside[x]()
                    if x == KD - 1:
                        norm_rsqrt(norm, 1, eps)
                    act.wait_ge(norm.tmp, x + 1)
                    if shift is None:
                        act.activation(xh[:, k, half(j)], norm_tile(x), ACT.Copy).then_inc(norm.hi, 1)
                    else:
                        act.activation(xh[:, k, half(j)], norm_tile(x), ACT.Identity, bias=mod[:, shift, k:k + 1]).then_inc(norm.hi, 1)

            def heads_high(a, p):
                act.wait_ge(att.pv, unit(a, PAIR_UNITS * (p + 1)))
                act.activation(head_tiles(a, p)[0], HEADS_BANKS[p % 2][:, :], ACT.Copy).then_inc(heads.hi, 1)

            def attend(a, prob, probT, neg_max, row_sum, col0, after=None, beside=None):
                for step in range(UNITS + LAG):
                    if beside is not None:
                        beside(step)
                    if step >= LAG:
                        U, w = unit(a, step - LAG), P * ((step - LAG) % TB + 1)
                        act.wait_ge(att.pt, U + 1)
                        if U >= 2:
                            act.wait_ge(att.pv, U - 1)
                        act.activation(probT[U % 2][:, 0:w], bank[3 + U % 2][:, 0:w], ACT.Copy).then_inc(att.ptc, 1)
                    if step < UNITS:
                        U, w = unit(a, step), P * (step % TB + 1)
                        c = col0 + step
                        act.wait_ge(att.max, U + 1)
                        if U >= 4:
                            act.wait_ge(att.pt, U - 3)
                        act.activation(prob[U % 4][:, 0:w], scores_bank(a, U)[:, 0:w], ACT.Exp, bias=neg_max[:, c:c + 1],
                                       scale=1.0, accum_out=row_sum[:, c:c + 1]).then_inc(att.exp, 1)
                        if after is not None and step % TB == TB - 1:
                            after(step // TB)
                    if step > PAIR_UNITS + LAG and (step - LAG - 1) % PAIR_UNITS == 0:
                        heads_high(a, (step - LAG - 1) // PAIR_UNITS - 1)
                heads_high(a, PAIRS - 1)

            def piece(res, norm, x):
                m, j, _ = PIECES[x]
                square(norm, m, res.h, WHOLE + x + 1, WHOLE + x + 1, half(j))

            def residual_out(res, norm, base):
                for c in range(KD // 2):
                    if c < KD // 2 - 1:
                        for m in (2 * c, 2 * c + 1):
                            square(norm, m, res.h, m + 1, m + 1)
                        split_next(base + c, res.mm, 2 * c + 2)
                piece(res, norm, 0)
                piece(res, norm, 1)
                norm_rsqrt(norm, 0, eps_c)
                piece(res, norm, 2)

            def after_out(res, norm, base):
                return {3: lambda: piece(res, norm, 3)} | quarters(base + KD // 2 - 1, res.mm, WHOLE + len(PIECES))

            def residual_down(res, norm, base, aside=None):
                def tile(m, base, i=None):
                    for e in range(2):
                        split_next(base + e, res.mm, m * 2 + (e + 1), i)
                    if norm is not None:
                        square(norm, m, res.h, m + 1, m + 1)

                tile(0, base)
                if aside is not None:
                    aside()
                with act.Fori(0, KD - 2) as i:
                    tile(i + 1, base + 2, i)
                if norm is not None:
                    split_next(base + 2 * KD - 2, res.mm, 2 * KD - 1)
                    square(norm, KD - 1, res.h, KD, KD, half(0))

            def up(L, base):
                act.preload_act_table(ACT.Silu)
                with act.Fori(0, KF // 2) as i:
                    def start(r):
                        act.wait_ge(L.mm, i * 4 + (r + 1))
                        act.activation(scratch[r][:, :], bank[r][:, :], ACT.Identity, bias=col(L.b, i * 4 + r),
                                       scale=col(L.w, i * 12 + (3 * r + 2))).then_inc(L.base, 1)

                    start(0)
                    split_next(base, L.mm, i * 4 + 2, i)
                    start(1)
                    for r in range(2):
                        act.wait_ge(L.conv, i * 4 + (r + 1))
                        act.activation(scratch[r][:, :], scratch[r][:, :], ACT.Silu).then_inc(L.silu, 1)
                    start(2)
                    split_next(base + 1, L.mm, i * 4 + 4, i)
                    start(3)
                    for r in range(2):
                        act.wait_ge(L.gated, i * 2 + (r + 1))
                        act.activation(acth[:, i * 2 + r, :], scratch[2 + r][:, :], ACT.Copy).then_inc(L.hi, 1)

            act.dma_start(cols[:, :], cols_in).then_inc(cols_landed, 16)
            act.preload_act_table_set(LN_EXP)
            act.wait_ge(setup1, 5)

            def input_squares(j):
                act.wait_ge(x_landed[j], 16)
                for k in range(KD):
                    n = KD * j + k
                    if k >= 4:
                        act.wait_ge(norm_mix.acc, n - 2)
                    act.activation(sq_room(n), h[:, k, half(j)], ACT.Square).then_inc(norm_mix.sq, 1)

            input_squares(0)
            w = CHUNK // 2
            act.wait_ge(landed[0], 16)
            act.activation(wh[0][:, 0:w], raw[0][:, 0:w], ACT.Copy).then_inc(hi_first, 1)
            act.activation(wh[0][:, w:], raw[0][:, w:], ACT.Copy).then_inc(hi_done, 1)
            norm_rsqrt(norm_mix, 0, eps_c)
            norm_high(norm_mix, eps_c, None, {3: lambda: input_squares(1), KD - 2: lambda: high(1, 1)})
            act.wait_ge(c_landed, 16)
            act.activation(csil[:, :], c_raw, ACT.Exp, scale=-1.0).then_inc(csil_done, 1)
            act.wait_ge(csil_done, 1)
            act.activation(csil[:, :], csil[:, :], ACT.Ln, bias=ones[:, 0:1]).then_inc(csil_done, 1)
            act.wait_ge(csil_done, 2)
            act.activation(csil[:, :], csil[:, :], ACT.Exp, scale=-1.0).then_inc(csil_done, 1)

            def gelu_u(t):
                act.wait_ge(p1.mm, P1["u"][t])
                act.activation(u_sb[:, t, :], bank[4 + t][:, :], ACT.Gelu_apprx_tanh).then_inc(p1.act, 1)

            split_next(0, p1.mm, P1["u"][1])
            gelu_u(0)
            gelu_u(1)
            split_next(1, p1.mm, P1["vg0"])
            split_next(2, p1.mm, P1["vg"][3])
            for t in range(TB):
                act.activation(vg[:, t, :], bank[t][:, :], ACT.Gelu_apprx_tanh).then_inc(p1.act, 1)
            split_next(3, p1.mm, P1["u"][3])
            gelu_u(2)
            gelu_u(3)
            split_next(4, p1.mm, P1["f"])
            act.preload_act_table_set(LN_EXP)
            act.wait_ge(gate.sum, TB)
            rsqrt(vrs[:, :], vsum[:, :], HD, eps_c, gate.rstd, 0)
            act.wait_ge(forget.dve, 1)
            act.activation(lf[0][:, :], bank[4][:, :], ACT.Abs, bias=col("b_forget")).then_inc(forget.act, 1)
            act.wait_ge(forget.act, 1)
            act.activation(lf[0][:, :], lf[0][:, :], ACT.Exp, scale=-1.0).then_inc(forget.act, 1)
            act.wait_ge(forget.act, 2)
            act.activation(lf[0][:, :], lf[0][:, :], ACT.Ln, bias=ones[:, 0:1]).then_inc(forget.act, 1)
            act.wait_ge(forget.dve, 4)
            act.activation(dec_q[:, :], dec_all[:, :], ACT.Copy).then_inc(decay.hi, 1)
            split_next(5, p1.mm, P1["v0"])
            split_next(6, p1.mm, P1["v"][3])

            def queries(p):
                act.wait_ge(p1.mm, P1["q"][p])
                act.activation(q1[:, p, :], (bank[0] if p == 0 else NEXT_BANK)[:, :], ACT.Copy, scale=HD ** -0.5).then_inc(p1.act, 1)

            queries(0)
            split_next(7, p1.mm, P1["k"][0])

            def beside(step):
                p = step // PAIR_UNITS + 1
                if p < PAIRS and step % PAIR_UNITS == Q_STEPS:
                    queries(p)
                if p < PAIRS and step % PAIR_UNITS == PAIR_UNITS - 1:
                    split_next(7 + p, p1.mm, P1["k"][p])
                t = step - PAIR_UNITS * (PAIRS - 1)
                if 0 <= t < 4:
                    act.wait_ge(p1.mm, P1["k"][PAIRS - 1])
                    act.wait_ge(mixing.done, t + 1)
                    act.activation(xh[:, 4 + t, :], scratch[t][:, :], ACT.Copy).then_inc(mix.hi, 1)

            attend(0, prob1, probT1, neg_max1, row_sum1, 0, None, beside)
            residual_out(res_out1, norm_ffn, BASE1["out"])
            norm_high(norm_ffn, eps_c, None, after_out(res_out1, norm_ffn, BASE1["out"]))
            up(up1, BASE1["up"])

            def sines():
                act.wait_ge(trig.dve, 8)
                act.activation(turn, ang, ACT.Abs).then_inc(trig.act, 1)
                act.wait_ge(trig.act, 1)
                act.activation(q_trig[64:96, :], turn[64:96, :], ACT.Sin, bias=halfpi_c[64:96, :], scale=-1.0).then_inc(trig.act, 1)
                act.activation(k_trig[0:64, :], turn[0:64, :], ACT.Sin, bias=halfpi_c[0:64, :], scale=-1.0).then_inc(trig.act, 1)
                act.activation(q_trig[96:P, :], ang[96:P, :], ACT.Sin).then_inc(trig.act, 1)
                act.activation(k_trig[64:P, :], ang[64:P, :], ACT.Sin).then_inc(trig.act, 1)
                act.preload_act_table_set(LN_EXP)

            act.wait_ge(ada_red, N_ADA)
            act.dma_start(pos_i, positions.partition_broadcast(P)).then_inc(pos_landed, 16)
            residual_down(res_down1, norm_final, BASE1["down"], sines)

            def load_rel(hd):
                if hd >= 2:
                    act.wait_ge(rel_low, hd - 1)
                src = bass.AP(rel_rows.tensor, hd * REL_LEN, [[1, P], [1, T - 64]])
                act.dma_start(rel[hd % 2][:, 0:T - 64], src).then_inc(rel_landed[hd % 2], 16)
                src = bass.AP(rel_rows.tensor, hd * REL_LEN + T - 64, [[1, 64], [1, 64]])
                act.dma_start(rel[hd % 2][0:64, T - 64:T], src).then_inc(rel_landed[hd % 2], 16)

            norm_rsqrt(norm_attn2, 0, eps2_c)

            def last_half():
                square(norm_final, KD - 1, res_down1.h, KD + 1, KD, half(1))

            norm_high(norm_attn2, eps2_c, 0, {3: last_half} | quarters(N1 + N_DOWN - 1, res_down1.mm, 2 * KD + 1))
            act.wait_ge(res_down1.h, KD + 1)
            load_rel(0)
            load_rel(1)
            act.wait_ge(norm_final.ss, 1)
            rsqrt(ss_acc[:, :], SS_FINAL[:, :], D, eps_c, norm_final.rstd, 0)
            base = N1 + N_DOWN

            def head_square(out, tile, mm):
                act.wait_ge(p2.mm, mm)
                act.activation(out, tile, ACT.Square).then_inc(head.sq, 1)

            def head_root(job, width, ss_bank, times=1):
                act.wait_ge(head.ss, job + 1)
                if job >= 4:
                    act.wait_ge(head.done, job - 3)
                r = scratch[job % 4]
                act.activation(r[:, :], ss_bank[:, :], ACT.Ln, bias=(eps_c if times == 1 else eps64_c)[:, :],
                               scale=float(times * times) / width).then_inc(head.root, 1)
                act.wait_ge(head.root, job + 1)
                act.activation(r[:, :], r[:, :], ACT.Exp, scale=-0.5).then_inc(head.rstd, 1)

            split_next(base, p2.mm, P2["rope"])
            head_square(sq2[0][:, :], bank[0][:, :], P2["kv"])
            for b in range(2):
                act.activation(sqk[b][64:P, :], bank[1][64:P, :], ACT.Square).then_inc(rope.sq, 1)
            split_next(base + 1, p2.mm, P2["ql"][1])
            head_square(sq2[1][:, :], bank[2][:, :], P2["ql"][0])
            act.wait_ge(norm_attn2.lo, 2 * KD)
            head_square(scratch[3][:, :], bank[3][:, :], P2["ql"][1])
            head_root(JOB_KV, P, bank[4])
            head_root(JOB_QL, 2 * P, bank[5])
            act.wait_ge(head.pre, 1)
            act.activation(kvh[:, :], scratch[0][:, :], ACT.Copy).then_inc(lat.hi, 1)
            for t in range(2):
                act.wait_ge(head.pre, 2 + t)
                act.activation(qlh[:, t, :], scratch[2 + t][:, :], ACT.Copy).then_inc(lat.hi, 1)
            act.wait_ge(lat.lo, 3)
            for p in range(PAIRS + 1):
                if p < PAIRS:
                    for which in range(2):
                        x = job_c(p, which)
                        if x >= 2:
                            act.wait_ge(head.ss, x - 1)
                        head_square(sq2[which][:, :], bank[c_bank(p) + which][:, :], P2["qk"[which]][p])
                    split_next(base + 2 + p, p2.mm, P2["k"][p])
                if p:
                    for which in range(2):
                        x = job_c(p - 1, which)
                        head_root(x, HD, SS_BANKS[which], 1 if which else 8)
            split_next(base + 6, p2.mm, P2["v0"])
            load_rel(2)

            def next_chunk(step):
                if TB <= step < TB + 4:
                    split_quarter(base + 7, step - TB, p2.mm, P2["v"][TB - 1])

            attend(1, prob2, probT2, neg_max2, row_sum2, 0, lambda hd: load_rel(hd + 3) if hd + 3 < HEADS else None, next_chunk)
            for hd in range(HEADS + 1):
                if hd < HEADS:
                    for which in range(2):
                        x = job_m(hd, which)
                        act.wait_ge(head.ss, x - 3 if hd else x - which)
                        if which == 0:
                            head_square(sq2[hd % 2][:, :], bank[m_bank(hd)][:, :], P2["mq"][hd])
                        else:
                            head_square(sqk[hd % 2][0:64, :], bank[m_bank(hd) + 1][0:64, :], P2["mk"][hd])
                if hd:
                    for which in range(2):
                        head_root(job_m(hd - 1, which), MLA_QK, bank[6 + which])

            def next_chunks(step):
                if TB <= step < TB + 8:
                    n, x = (step - TB) // 4, (step - TB) % 4
                    split_quarter(base + 8 + n, x, p2.mm, (P2["mq"][HEADS - 1], P2["mv"][TB - 1])[n])

            attend(2, prob2, probT2, neg_max2, row_sum2, UNITS, None, next_chunks)
            residual_out(res_out2, norm_mlp2, BASE2["out"])
            norm_high(norm_mlp2, eps_c, 3, after_out(res_out2, norm_mlp2, BASE2["out"]))
            up(up2, BASE2["up"])
            residual_down(res_down2, None, BASE2["down"])

        @block.vector
        def _(dve):
            def ada_sum(a):
                dve.wait_ge(ada_landed, a * 16 + 16)
                if isinstance(a, int) and a < ADA_EARLY:
                    dve.tensor_tensor(ada_raw[:, :, :], ada_raw[:, :, :],
                                      csil[:, :].rearrange("p (e k) -> p e k", e=1).broadcast_to([P, ADA_TILES, D]),
                                      ALU.mult).then_inc(ada_scaled, 1)
                    dve.wait_ge(ada_scaled, a + 1)
                else:
                    dve.wait_ge(csil_moved, 2)
                    for e, c in enumerate(CSIL_HALVES):
                        part = ada_raw[:, :, T * e:T * e + T]
                        dve.tensor_tensor(part, part, c[:, :].rearrange("p (e k) -> p e k", e=1).broadcast_to([P, ADA_TILES, T]),
                                          ALU.mult).then_inc(ada_scaled, 1)
                    dve.wait_ge(ada_scaled, a * 2 - (ADA_EARLY - 2))
                dve.tensor_reduce(mod_sum[:, bass.ds(a * ADA_TILES, ADA_TILES)], ada_raw[:, :, :], AX_X, ALU.add).then_inc(ada_red, 1)

            def zero(norm, acc):
                dve.memset(acc[:, :], 0.0).then_inc(norm.acc, 1)

            def add_square(norm, acc, n, tokens=slice(0, T)):
                dve.wait_ge(norm.acc, n + 1)
                dve.wait_ge(norm.sq, n + 1)
                dve.tensor_tensor(acc[:, tokens], acc[:, tokens], scratch[0][:, tokens], ALU.add).then_inc(norm.acc, 1)

            def norm_tiles(norm, scale, shift=None, aside=None):
                for x in range(2 * KD + 1):
                    if x == 3 and aside is not None:
                        aside()
                    if x < 2 * KD:
                        j, k = x // KD, x % KD
                        if k == 0:
                            dve.wait_ge(norm.rstd, 2 * j + 2)
                        if x >= 4:
                            dve.wait_ge(norm.lo, x - 3)
                        dve.scalar_tensor_tensor(norm_tile(x), h[:, k, half(j)], scale(k), scratch[1][:, half(j)], ALU.mult, ALU.mult).then_inc(norm.tmp, 1)
                    if x:
                        j, k = (x - 1) // KD, (x - 1) % KD
                        hi = xh[:, k, half(j)].bitcast(F32)
                        dve.wait_ge(norm.hi, x)
                        if shift is None:
                            dve.tensor_tensor(xl[:, k, half(j)], norm_tile(x - 1), hi, ALU.subtract).then_inc(norm.lo, 1)
                        else:
                            dve.scalar_tensor_tensor(xl[:, k, half(j)], norm_tile(x - 1), shift(k), hi, ALU.add, ALU.subtract).then_inc(norm.lo, 1)

            def add_residual(res, m, b, value, gain, tokens=slice(0, T)):
                dve.wait_ge(res.mm, value)
                if gain is None:
                    dve.tensor_tensor(h[:, m, tokens], h[:, m, tokens], b[:, tokens], ALU.add).then_inc(res.h, 1)
                else:
                    dve.scalar_tensor_tensor(h[:, m, tokens], b[:, tokens], mod[:, gain, bass.ds(m, 1)], h[:, m, tokens], ALU.mult, ALU.add).then_inc(res.h, 1)

            def piece(res, norm, gain, x):
                m, j, b = PIECES[x]
                add_residual(res, m, b, WHOLE + x + 1, gain, half(j))
                add_square(norm, ss_acc, WHOLE + x, half(j))

            def residual_out(res, norm, gain, ada_too):
                zero(norm, ss_acc)
                for m in range(WHOLE):
                    if ada_too and m in (0, 2):
                        ada_sum(m // 2 + 1)
                    add_residual(res, m, (FIRST_OUT[m] if m < 2 else OUT_BANKS[m % 4]), m + 1, gain)
                    add_square(norm, ss_acc, m)
                for x in range(len(PIECES) - 1):
                    piece(res, norm, gain, x)

            def residual_down(res, gain):
                with dve.Fori(0, KD // 2) as i:
                    for r in range(2):
                        add_residual(res, i * 2 + r, bank[4 + r], i * 4 + (2 * r + 2), gain)

            def add_weighted(n, m, norm, tokens=slice(0, T)):
                dve.wait_ge(weighted_acc, n + 1)
                dve.wait_ge(norm.sq, n + 1)
                dve.scalar_tensor_tensor(ss_acc[:, tokens], scratch[0][:, tokens], final_w[:, bass.ds(m, 1)], ss_acc[:, tokens],
                                         ALU.mult, ALU.add).then_inc(weighted_acc, 1)
                add_square(norm, ss_final, n, tokens)

            def residual_down_final(res, norm, aside):
                zero(norm, ss_final)
                dve.memset(ss_acc[:, :], 0.0).then_inc(weighted_acc, 1)

                def tiles(m0, i, count=2):
                    for r in range(count):
                        m = i * 2 + (m0 + r)
                        add_residual(res, m, bank[4 + r], i * 4 + (2 * m0 + 2 * r + 2), None)
                        add_weighted(m, m, norm)

                tiles(0, 0)
                aside()
                with dve.Fori(0, KD // 2 - 2) as i:
                    tiles(2, i)
                tiles(KD - 2, 0, 1)
                last_half(res, norm, 0)

            def last_half(res, norm, j):
                add_residual(res, KD - 1, DOWN_PIECES[j], 2 * KD + j, None, half(j))
                add_weighted(KD - 1 + j, KD - 1, norm, half(j))

            def up(L, ada_too):
                def four_tiles(i, ada_chunks):
                    def conv(r):
                        for tap in (1, 0):
                            d = 2 - tap
                            if tap == 1:
                                dve.wait_ge(L.base, i * 4 + (r + 1))
                            else:
                                dve.wait_ge(L.tap, i * 4 + (r + 1))
                            dve.scalar_tensor_tensor(scratch[r][:, d:T], bank[r][:, 0:T - d], col(L.w, i * 12 + (3 * r + tap)),
                                                     scratch[r][:, d:T], ALU.mult, ALU.add).then_inc(L.tap if tap else L.conv, 1)

                    def gated(r):
                        dve.wait_ge(L.conv, i * 4 + (r + 1))
                        dve.wait_ge(L.silu, i * 2 + (r - 1))
                        dve.tensor_tensor(scratch[r][:, :], scratch[r][:, :], scratch[r - 2][:, :], ALU.mult).then_inc(L.gated, 1)

                    def low(r):
                        dve.wait_ge(L.hi, i * 2 + (r - 1))
                        dve.tensor_tensor(actl[:, i * 2 + (r - 2), :], scratch[r][:, :], acth[:, i * 2 + (r - 2), :].bitcast(F32), ALU.subtract).then_inc(L.lo, 1)

                    if ada_chunks > 0:
                        ada_sum(i * 2 + 3)
                    conv(0)
                    conv(1)
                    if ada_chunks > 1:
                        ada_sum(i * 2 + 4)
                    conv(2)
                    gated(2)
                    conv(3)
                    gated(3)
                    low(2)
                    low(3)

                with dve.Fori(0, KF // 2 - 1) as i:
                    four_tiles(i, 2 if ada_too else 0)
                four_tiles(KF // 2 - 1, 1 if ada_too else 0)

            def heads_low(a, p):
                high, low = head_tiles(a, p)
                dve.wait_ge(heads.hi, PAIRS * a + p + 1)
                dve.tensor_tensor(low, HEADS_BANKS[p % 2][:, :], high.bitcast(F32), ALU.subtract).then_inc(heads.lo, 1)

            def attend(a, prob, neg_max, row_sum, col0, before=None, beside=None):
                for step in range(UNITS + NORM_LAG):
                    if step >= NORM_LAG:
                        u = step - NORM_LAG
                        U, w, c = unit(a, u), P * (u % TB + 1), col0 + u
                        dve.wait_ge(att.exp, U + 1)
                        dve.reciprocal(row_sum[:, c:c + 1], row_sum[:, c:c + 1]).then_inc(att.rinv, 1)
                        dve.wait_ge(att.rinv, U + 1)
                        dve.tensor_scalar(prob[U % 4][:, 0:w], prob[U % 4][:, 0:w], row_sum[:, c:c + 1], None, ALU.mult).then_inc(att.norm, 1)
                    if step < UNITS:
                        if before is not None:
                            before(step)
                        U, w, c = unit(a, step), P * (step % TB + 1), col0 + step
                        dve.wait_ge(att.qk, U + 1)
                        dve.tensor_reduce(neg_max[:, c:c + 1], scores_bank(a, U)[:, 0:w], AX_X, ALU.max, negate=True).then_inc(att.max, 1)
                        if beside is not None:
                            beside(step)
                    if step > PAIR_UNITS + LAG + 1 and (step - LAG - 2) % PAIR_UNITS == 0:
                        heads_low(a, (step - LAG - 2) // PAIR_UNITS - 1)
                heads_low(a, PAIRS - 1)

            def mix_low(e0, count, tile0, source):
                for e in range(count):
                    dve.wait_ge(mix.hi, e0 + e + 1)
                    dve.tensor_tensor(xl[:, tile0 + e, :], source(e)[:, :], xh[:, tile0 + e, :].bitcast(F32), ALU.subtract).then_inc(mix.lo, 1)

            zero(norm_mix, ss_acc)

            def input_sums(j):
                for n in range(KD * j, KD * j + KD):
                    dve.wait_ge(norm_mix.acc, n + 1)
                    dve.wait_ge(norm_mix.sq, n + 1)
                    dve.tensor_tensor(ss_acc[:, half(j)], ss_acc[:, half(j)], sq_room(n), ALU.add).then_inc(norm_mix.acc, 1)

            input_sums(0)
            dve.wait_ge(cols_landed, 16)
            norm_tiles(norm_mix, lambda k: col("mix_g", k), None, lambda: input_sums(1))
            dve.wait_ge(csil_done, 3)
            dve.tensor_tensor(csil[:, :], csil[:, :], c_raw, ALU.mult).then_inc(csil_done, 1)
            dve.wait_ge(csil_done, 4)
            ada_sum(0)
            for t in range(TB):
                dve.wait_ge(p1.act, 3 + t)
                dve.tensor_tensor(scratch[2 + t % 2][:, :], vg[:, t, :], vg[:, t, :], ALU.mult).then_inc(gate.sq, 1)
                dve.wait_ge(gate.sq, t + 1)
                dve.tensor_reduce(vsum[:, HEADS * t:HEADS * t + HEADS], scratch[2 + t % 2][:, :].rearrange("p (g d) -> p g d", g=HEADS),
                                  AX_X, ALU.add).then_inc(gate.sum, 1)
            dve.wait_ge(p1.mm, P1["f"])
            dve.tensor_scalar(lf[1][:, :], bank[4][:, :], col("b_forget"), 0.0, ALU.add, ALU.min).then_inc(forget.dve, 1)
            dve.memset(scratch[0][:, :], 1.0).then_inc(forget.dve, 1)
            dve.wait_ge(forget.act, 3)
            dve.wait_ge(forget.dve, 2)
            dve.tensor_tensor(lf[1][:, :], lf[1][:, :], lf[0][:, :], ALU.subtract).then_inc(forget.dve, 1)
            dve.wait_ge(forget.dve, 3)
            dve.tensor_tensor_scan(dec_all[:, :], scratch[0][:, :], lf[1][:, :], 0.0, ALU.mult, ALU.add).then_inc(forget.dve, 1)
            dve.wait_ge(decay.hi, 1)
            dve.tensor_tensor(lf[0][:, :], dec_all[:, :], dec_q[:, :].bitcast(F32), ALU.subtract).then_inc(decay.dve, 1)
            dve.wait_ge(decay.dve, 1)
            dve.tensor_scalar(dec_all[0:32, :], dec_q[0:32, :].bitcast(F32), -1.0, None, ALU.mult).then_inc(decay.dve, 1)
            dve.tensor_scalar(dec_all[32:64, :], lf[0][32:64, :], -1.0, None, ALU.mult).then_inc(decay.dve, 1)
            dve.memset(dec_all[64:P, :], 1.0).then_inc(decay.dve, 1)
            dve.tensor_copy(dec_q[96:P, :], lf[0][96:P, :]).then_inc(decay.dve, 1)
            dve.wait_ge(decay.dve, 5)
            dve.tensor_scalar(dec_q[0:64, :], dec_all[0:64, :], 0.0, 1.0, ALU.mult, ALU.add).then_inc(decay.dve, 1)
            dve.wait_ge(decay.dve, 6)
            dve.wait_ge(gate.rstd, 2)
            for t in range(TB):
                groups = vg[:, t, :].rearrange("p (g d) -> p g d", g=HEADS)
                dve.tensor_tensor(groups, groups,
                                  vrs[:, HEADS * t:HEADS * t + HEADS].rearrange("p (g c) -> p g c", c=1).broadcast_to([P, HEADS, HD]),
                                  ALU.mult).then_inc(gate.done, 1)
            for t in range(TB):
                dve.wait_ge(p1.mm, P1["v"][t])
                dve.tensor_copy(v1[:, t, :], bank[t][:, :]).then_inc(p1.dve, 1)
            dve.wait_ge(small_landed, 32)
            for t in range(4):
                dve.wait_ge(mixing.mm, t + 1)
                dve.scalar_tensor_tensor(scratch[t][:, :].rearrange("p (n i) -> p n i", n=TB), MIX_BANKS[t][:, :].rearrange("p (n i) -> p n i", n=TB),
                                         col("gmlp_g", t), bsp[:, t:t + 1, :].broadcast_to([P, TB, P]), ALU.mult, ALU.add).then_inc(mixing.bias, 1)
                dve.wait_ge(mixing.bias, t + 1)
                dve.tensor_tensor(scratch[t][:, :], scratch[t][:, :], u_sb[:, t, :], ALU.mult).then_inc(mixing.done, 1)

            def keys(p):
                dve.wait_ge(p1.mm, P1["k"][p])
                dve.tensor_copy(k1[:, p, :], (bank[1] if p == 0 else NEXT_BANK)[:, :]).then_inc(p1.dve, 1)

            keys(0)

            def decay_head(hd):
                if hd < HEADS:
                    dve.tensor_scalar(dec_k[hd % 2][:, :], dec_all[:, :], col("head_row", hd), None, ALU.mult).then_inc(decay.head, 1)

            decay_head(0)
            decay_head(1)

            def next_keys(step):
                p = step // PAIR_UNITS + 1
                if p < PAIRS and step % PAIR_UNITS == PAIR_UNITS - 1:
                    keys(p)

            def beside(step):
                if step % TB == TB - 1:
                    decay_head(step // TB + 2)
                if step in (UNITS - 2, UNITS - 1):
                    e = step - (UNITS - 2)
                    dve.tensor_copy(CSIL_HALVES[e][:, :], csil[:, T * e:T * e + T]).then_inc(csil_moved, 1)
                t = step - PAIR_UNITS * (PAIRS - 1) - 1
                if 0 <= t < 4:
                    mix_low(t, 1, 4 + t, lambda e: scratch[t])

            attend(0, prob1, neg_max1, row_sum1, 0, next_keys, beside)
            residual_out(res_out1, norm_ffn, None, True)
            norm_tiles(norm_ffn, lambda k: col("ffn_g", k), None, lambda: piece(res_out1, norm_ffn, None, 3))
            up(up1, True)
            dve.wait_ge(ada_red, N_ADA)
            a = COLS["b_ada"][0]
            dve.tensor_tensor(mod[:, :, :], mod_sum[:, :].rearrange("p (j k) -> p j k", j=6),
                              cols[:, a:a + 6 * KD].rearrange("p (j k) -> p j k", j=6), ALU.add).then_inc(mod_done, 1)
            dve.wait_ge(mod_done, 1)
            for j, g in enumerate(("attn2_g", "mlp2_g")):
                a = COLS[g][0]
                dve.scalar_tensor_tensor(modA[:, j, :], mod[:, 3 * j + 1, :], 1.0, cols[:, a:a + KD], ALU.add, ALU.mult).then_inc(mod_done, 1)
            a = COLS["final_g"][0]
            gains = cols[:, a:a + KD]
            dve.tensor_tensor(final_w[:, :], gains, gains, ALU.mult).then_inc(mod_done, 1)
            dve.wait_ge(mod_done, 4)
            dve.tensor_scalar(final_w[:, :], final_w[:, :], EPS, None, ALU.add).then_inc(mod_done, 1)
            dve.tensor_tensor(modA[:, 0, :], modA[:, 0, :], gains, ALU.mult).then_inc(mod_done, 1)
            dve.wait_ge(mod_done, 6)
            TURNS = 1.5 * 2.0 ** 23
            C1, C2 = 6.28125, 507.0 / 2 ** 18
            C3 = float(2 * np.pi - C1 - C2)
            dve.wait_ge(pos_landed, 16)
            steps = [
                lambda: dve.tensor_copy(ang, pos_i),
                lambda: dve.tensor_scalar(ang, ang, col("inv_freq"), None, ALU.mult),
                lambda: dve.tensor_scalar(turn, ang, float(0.5 / np.pi), TURNS, ALU.mult, ALU.add),
                lambda: dve.tensor_scalar(turn, turn, -TURNS, None, ALU.add),
                lambda: dve.scalar_tensor_tensor(ang, turn, -C1, ang, ALU.mult, ALU.add),
                lambda: dve.scalar_tensor_tensor(ang, turn, -C2, ang, ALU.mult, ALU.add),
                lambda: dve.scalar_tensor_tensor(ang, turn, -C3, ang, ALU.mult, ALU.add),
                lambda: dve.tensor_scalar(ang, ang, 3.1415925, -3.1415925, ALU.min, ALU.max),
            ]
            for n, step in enumerate(steps):
                step().then_inc(trig.dve, 1)
                dve.wait_ge(trig.dve, n + 1)
            dve.memset(q_trig[0:64, :], 1.0).then_inc(trig.dve, 1)

            def trig_rows():
                dve.wait_ge(trig.act, 5)
                dve.wait_ge(trig.dve, 9)
                dve.tensor_scalar(q_trig, q_trig, col("mq_g"), col("q_sign"), ALU.mult, ALU.mult).then_inc(trig.row, 1)
                dve.tensor_scalar(k_trig, k_trig, col("mkr_g"), col("k_sign"), ALU.mult, ALU.mult).then_inc(trig.row, 1)

            residual_down_final(res_down1, norm_final, trig_rows)

            norm_tiles(norm_attn2, lambda k: modA[:, 0, k:k + 1], lambda k: mod[:, 0, k:k + 1], lambda: last_half(res_down1, norm_final, 1))
            dve.wait_ge(trig.row, 2)
            dve.wait_ge(rope.sq, 2)
            dve.tensor_tensor(k_rope[64:P, :], bank[1][64:P, :], k_trig[64:P, :], ALU.mult).then_inc(rope.dve, 1)
            dve.tensor_tensor(turn[64:P, :], bank[1][0:64, :], k_trig[0:64, :], ALU.mult).then_inc(rope.dve, 1)
            dve.wait_ge(rope.dve, 2)
            dve.tensor_tensor(k_rope[64:P, :], k_rope[64:P, :], turn[64:P, :], ALU.add).then_inc(rope.dve, 1)

            def head_rstd(job):
                dve.wait_ge(head.rstd, job + 1)
                return scratch[job % 4]

            r = head_rstd(JOB_KV)
            dve.scalar_tensor_tensor(r[:, :], bank[0][:, :], col("kvl_g"), r[:, :], ALU.mult, ALU.mult).then_inc(head.pre, 1)
            r = head_rstd(JOB_QL)
            for t in range(2):
                dve.scalar_tensor_tensor(scratch[2 + t][:, :], bank[2 + t][:, :], col("ql_g", t), r[:, :], ALU.mult, ALU.mult).then_inc(head.pre, 1)
            dve.wait_ge(lat.hi, 1)
            dve.tensor_tensor(kvl[:, :], scratch[0][:, :], kvh[:, :].bitcast(F32), ALU.subtract).then_inc(lat.lo, 1)
            for t in range(2):
                dve.wait_ge(lat.hi, 2 + t)
                dve.tensor_tensor(qll[:, t, :], scratch[2 + t][:, :], qlh[:, t, :].bitcast(F32), ALU.subtract).then_inc(lat.lo, 1)
            dve.wait_ge(norm_final.rstd, 2)
            for k in range(KD):
                dve.scalar_tensor_tensor(h[:, k, :], h[:, k, :], col("final_g", k), ss_acc[:, :], ALU.mult, ALU.mult).then_inc(norm_final.tmp, 1)
            for p in range(PAIRS):
                for which, (out, g) in enumerate(((cq, "cq_g"), (ck, "ck_g"))):
                    r = head_rstd(job_c(p, which))
                    dve.scalar_tensor_tensor(out[:, p, :], bank[c_bank(p) + which][:, :], col(g), r[:, :], ALU.mult, ALU.mult).then_inc(head.done, 1)
            for t in range(TB):
                dve.wait_ge(p2.mm, P2["v"][t])
                dve.tensor_copy(v2[:, t, :], V2_BANKS[t][:, :]).then_inc(p2.dve, 1)
            attend(1, prob2, neg_max2, row_sum2, 0)

            def mla_values(t):
                dve.wait_ge(p2.mm, P2["mv"][t])
                dve.tensor_copy(v2[:, t, :], V2_BANKS[t][:, :]).then_inc(p2.dve, 1)

            for hd in range(HEADS):
                if hd == HEADS - 1:
                    for t in range(TB):
                        mla_values(t)
                tile = bank[m_bank(hd)]
                r = head_rstd(job_m(hd, 0))
                dve.tensor_tensor(mq[:, hd, :], tile[:, :], q_trig, ALU.mult).then_inc(head.pre, 1)
                dve.wait_ge(head.pre, 4 + 2 * hd)
                dve.tensor_tensor(mq[:, hd, :], mq[:, hd, :], r[:, :], ALU.mult).then_inc(head.done, 1)
                tile = bank[m_bank(hd) + 1]
                r = head_rstd(job_m(hd, 1))
                dve.scalar_tensor_tensor(mk[0:64, hd, :], tile[0:64, :], col_at("mk_g", 0, 64), r[0:64, :], ALU.mult, ALU.mult).then_inc(head.pre, 1)
                dve.tensor_tensor(mk[64:P, hd, :], k_rope[64:P, :], r[64:P, :], ALU.mult).then_inc(head.done, 1)
            attend(2, prob2, neg_max2, row_sum2, UNITS)
            dve.wait_ge(norm_final.tmp, KD)
            residual_out(res_out2, norm_mlp2, 2, False)
            norm_tiles(norm_mlp2, lambda k: modA[:, 1, k:k + 1], lambda k: mod[:, 3, k:k + 1], lambda: piece(res_out2, norm_mlp2, 2, 3))
            up(up2, False)
            residual_down(res_down2, 5)

        @block.tensor
        def _(pe):
            def split_product(out, lhs, rhs, first, last):
                for n, (a, b) in enumerate(((0, 0), (0, 1), (1, 0))):
                    ins = pe.matmul(out, lhs[a], rhs[b], start=first and n == 0, stop=last and n == 2)
                return ins

            def weights(slot, a, b):
                return wh[slot][:, a:b], wl[slot][:, a:b]

            def inputs(k, a=0, b=T):
                return xh[:, k, a:b], xl[:, k, a:b]

            def features_tile(out, slot, e, tokens=slice(0, T), inputs=inputs):
                for k in range(KD):
                    a = PAIR_COLS * k + P * e
                    ins = split_product(out[:, tokens], weights(slot, a, a + P), inputs(k, tokens.start, tokens.stop), k == 0, k == KD - 1)
                return ins

            def normed_pair(banks, slot, mm, norm, aside):
                for j in range(2):
                    for k in range(KD):
                        if j == 0 and k == 3:
                            aside()
                        pe.wait_ge(norm.lo, KD * j + k + 1)
                        for e in range(2):
                            a = PAIR_COLS * k + P * e
                            ins = split_product(banks[e][:, half(j)], weights(slot, a, a + P), inputs(k, H * j, H * j + H), k == 0, k == KD - 1)
                            if j == 1 and k == KD - 1:
                                ins.then_inc(mm, 1)

            def tokens_tiles(banks, order, slots, n0, mm, ready=None):
                for c in range(2):
                    pe.wait_ge(lo_done, n0 + c + 1)
                    for t in order:
                        if c == 0 and ready is not None:
                            ready(t)
                        for kk in range(4):
                            k = 4 * c + kk
                            ins = split_product(banks[t][:, :], inputs(k, P * t, P * t + P), weights(slots[c], 512 * kk, 512 * kk + 512),
                                                k == 0, k == KD - 1)
                        if c == 1 or t == order[-1]:
                            ins.then_inc(mm, 1)

            def norm_sum(norm, j, acc, count):
                pe.wait_ge(acc, count)
                pe.matmul(SS_BANKS[j][:, half(j)], ones[:, :], ss_acc[:, half(j)], start=True, stop=True).then_inc(norm.ss, 1)

            def attend(a, scores, v, prob, probT, ident, beside=None):
                for step in range(UNITS + LAG + 1):
                    if step < UNITS:
                        U, hd, i = unit(a, step), step // TB, step % TB
                        n = len(S_BANKS[a])
                        if U >= n:
                            pe.wait_ge(att.exp, U - n + 1)
                        scores(hd, i, scores_bank(a, U), P * (i + 1)).then_inc(att.qk, 1)
                    if LAG <= step < UNITS + LAG:
                        U, i = unit(a, step - LAG), (step - LAG) % TB
                        pe.wait_ge(att.norm, U + 1)
                        if U >= 2:
                            pe.wait_ge(att.ptc, U - 1)
                        for j in range(i + 1):
                            ins = pe.transpose(bank[3 + U % 2][:, P * j:P * j + P], prob[U % 4][:, P * j:P * j + P], ident[:, :])
                        ins.then_inc(att.pt, 1)
                    if step > LAG:
                        u = step - LAG - 1
                        U, hd, i = unit(a, u), u // TB, u % TB
                        pe.wait_ge(att.ptc, U + 1)
                        p, r = hd // 2, HD * (hd % 2)
                        if p >= 2 and u % PAIR_UNITS == 0:
                            pe.wait_ge(heads.lo, PAIRS * a + p - 1)
                        for j in range(i + 1):
                            ins = pe.matmul(HEADS_BANKS[p % 2][r:r + HD, P * i:P * i + P], v[:, j, HD * hd:HD * hd + HD],
                                            probT[U % 2][:, P * j:P * j + P], start=j == 0, stop=j == i)
                        ins.then_inc(att.pv, 1)
                    if beside is not None:
                        beside(step)

            def mixed(a, k, t0=0, t1=T):
                if k >= PAIRS:
                    return inputs(k, t0, t1)
                high, low = head_tiles(a, k)
                return high[:, t0:t1], low[:, t0:t1]

            def first_out(base, a, k):
                for e in range(2):
                    c = PAIR_COLS * k + P * e
                    ins = split_product(FIRST_OUT[e][:, :], weights(base % 2, c, c + P), mixed(a, k), k == PAIRS, k == PAIRS - 1)
                return ins

            def out_begins(base, a, step):
                k = PAIRS + step - UNITS
                if step < UNITS or k >= KD:
                    return
                if k == PAIRS:
                    pe.wait_ge(lo_done, base + 1)
                    if a == 0:
                        pe.wait_ge(mix.lo, 4)
                    else:
                        pe.wait_ge(heads.lo, PAIRS * a)
                    pe.wait_ge(att.exp, unit(a, UNITS - 1))
                first_out(base, a, k)

            def residual_out(res, norm, base, a):
                for k in range(PAIRS):
                    pe.wait_ge(heads.lo, PAIRS * a + k + 1)
                    ins = first_out(base, a, k)
                    if k == PAIRS - 1:
                        ins.then_inc(res.mm, 2)

                def inputs(k, t0, t1):
                    return mixed(a, k, t0, t1)

                for m in range(2, WHOLE):
                    n = base + m // 2
                    if m % 2 == 0:
                        pe.wait_ge(lo_done, n + 1)
                    if m >= 4:
                        pe.wait_ge(res.h, m - 3)
                    features_tile(OUT_BANKS[m % 4], n % 2, m % 2, inputs=inputs).then_inc(res.mm, 1)
                n = base + WHOLE // 2
                pe.wait_ge(lo_done, n + 1)
                for x, (m, j, b) in enumerate(PIECES):
                    pe.wait_ge(res.h, WHOLE - 3 + x)
                    if x == 3:
                        norm_sum(norm, 0, norm.acc, WHOLE + 3)
                    features_tile(b, n % 2, m % 2, half(j), inputs).then_inc(res.mm, 1)

            def residual_down(L, res, base, norm):
                def two_tiles(i, first=False):
                    m0, c0 = (0, base) if first else (2, base + 4)
                    for r in range(2):
                        for e in range(2):
                            slot = (base + e) % 2
                            pe.wait_ge(lo_done, i * 4 + (c0 + 2 * r + e + 1))
                            if e == 0 and not first:
                                pe.wait_ge(res.h, i * 2 + (m0 + r - 1))
                            for kk in range(KF // 2):
                                k = KF // 2 * e + kk
                                if first and r == 0:
                                    pe.wait_ge(L.lo, k + 1)
                                ins = split_product(bank[4 + r][:, :], weights(slot, P * kk, P * kk + P), (acth[:, k, :], actl[:, k, :]),
                                                    k == 0, k == KF - 1)
                            ins.then_inc(res.mm, 1)

                two_tiles(0, True)
                if norm is None:
                    with pe.Fori(0, KD // 2 - 1) as i:
                        two_tiles(i)
                    return
                with pe.Fori(0, KD // 2 - 2) as i:
                    two_tiles(i)
                pe.wait_ge(ada_red, N_ADA)
                for m, j, e in ((KD - 2, None, 0), (KD - 2, None, 1), (KD - 1, 1, 0), (KD - 1, 0, 0), (KD - 1, 0, 1), (KD - 1, 1, 1)):
                    n = base + 2 * m + e
                    pe.wait_ge(lo_done, n + 1)
                    if m == KD - 2:
                        pe.wait_ge(res.h, m - 1)
                    out, tokens = (bank[4], slice(0, T)) if j is None else (DOWN_PIECES[j], half(j))
                    if j == 0 and e == 0:
                        pe.wait_ge(res.h, m - 1)
                    for kk in range(KF // 2):
                        k = KF // 2 * e + kk
                        if (j, e) == (1, 1) and kk == KF // 4:
                            norm_sum(norm, 0, weighted_acc, KD + 1)
                        ins = split_product(out[:, tokens], weights(n % 2, P * kk, P * kk + P), (acth[:, k, tokens], actl[:, k, tokens]),
                                            k == 0, k == KF - 1)
                    if (j, e) != (1, 0):
                        ins.then_inc(res.mm, 1)

            def up(L, norm, base):
                def chunks(count, i, first=False):
                    c0 = 0 if first else 2
                    for c in range(count):
                        pe.wait_ge(lo_done, i * count + (base + c0 + c + 1))
                        for e in range(2):
                            r = 2 * (c % 2) + e
                            m = c0 // 2 + c // 2
                            if not first:
                                pe.wait_ge(L.conv, i * (2 * count) + (4 * m + r - 3))
                            if first and c == 0:
                                if e == 0:
                                    normed_pair(bank[0:2], base % 2, L.mm, norm, lambda: norm_sum(norm, 1, norm.acc, WHOLE + len(PIECES) + 1))
                            else:
                                features_tile(bank[r], (base + c) % 2, e).then_inc(L.mm, 1)

                chunks(2, 0, True)
                with pe.Fori(0, (KF - 2) // 4) as i:
                    chunks(4, i)

            pe.wait_ge(setup1, 1)
            norm_sum(norm_mix, 0, norm_mix.acc, KD + 1)
            pe.wait_ge(lo_first, 1)

            def second_half():
                norm_sum(norm_mix, 1, norm_mix.acc, 2 * KD + 1)
                pe.wait_ge(lo_done, 1)

            normed_pair(bank[4:6], BASE1["ua"] % 2, p1.mm, norm_mix, second_half)
            n = BASE1["vg"]
            tokens_tiles(bank[0:4], range(TB), (n % 2, (n + 1) % 2), n, p1.mm)
            n = BASE1["ub"]
            pe.wait_ge(lo_done, n + 1)
            for e in range(2):
                features_tile(bank[6 + e], n % 2, e).then_inc(p1.mm, 1)
            n = BASE1["f"]
            pe.wait_ge(lo_done, n + 1)
            pe.wait_ge(p1.act, 1)
            features_tile(bank[4], n % 2, 0).then_inc(p1.mm, 1)
            n = BASE1["v"]
            tokens_tiles(bank[0:4], range(TB), (n % 2, (n + 1) % 2), n, p1.mm,
                         lambda t: pe.wait_ge(p1.act, 3 + t))
            pe.wait_ge(setup1, 12)
            pe.wait_ge(gate.done, TB)
            pe.wait_ge(forget.act, 1)
            pe.wait_ge(forget.dve, 1)
            pe.wait_ge(p1.act, 8)
            for t in range(4):
                for c in range(TB):
                    for g in (2 * t, 2 * t + 1):
                        a = HD * (g % 2)
                        ins = pe.matmul(MIX_BANKS[t][a:a + HD, P * c:P * c + P], vg[:, c, HD * g:HD * g + HD], wsT[:, g, :], start=True, stop=True)
                ins.then_inc(mixing.mm, 1)
            n = BASE1["qk"]
            pe.wait_ge(lo_done, n + 1)
            for e in range(2):
                pe.wait_ge(p1.dve, e + 1)
                features_tile(bank[e], n % 2, e).then_inc(p1.mm, 1)

            def next_pair(step):
                out_begins(BASE1["out"], 0, step)
                p, x = step // PAIR_UNITS + 1, step % PAIR_UNITS
                e = 0 if x < Q_STEPS else 1
                share = (2, 3)[e]
                first = (x - e * Q_STEPS) * share
                if p >= PAIRS or first >= KD:
                    return
                n = BASE1["qk"] + p
                if x == 0:
                    pe.wait_ge(lo_done, n + 1)
                    if p == 1:
                        pe.wait_ge(mixing.done, 2)
                    else:
                        pe.wait_ge(p1.dve, TB + p)
                elif x == Q_STEPS:
                    pe.wait_ge(p1.act, 9 + p)
                for k in range(first, min(first + share, KD)):
                    a = PAIR_COLS * k + P * e
                    ins = split_product(NEXT_BANK[:, :], weights(n % 2, a, a + P), inputs(k), k == 0, k == KD - 1)
                    if k == KD - 1:
                        ins.then_inc(p1.mm, 1)

            def rows(hd):
                return slice(HD * (hd % 2), HD * (hd % 2) + HD)

            def forgetting(hd, i, out, w):
                r = rows(hd)
                if hd % 2 == 0 and i == 0:
                    pe.wait_ge(p1.act, 9 + hd // 2)
                    pe.wait_ge(p1.dve, TB + 1 + hd // 2)
                pe.matmul(out[:, 0:w], q1[r, hd // 2, P * i:P * i + P], k1[r, hd // 2, 0:w], start=True, stop=False)
                pe.wait_ge(decay.head, hd + 1)
                pe.matmul(out[:, 0:w], dec_q[:, P * i:P * i + P], dec_k[hd % 2][:, 0:w], start=False, stop=False)
                return pe.matmul(out[:, w - P:w], ident_b1[:, :], causal_b[:, :], start=False, stop=True)

            pe.wait_ge(mixing.done, 4)
            attend(0, forgetting, v1, prob1, probT1, ident1, next_pair)
            residual_out(res_out1, norm_ffn, BASE1["out"], 0)
            up(up1, norm_ffn, BASE1["up"])
            residual_down(up1, res_down1, BASE1["down"], norm_attn2)
            base = N1 + N_DOWN

            def head_sum(job, out, ones_of, squares):
                pe.wait_ge(head.sq, N_SQ[job])
                for n, sq in enumerate(squares):
                    ins = pe.matmul(out[:, :], ones_of[:, :], sq[:, :], start=n == 0, stop=n == len(squares) - 1)
                ins.then_inc(head.ss, 1)

            def last_sums():
                norm_sum(norm_attn2, 1, weighted_acc, KD + 2)
                pe.wait_ge(norm_final.acc, KD + 2)
                pe.matmul(SS_FINAL[:, :], ones[:, :], ss_final[:, :], start=True, stop=True).then_inc(norm_final.ss, 1)

            pe.wait_ge(lo_done, base + 1)
            normed_pair(bank[0:2], base % 2, p2.mm, norm_attn2, last_sums)
            pe.wait_ge(lo_done, base + 2)
            for e in range(2):
                features_tile(bank[2 + e], (base + 1) % 2, e).then_inc(p2.mm, 1)
            pe.wait_ge(setup2, 14)

            def pair_sums(p):
                for which in range(2):
                    if p == 0:
                        pe.wait_ge(lat.lo, 3)
                    else:
                        pe.wait_ge(head.root, job_c(p - 1, which) + 1)
                    head_sum(job_c(p, which), SS_BANKS[which], ones64, [sq2[which]])

            for p in range(PAIRS):
                n = BASE2["cqk"] + p
                pe.wait_ge(lo_done, n + 1)
                for which in range(2):
                    if p == 0 and which == 0:
                        pe.wait_ge(norm_final.rstd, 1)
                    elif p == 1:
                        pe.wait_ge(head.root, which + 1)
                    elif p == 2:
                        pe.wait_ge(lat.lo, 3)
                        pe.wait_ge(rope.dve, 2)
                    elif p == 3:
                        pe.wait_ge(head.done, which + 1)
                    features_tile(bank[c_bank(p) + which], n % 2, which).then_inc(p2.mm, 1)
                    if p == 0 and which == 0:
                        head_sum(JOB_KV, bank[4], ones, [sq2[0]])
                        head_sum(JOB_QL, bank[5], ones, [sq2[1], scratch[3]])
                if p:
                    pair_sums(p - 1)

            def pairs_taken(t):
                if t == 2:
                    pair_sums(PAIRS - 1)
                pe.wait_ge(head.done, 3 + t)

            n = BASE2["cv"]
            tokens_tiles(V2_BANKS, range(TB), (n % 2, (n + 1) % 2), n, p2.mm, pairs_taken)

            def chunked(hd, i, out, w):
                r = rows(hd)
                if hd == 0 and i == 0:
                    pe.wait_ge(head.root, job_c(PAIRS - 1, 0) + 1)
                if hd == 0 and i == 1:
                    pe.wait_ge(head.done, 2 * PAIRS)
                if hd == 0 and i >= 2:
                    pe.wait_ge(p2.dve, i + 1)
                pe.matmul(out[:, 0:w], cq[r, hd // 2, P * i:P * i + P], ck[r, hd // 2, 0:w], start=True, stop=False)
                if i == 0:
                    pe.wait_ge(rel_low, hd + 1)
                pe.matmul(out[:, 0:w], flip_r[:, :], rel_h[hd % 2][:, T - w:T], start=False, stop=False)
                return pe.matmul(out[:, 0:w], flip_r[:, :], rel_l[hd % 2][:, T - w:T], start=False, stop=True)

            attend(1, chunked, v2, prob2, probT2, ident2)
            n = BASE2["mkv"]
            pe.wait_ge(lo_done, n + 1)

            def mla_values(t):
                pe.wait_ge(head.done, 2 * PAIRS + 2 * (6 + t // 2))
                split_product(V2_BANKS[t][:, :], (kvh[:, P * t:P * t + P], kvl[:, P * t:P * t + P]), weights(n % 2, 1024, 1536),
                              True, True).then_inc(p2.mm, 1)

            nq = BASE2["mq"]
            for hd in range(HEADS + 1):
                if hd < HEADS:
                    if hd == 0:
                        pe.wait_ge(att.exp, unit(1, UNITS))
                    if hd >= 3:
                        pe.wait_ge(head.done, 2 * PAIRS + 2 * (hd - 2))
                    for k in range(2):
                        a = 1024 * k + P * hd
                        ins = split_product(bank[m_bank(hd)][:, :], weights(nq % 2, a, a + P), (qlh[:, k, :], qll[:, k, :]), k == 0, k == 1)
                    ins.then_inc(p2.mm, 1)
                    split_product(bank[m_bank(hd) + 1][:, :], weights(n % 2, P * hd, P * hd + P), (kvh[:, :], kvl[:, :]), True, True).then_inc(p2.mm, 1)
                if hd == HEADS:
                    mla_values(0)
                    mla_values(1)
                if hd:
                    for which in range(2):
                        x = job_m(hd - 1, which)
                        if hd == 1:
                            pe.wait_ge(heads.lo, 2 * PAIRS)
                        if hd >= 2:
                            pe.wait_ge(head.root, x - 1)
                        head_sum(x, bank[6 + which], ones96, [(sq2, sqk)[which][(hd - 1) % 2]])

            mla_values(2)
            mla_values(3)

            def latent(hd, i, out, w):
                if hd == 0 and i < 2:
                    pe.wait_ge(p2.dve, TB + i + 3)
                if hd == 0 and i == 2:
                    pe.wait_ge(head.root, job_m(HEADS - 1, 1) + 1)
                if hd == 0 and i == 3:
                    pe.wait_ge(head.done, 2 * PAIRS + 2 * HEADS)
                pe.matmul(out[:, 0:w], mq[:, hd, P * i:P * i + P], mk[:, hd, 0:w], start=True, stop=False)
                return pe.matmul(out[:, w - P:w], ident_b2[:, :], chunk_b[:, :], start=False, stop=True)

            attend(2, latent, v2, prob2, probT2, ident2, lambda step: out_begins(BASE2["out"], 2, step))
            residual_out(res_out2, norm_mlp2, BASE2["out"], 2)
            up(up2, norm_mlp2, BASE2["up"])
            residual_down(up2, res_down2, BASE2["down"], None)


def pair_chunks(w):
    n = w.shape[1] // PAIR_COLS
    return w.reshape(KD, P, n, PAIR_COLS).transpose(2, 1, 0, 3).reshape(n * P, CHUNK)


def wide_chunks(w):
    return w.reshape(2, 4, P, 512).transpose(0, 2, 1, 3).reshape(2 * P, CHUNK)


def down_chunks(w):
    return w.reshape(2, KF // 2, P, KD, P).transpose(3, 0, 2, 1, 4).reshape(N_DOWN * P, DOWN_CHUNK)


def up_chunks(w, gate, value):
    g, v = pair_chunks(w[:, gate * FF:(gate + 1) * FF]), pair_chunks(w[:, value * FF:(value + 1) * FF])
    return np.stack([g.reshape(-1, P, CHUNK), v.reshape(-1, P, CHUNK)], 1).reshape(-1, CHUNK)


def pad_columns(w, n):
    return np.concatenate([w, np.zeros((w.shape[0], n - w.shape[1]), w.dtype)], 1)


def up_columns(a, gate, value):
    t = a.reshape(a.shape[0], 2, KF // 2, 2, P)
    return np.stack([t[:, gate], t[:, value]], 2).reshape(a.shape[0], UP_TILES, P)


def kernel(**inputs):
    import concourse.bacc as bacc
    from concourse.bass_utils import run_bass_kernel_spmd

    f = {k: np.asarray(v) for k, v in inputs.items()}
    f32 = np.float32

    w = f["w_in"][0]
    wf = np.zeros((D, 2 * P), f32)
    for quadrant in range(4):
        wf[:, 32 * quadrant:32 * quadrant + HEADS] = w[:, 2560:2568]
    qk = np.concatenate([np.concatenate([w[:, P * p:P * p + P], w[:, 512 + P * p:512 + P * p + P]], 1) for p in range(PAIRS)], 1)
    stream1 = np.concatenate([
        pair_chunks(w[:, 1536:1792]), wide_chunks(w[:, 2048:2560]), pair_chunks(w[:, 1792:2048]), pair_chunks(wf), wide_chunks(w[:, 1024:1536]), pair_chunks(qk),
        pair_chunks(f["w_out"][0]), up_chunks(f["w_up"][0], 1, 0)])
    w = f["w_in_2"][0]
    x, xs = w[:, 384:416], np.concatenate([w[:, 400:416], w[:, 384:400]], 1)
    kvr = np.concatenate([w[:, 256:384], x, x, xs, xs], 1)
    ca = w[:, 416:]
    cqk = np.concatenate([np.concatenate([ca[:, P * p:P * p + P], ca[:, 512 + P * p:512 + P * p + P]], 1) for p in range(PAIRS)], 1)
    wq = f["w_q_up_2"][0].reshape(2 * P, HEADS, MLA_QK)
    wq = np.concatenate([wq, wq[:, :, 80:96], wq[:, :, 64:80]], 2).reshape(2, P, HEADS * P)
    wkv = f["w_kv_up_2"][0].reshape(P, HEADS, P)
    wk = np.concatenate([wkv[:, :, :HD], np.zeros((P, HEADS, HD), f32)], 2).reshape(P, HEADS * P)
    mkv = pad_columns(np.concatenate([wk, wkv[:, :, HD:].reshape(P, 512)], 1), CHUNK)
    stream2 = np.concatenate([
        pair_chunks(kvr), pair_chunks(w[:, :256]), pair_chunks(cqk), wide_chunks(ca[:, 1024:]),
        wq.transpose(1, 0, 2).reshape(P, CHUNK), mkv, pair_chunks(f["w_out_2"][0]), up_chunks(f["w_up_2"][0], 0, 1)])

    parts = {}

    def features(name, a):
        parts[name] = a.reshape(-1, P).T

    features("mix_g", f["norm_mix_g"][0])
    features("ffn_g", f["norm_ffn_g"][0])
    features("final_g", f["norm_final_g"])
    features("attn2_g", f["g_attn_norm_2"][0])
    features("mlp2_g", f["g_mlp_norm_2"][0])
    features("gmlp_g", f["gmlp_norm_g"][0])
    parts["conv_w"] = up_columns(f["conv_w"][0], 1, 0).transpose(2, 1, 0).reshape(P, -1)
    parts["conv_b"] = up_columns(f["conv_b"], 1, 0)[0].T
    parts["conv_w2"] = up_columns(f["conv_w_2"][0], 0, 1).transpose(2, 1, 0).reshape(P, -1)
    parts["conv_b2"] = up_columns(f["conv_b_2"], 0, 1)[0].T
    features("b_ada", f["b_ada_2"][0])
    features("ql_g", f["g_q_latent_2"][0])
    features("kvl_g", f["g_kv_latent_2"][0])
    g = f["g_mla_q_2"][0]
    features("mq_g", np.concatenate([g, g[80:96], g[64:80]]))
    g = f["g_mla_k_2"][0]
    features("mk_g", np.concatenate([g[:64], g[:64]]))
    swapped = np.concatenate([g[80:96], g[64:80]])
    features("mkr_g", np.concatenate([g[64:96], g[64:96], swapped, swapped]))
    features("cq_g", np.tile(f["g_ca_q_2"][0], 2))
    features("ck_g", np.tile(f["g_ca_k_2"][0], 2))
    b_forget = np.zeros(P, f32)
    for quadrant in range(4):
        b_forget[32 * quadrant:32 * quadrant + HEADS] = f["b_forget"][0]
    features("b_forget", b_forget)
    parts["head_row"] = (np.arange(P)[:, None] % 32 == np.arange(HEADS)[None, :]).astype(f32)
    half = ROPE // 2
    inv = np.power(f32(ROPE_THETA), -np.arange(half, dtype=f32) / f32(half)).astype(f32)
    features("inv_freq", np.tile(inv, P // half))
    sign = np.concatenate([-np.ones(half, f32), np.ones(half, f32)])
    scale = f32(MLA_QK ** -0.5)
    features("q_sign", np.concatenate([np.ones(96, f32), sign]) * scale)
    features("k_sign", np.concatenate([np.ones(64, f32), sign, sign]))
    packed = np.concatenate([parts[name].astype(f32) for name in COLS], 1)

    distance = np.clip(T - 1 - np.arange(REL_LEN), -REL_CLIP, REL_CLIP)
    arrays = {
        "xT": f["x"][0].T,
        "cols_in": packed,
        "stream1": stream1,
        "down1": down_chunks(f["w_down"][0]),
        "stream2": stream2,
        "down2": down_chunks(f["w_down_2"][0]),
        "ada": f["w_ada_2"][0].T.reshape(N_ADA, ADA_TILES, P, D).transpose(0, 2, 1, 3).reshape(N_ADA * P, ADA_TILES * D),
        "c_row": f["c_2"].reshape(1, D),
        "w_spatial_T": f["w_spatial"][0].transpose(2, 0, 1).reshape(P, HEADS * P),
        "b_spatial_rows": np.repeat(f["b_spatial"][0].reshape(4, 2, 1, P), HD, axis=2).transpose(1, 2, 0, 3).reshape(P, 4 * P),
        "positions": f["positions_2"].reshape(1, T).astype(np.int32),
        "rel_rows": f["rel_bias_2"][0][:, distance + REL_CLIP],
    }
    nc = bacc.Bacc("TRN2", target_bir_lowering=False, num_devices=1)
    args = {}
    for name, a in arrays.items():
        a = arrays[name] = np.ascontiguousarray(a)
        args[name] = nc.dram_tensor(name, a.shape, mybir.dt.from_np(a.dtype), kind="ExternalInput").ap()
    outT = nc.dram_tensor("outT", (D, T), F32, kind="ExternalOutput").ap()
    build(nc, **args, outT=outT)
    r = run_bass_kernel_spmd(nc, [arrays], core_ids=[0])
    return np.ascontiguousarray(r.results[0]["outT"].T).reshape(1, T, D)
```
